# Optimizing a Trainium2 kernel written in Bass

```python
import math
import jax, jax.numpy as jnp
from jax import lax
import numpy as np

D_MODEL = 1024
BATCH = 1
SEQ = 1024
DEPTH = 2

CHUNK = 64
N_MIXERS = 2
EPS = 1e-6

RET_HEADS = 4
RET_QK_DIM = D_MODEL // RET_HEADS
RET_V_DIM = 2 * D_MODEL // RET_HEADS
RET_QK_WIDTH = RET_HEADS * RET_QK_DIM
RET_WIDTH = RET_HEADS * RET_V_DIM
ROPE_BASE = 10000.0

ATT_HEADS = 16
ATT_HEAD_DIM = 2 * D_MODEL // ATT_HEADS
ATT_WIDTH = ATT_HEADS * ATT_HEAD_DIM
LEFT_CHUNKS = 8
BAND = (LEFT_CHUNKS + 1) * CHUNK
MAX_REL = 2 * CHUNK

N_RET_LAYERS = (DEPTH + 1) // 2
N_ATT_LAYERS = DEPTH // 2


def rms_norm_f32(t, gain):
    t32 = t.astype(jnp.float32)
    return t32 * lax.rsqrt(jnp.mean(t32 * t32, axis=-1, keepdims=True) + EPS) * gain.astype(jnp.float32)

def apply_rope(t, cos, sin):
    t1, t2 = jnp.split(t, 2, axis=-1)
    return jnp.concatenate([t1 * cos - t2 * sin, t1 * sin + t2 * cos], axis=-1)

def retention_mixer(h, positions, w_in, gn_g, w_out):
    B, S, _ = h.shape
    nc = S // CHUNK
    proj = h @ w_in
    q, k, v, g = jnp.split(proj, [RET_QK_WIDTH, 2 * RET_QK_WIDTH, 2 * RET_QK_WIDTH + RET_WIDTH], axis=-1)
    q = q.reshape(B, S, RET_HEADS, RET_QK_DIM).astype(jnp.float32)
    k = k.reshape(B, S, RET_HEADS, RET_QK_DIM).astype(jnp.float32)
    v = v.reshape(B, S, RET_HEADS, RET_V_DIM).astype(jnp.float32)

    inv_freq = 1.0 / (ROPE_BASE ** (jnp.arange(0, RET_QK_DIM, 2, dtype=jnp.float32) / RET_QK_DIM))
    ang = positions.astype(jnp.float32)[..., None] * inv_freq
    cos, sin = jnp.cos(ang)[:, :, None, :], jnp.sin(ang)[:, :, None, :]
    q = apply_rope(q, cos, sin)
    k = apply_rope(k, cos, sin) * (RET_QK_DIM ** -0.5)

    def to_chunks(t):
        return t.reshape(B, nc, CHUNK, RET_HEADS, t.shape[-1]).transpose(0, 3, 1, 2, 4)

    qc, kc, vc = to_chunks(q), to_chunks(k), to_chunks(v)

    log_gamma = jnp.log(1.0 - 2.0 ** (-5.0 - jnp.arange(RET_HEADS, dtype=jnp.float32)))
    idx = jnp.arange(CHUNK, dtype=jnp.float32)
    intra_decay = jnp.exp(log_gamma[:, None, None] * jnp.abs(idx[:, None] - idx[None, :]))
    q_decay = jnp.exp(log_gamma[:, None] * (idx + 1.0))
    k_decay = jnp.exp(log_gamma[:, None] * (CHUNK - 1.0 - idx))
    chunk_decay = jnp.exp(log_gamma * CHUNK)

    scores = jnp.einsum('bhncd,bhnkd->bhnck', qc, kc) * intra_decay[:, None]
    o_intra = jnp.einsum('bhnck,bhnke->bhnce', scores, vc)

    def step(state, xs):
        q_j, k_j, v_j = xs
        o_j = jnp.einsum('bhcd,bhde->bhce', q_j * q_decay[:, :, None], state)
        state = chunk_decay[:, None, None] * state + jnp.einsum(
            'bhcd,bhce->bhde', k_j * k_decay[:, :, None], v_j)
        return state, o_j

    xs = (qc.transpose(2, 0, 1, 3, 4), kc.transpose(2, 0, 1, 3, 4), vc.transpose(2, 0, 1, 3, 4))
    state0 = jnp.zeros((B, RET_HEADS, RET_QK_DIM, RET_V_DIM), jnp.float32)
    _, o_inter = lax.scan(step, state0, xs)

    o = o_intra + o_inter.transpose(1, 2, 0, 3, 4)
    o = o.transpose(0, 2, 3, 1, 4).reshape(B, S, RET_HEADS, RET_V_DIM)
    o = rms_norm_f32(o, gn_g.reshape(RET_HEADS, RET_V_DIM))
    o = o.reshape(B, S, RET_WIDTH) * jax.nn.silu(g.astype(jnp.float32))
    return o.astype(h.dtype) @ w_out

def chunked_attention_mixer(h, w_in, q_g, k_g, rel_table, w_out):
    B, S, _ = h.shape
    nc = S // CHUNK
    proj = h @ w_in
    q, k, v, g = jnp.split(proj, 4, axis=-1)
    q = rms_norm_f32(q.reshape(B, S, ATT_HEADS, ATT_HEAD_DIM), q_g)
    k = rms_norm_f32(k.reshape(B, S, ATT_HEADS, ATT_HEAD_DIM), k_g)
    v = v.reshape(B, S, ATT_HEADS, ATT_HEAD_DIM).astype(jnp.float32)

    pad = LEFT_CHUNKS * CHUNK
    k_pad = jnp.pad(k, ((0, 0), (pad, 0), (0, 0), (0, 0)))
    v_pad = jnp.pad(v, ((0, 0), (pad, 0), (0, 0), (0, 0)))

    qi = jnp.arange(CHUNK)
    kb = jnp.arange(BAND)
    rel = qi[:, None] + pad - kb[None, :]
    bias = rel_table.astype(jnp.float32)[:, jnp.clip(rel, -MAX_REL, MAX_REL) + MAX_REL]
    scale = ATT_HEAD_DIM ** -0.5

    q_chunks = q.reshape(B, nc, CHUNK, ATT_HEADS, ATT_HEAD_DIM).transpose(1, 0, 2, 3, 4)

    def one_chunk(args):
        j, q_j = args
        k_j = lax.dynamic_slice_in_dim(k_pad, j * CHUNK, BAND, axis=1)
        v_j = lax.dynamic_slice_in_dim(v_pad, j * CHUNK, BAND, axis=1)
        s = jnp.einsum('bqhd,bkhd->bhqk', q_j, k_j) * scale + bias
        valid = kb >= (LEFT_CHUNKS - j) * CHUNK
        s = jnp.where(valid, s, jnp.float32(-1e30))
        p = jax.nn.softmax(s, axis=-1)
        return jnp.einsum('bhqk,bkhd->bqhd', p, v_j)

    o = lax.map(one_chunk, (jnp.arange(nc), q_chunks))
    o = o.transpose(1, 0, 2, 3, 4).reshape(B, S, ATT_WIDTH)
    o = o * jax.nn.silu(g.astype(jnp.float32))
    return o.astype(h.dtype) @ w_out

def first_inputs(seed: int = 0) -> dict:
    key = jax.random.key(seed)
    ks = jax.random.split(key, 16)
    D = D_MODEL
    x = jax.random.normal(ks[0], (BATCH, SEQ, D), jnp.float32)
    c = jax.random.normal(ks[1], (BATCH, D), jnp.float32)
    offsets = jax.random.randint(ks[2], (BATCH, 1), 0, 4096, dtype=jnp.int32)
    positions = offsets + jnp.arange(SEQ, dtype=jnp.int32)[None, :]
    norm_g = 1.0 + 0.1 * jax.random.normal(ks[3], (DEPTH, D), jnp.float32)
    ada_w = jax.random.normal(ks[4], (DEPTH, D, 3 * D), jnp.float32) * D ** -0.5
    ada_b = 0.02 * jax.random.normal(ks[5], (DEPTH, 3 * D), jnp.float32)
    ret_w_in = jax.random.normal(ks[6], (N_RET_LAYERS, D, 2 * RET_QK_WIDTH + 2 * RET_WIDTH), jnp.float32) * D ** -0.5
    ret_gn_g = 1.0 + 0.1 * jax.random.normal(ks[7], (N_RET_LAYERS, RET_WIDTH), jnp.float32)
    ret_w_out = jax.random.normal(ks[8], (N_RET_LAYERS, RET_WIDTH, D), jnp.float32) * RET_WIDTH ** -0.5
    att_w_in = jax.random.normal(ks[9], (N_ATT_LAYERS, D, 4 * ATT_WIDTH), jnp.float32) * D ** -0.5
    att_q_g = 1.0 + 0.1 * jax.random.normal(ks[10], (N_ATT_LAYERS, ATT_HEAD_DIM), jnp.float32)
    att_k_g = 1.0 + 0.1 * jax.random.normal(ks[11], (N_ATT_LAYERS, ATT_HEAD_DIM), jnp.float32)
    att_rel_bias = 0.5 * jax.random.normal(ks[12], (N_ATT_LAYERS, ATT_HEADS, 2 * MAX_REL + 1), jnp.float32)
    att_w_out = jax.random.normal(ks[13], (N_ATT_LAYERS, ATT_WIDTH, D), jnp.float32) * ATT_WIDTH ** -0.5
    return {"x": x, "c": c, "positions": positions, "norm_g": norm_g, "ada_w": ada_w,
            "ada_b": ada_b, "ret_w_in": ret_w_in, "ret_gn_g": ret_gn_g, "ret_w_out": ret_w_out,
            "att_w_in": att_w_in, "att_q_g": att_q_g, "att_k_g": att_k_g,
            "att_rel_bias": att_rel_bias, "att_w_out": att_w_out}

def first_block(x, c, positions, norm_g, ada_w, ada_b, ret_w_in, ret_gn_g, ret_w_out,
              att_w_in, att_q_g, att_k_g, att_rel_bias, att_w_out):
    cond = jax.nn.silu(c.astype(jnp.float32))
    for i in range(DEPTH):
        mod = cond @ ada_w[i].astype(jnp.float32) + ada_b[i].astype(jnp.float32)
        shift, scale, gate = jnp.split(mod[:, None, :], 3, axis=-1)
        h = (rms_norm_f32(x, norm_g[i]) * (1.0 + scale) + shift).astype(x.dtype)
        j = i // N_MIXERS
        if i % N_MIXERS == 0:
            out = retention_mixer(h, positions, ret_w_in[j], ret_gn_g[j], ret_w_out[j])
        else:
            out = chunked_attention_mixer(h, att_w_in[j], att_q_g[j], att_k_g[j],
                                          att_rel_bias[j], att_w_out[j])
        x = x + (gate * out.astype(jnp.float32)).astype(x.dtype)
    return x


DEPTH_2 = 1

POOL_WINDOWS = (2, 4, 8, 16)
POOL_WIDTH = D_MODEL // 2
POOL_GROUP = POOL_WIDTH // len(POOL_WINDOWS)
N_HEADS = 8
QK_NOPE = 64
QK_ROPE = 32
QK_HEAD = QK_NOPE + QK_ROPE
V_HEAD = 64
ATTN_WIDTH = N_HEADS * V_HEAD
Q_LORA = D_MODEL // 4
KV_LORA = D_MODEL // 8
MIX_WIDTH = POOL_WIDTH + ATTN_WIDTH
IN_SPLITS = (POOL_WIDTH, POOL_WIDTH, Q_LORA, KV_LORA, QK_ROPE, ATTN_WIDTH)
IN_WIDTH = sum(IN_SPLITS)
ROPE_THETA = 10000.0
Q_BLOCK = 128


def rmsnorm(x, g):
    xf = x.astype(jnp.float32)
    r = lax.rsqrt(jnp.mean(xf * xf, axis=-1, keepdims=True) + EPS)
    return (xf * r).astype(x.dtype) * g

def rope_tables(positions):
    inv = ROPE_THETA ** (-jnp.arange(0, QK_ROPE, 2, dtype=jnp.float32) / QK_ROPE)
    ang = positions.astype(jnp.float32)[..., None] * inv
    return jnp.cos(ang)[:, :, None, :], jnp.sin(ang)[:, :, None, :]

def apply_rope_2(x, cos, sin):
    x1, x2 = jnp.split(x, 2, axis=-1)
    cos = cos.astype(x.dtype)
    sin = sin.astype(x.dtype)
    return jnp.concatenate([x1 * cos - x2 * sin, x2 * cos + x1 * sin], axis=-1)

def multiscale_pool(u, pool_w, pool_scale):
    B, S, P = u.shape
    uf = u.astype(jnp.float32)
    cs = jnp.concatenate([jnp.zeros((B, 1, P), jnp.float32), jnp.cumsum(uf, axis=1)], axis=1)
    t = jnp.arange(S)
    outs = []
    for gi, w in enumerate(POOL_WINDOWS):
        lo = jnp.clip(t - w // 2, 0, S)
        hi = jnp.clip(t + (w - w // 2), 0, S)
        csg = cs[..., gi * POOL_GROUP:(gi + 1) * POOL_GROUP]
        cnt = (hi - lo).astype(jnp.float32)[None, :, None]
        mean = (jnp.take(csg, hi, axis=1) - jnp.take(csg, lo, axis=1)) / cnt
        diff = (mean - uf[..., gi * POOL_GROUP:(gi + 1) * POOL_GROUP]).astype(u.dtype)
        outs.append(jnp.einsum('bsc,cd->bsd', diff, pool_w[gi]))
    return jnp.concatenate(outs, axis=-1) * pool_scale

def latent_attention(q_lat, kv_lat, k_rope_raw, cos, sin, g_q_lat, w_uq, g_kv_lat, w_ukv, g_qnorm, g_knorm):
    B, S, _ = q_lat.shape
    q = jnp.einsum('bsr,rd->bsd', rmsnorm(q_lat, g_q_lat), w_uq).reshape(B, S, N_HEADS, QK_HEAD)
    kv = jnp.einsum('bsr,rd->bsd', rmsnorm(kv_lat, g_kv_lat), w_ukv).reshape(B, S, N_HEADS, QK_NOPE + V_HEAD)
    k_nope, v = kv[..., :QK_NOPE], kv[..., QK_NOPE:]
    k_rope = jnp.broadcast_to(k_rope_raw[:, :, None, :], (B, S, N_HEADS, QK_ROPE))
    k = jnp.concatenate([k_nope, k_rope], axis=-1)
    q = rmsnorm(q, g_qnorm)
    k = rmsnorm(k, g_knorm)
    q = jnp.concatenate([q[..., :QK_NOPE], apply_rope_2(q[..., QK_NOPE:], cos, sin)], axis=-1)
    k = jnp.concatenate([k[..., :QK_NOPE], apply_rope_2(k[..., QK_NOPE:], cos, sin)], axis=-1)
    scale = QK_HEAD ** -0.5
    nblk = S // Q_BLOCK
    qb = q.reshape(B, nblk, Q_BLOCK, N_HEADS, QK_HEAD).transpose(1, 0, 2, 3, 4)

    def attend(qblk):
        s = jnp.einsum('bqhd,bkhd->bhqk', qblk, k, preferred_element_type=jnp.float32) * scale
        p = jax.nn.softmax(s, axis=-1)
        return jnp.einsum('bhqk,bkhd->bqhd', p.astype(v.dtype), v)

    o = lax.map(attend, qb)
    return o.transpose(1, 0, 2, 3, 4).reshape(B, S, ATTN_WIDTH)

def second_inputs(seed: int = 0) -> dict:
    key = jax.random.key(seed)
    ks = jax.random.split(key, 20)
    L, D = DEPTH_2, D_MODEL
    nrm = lambda k, shape, fan: jax.random.normal(k, shape, jnp.float32) * fan ** -0.5
    gain = lambda k, shape: 1.0 + 0.05 * jax.random.normal(k, shape, jnp.float32)
    return {
        "x": jax.random.normal(ks[0], (BATCH, SEQ, D), jnp.float32),
        "c": jax.random.normal(ks[1], (BATCH, D), jnp.float32),
        "positions": jnp.tile(jnp.arange(SEQ, dtype=jnp.int32)[None, :], (BATCH, 1)),
        "ada_w": nrm(ks[2], (L, D, 3 * D), D) * 0.5,
        "ada_b": 0.02 * jax.random.normal(ks[3], (L, 3 * D), jnp.float32),
        "norm_g": gain(ks[4], (L, D)),
        "w_in": nrm(ks[5], (L, D, IN_WIDTH), D),
        "pool_w": nrm(ks[6], (L, len(POOL_WINDOWS), POOL_GROUP, POOL_GROUP), POOL_GROUP),
        "pool_scale": gain(ks[7], (L, POOL_WIDTH)),
        "g_q_lat": gain(ks[8], (L, Q_LORA)),
        "w_uq": nrm(ks[9], (L, Q_LORA, N_HEADS * QK_HEAD), Q_LORA),
        "g_kv_lat": gain(ks[10], (L, KV_LORA)),
        "w_ukv": nrm(ks[11], (L, KV_LORA, N_HEADS * (QK_NOPE + V_HEAD)), KV_LORA),
        "g_qnorm": gain(ks[12], (L, QK_HEAD)),
        "g_knorm": gain(ks[13], (L, QK_HEAD)),
        "w_out": nrm(ks[14], (L, MIX_WIDTH, D), MIX_WIDTH),
    }

def second_block(x, c, positions, ada_w, ada_b, norm_g, w_in, pool_w, pool_scale, g_q_lat, w_uq,
              g_kv_lat, w_ukv, g_qnorm, g_knorm, w_out):
    cos, sin = rope_tables(positions)
    offs = list(np.cumsum(IN_SPLITS)[:-1])
    h = x
    c_act = jax.nn.silu(c)
    for l in range(DEPTH_2):
        mod = jnp.einsum('bd,de->be', c_act, ada_w[l]) + ada_b[l]
        shift, scale, gate = jnp.split(mod, 3, axis=-1)
        xn = rmsnorm(h, norm_g[l]) * (1.0 + scale[:, None, :]) + shift[:, None, :]
        proj = jnp.einsum('bsd,de->bse', xn, w_in[l])
        u_pool, g_pool, q_lat, kv_lat, k_rope_raw, g_attn = jnp.split(proj, offs, axis=-1)
        y_pool = multiscale_pool(u_pool, pool_w[l], pool_scale[l]) * jax.nn.silu(g_pool)
        y_attn = latent_attention(q_lat, kv_lat, k_rope_raw, cos, sin, g_q_lat[l], w_uq[l],
                                  g_kv_lat[l], w_ukv[l], g_qnorm[l], g_knorm[l]) * jax.nn.silu(g_attn)
        y = jnp.einsum('bsm,md->bsd', jnp.concatenate([y_pool, y_attn], axis=-1), w_out[l])
        h = h + gate[:, None, :] * y
    return h


def setup_inputs(seed=0):
    out = dict(first_inputs(seed))
    for name, value in second_inputs(seed + 1).items():
        if name != "x":
            out[name + "_2"] = value
    return out


def reference(
    x, c, positions, norm_g, ada_w, ada_b, ret_w_in, ret_gn_g, ret_w_out, att_w_in, att_q_g,
    att_k_g, att_rel_bias, att_w_out, c_2, positions_2, ada_w_2, ada_b_2, norm_g_2, w_in_2,
    pool_w_2, pool_scale_2, g_q_lat_2, w_uq_2, g_kv_lat_2, w_ukv_2, g_qnorm_2, g_knorm_2,
    w_out_2,
):
    x = first_block(
        x, c, positions, norm_g, ada_w, ada_b, ret_w_in, ret_gn_g, ret_w_out, att_w_in, att_q_g,
        att_k_g, att_rel_bias, att_w_out,
    )
    return second_block(
        x, c_2, positions_2, ada_w_2, ada_b_2, norm_g_2, w_in_2, pool_w_2, pool_scale_2,
        g_q_lat_2, w_uq_2, g_kv_lat_2, w_ukv_2, g_qnorm_2, g_knorm_2, w_out_2,
    )


_drawn_inputs = setup_inputs


def setup_inputs(seed=0):
    import zlib

    import numpy as np

    out = dict(_drawn_inputs(seed))
    spreads = {}
    factors = {'att_q_g': 8.0,
     'att_k_g': 8.0,
     'att_rel_bias': 2.772,
     'ada_b_2': 6.256,
     'norm_g_2': 6.959,
     'pool_scale_2': 8.0,
     'g_q_lat_2': 8.0,
     'w_uq_2': 5.587,
     'g_kv_lat_2': 8.0,
     'g_qnorm_2': 8.0,
     'g_knorm_2': 8.0}
    for name, (base, spread) in spreads.items():
        noise = np.random.default_rng([zlib.crc32(name.encode()), seed]).standard_normal(out[name].shape)
        drawn = base * np.exp(spread * noise) if base else spread * noise
        out[name] = __import__('jax').numpy.asarray(drawn.astype(out[name].dtype))
    for name, factor in factors.items():
        out[name] = (out[name] * factor).astype(out[name].dtype)
    return out
```

```python
from contextlib import ExitStack
import math

import numpy as np

import concourse.bass as bass
from concourse import mybir

F32 = mybir.dt.float32
F32R = mybir.dt.float32r
I32 = mybir.dt.int32
ALU = mybir.AluOpType
ACT = mybir.ActivationFunctionType
AX = mybir.AxisListType

P = 128
D = 1024
S = 1024
NT = S // P
KD = D // P
EPS = 1e-6
NEG = -1e30

RING = 8
STAGE = 4
RET_GROUPS, RET_SLOTS = 4, 32
ATT_GROUPS, ATT_SLOTS = 4, 40
GH = 4
MIX_SLOTS = 56
ATT0 = RET_GROUPS * RET_SLOTS
MIX0 = ATT0 + ATT_GROUPS * ATT_SLOTS
SLOTS = MIX0 + MIX_SLOTS

ADA = KD + 1
PIECES = 6
LEFT = 4
BANDW = (LEFT + 1) * P
POOLS = (2, 4, 8, 16)
LH, LQK, LNOPE, LROPE, LV = 8, 96, 64, 32, 64
QLAT, KVLAT = 256, 128
LATW = QLAT + KVLAT + LROPE
HR = LROPE // 2
PAD = 8
PADW = S + 2 * PAD

FREE = 1

TWO_PI = 2.0 * math.pi
C1 = 6.28125
C2 = round((TWO_PI - C1) * 2**20) / 2**20
C3 = TWO_PI - C1 - C2
MAGIC = 1.5 * 2**23


def build_program(nc, t, stop_after=3):
    with ExitStack() as ctx:
        def sb(name, shape, dt=F32, where=None):
            return (where or ctx).enter_context(nc.sbuf_tensor(name, shape, dt))

        def sem(name):
            return ctx.enter_context(nc.semaphore(name))

        def overlay(region, size, *sets):
            for n, tensors in enumerate(sets):
                with ExitStack() as own:
                    total = 0
                    for m, tensor in enumerate(tensors):
                        if isinstance(tensor, (int, float)):
                            tensor = (f"{region}_gap{n}_{m}", [P, int(tensor * 256)], F32)
                        name, shape, dt = tensor
                        b[name] = sb(name, shape, dt, own)
                        total += 4 * int(np.prod(shape[1:]))
                    assert total <= size * 1024, (region, n, total)
            sb(region, [P, int(size * 256)])

        slots_run = (ATT0, MIX0, SLOTS, SLOTS)[stop_after]
        b = {}
        w_hi = sb("w_hi", [P, RING, 512], F32R)
        w_lo = sb("w_lo", [P, RING, 512], F32R)
        stage = sb("stage", [P, STAGE, 512])
        ident = sb("ident", [P, P])
        ones = sb("ones", [P, 2])
        eps = sb("eps", [P, 1])
        ccol = sb("ccol", [P, 5, KD])
        gate = sb("gate", [P, D])
        st = sb("st", [P, 192])
        gains = sb("gains", [P, 16])
        qk_rows = sb("qk_rows", [P, 2, LQK])
        ps = ctx.enter_context(nc.psum_tensor("ps", [P, 8, 512], F32))
        psf = ps[:, :, :].rearrange("p b n -> p (b n)")

        overlay("region_h", 64,
                [("ada_a", [P, 3, ADA, 512], F32)],
                [("h_hi", [P, KD, S], F32R), ("h_lo", [P, KD, S], F32R)])
        norm = [("x_in", [P, 2, D], F32), ("xn", [P, 2, D], F32), ("arow", [P, D], F32),
                ("srow", [P, D], F32), ("ngrow", [P, D], F32), ("junk", [P, D], F32)]
        overlay("region_w", 97,
                norm + [("ada_b", [P, 3, ADA, 512], F32), ("mod_row", [1, 512], F32)],
                [("r_q", [P, 2, S], F32), ("r_k", [P, 2, S], F32), ("r_v", [P, NT, 512], F32),
                 ("r_g", [P, NT, 512], F32), ("r_ohi", [P, 4, 512], F32R), ("r_olo", [P, 4, 512], F32R),
                 ("r_tmp", [P, 512], F32), ("r_decay", [P, NT * P], F32), ("r_s", [P, 2, S], F32),
                 ("r_gn", [P, 512], F32), ("r_x", [P, 4, 512], F32),
                 1, ("cos", [P, S], F32), ("sin", [P, S], F32)],
                [48, ("ada_c", [P, ADA, 512], F32), 14, ("acc", [P, 3, 512], F32)],
                [("a_q", [P, GH, S], F32), ("a_k", [P, GH, S], F32), ("a_v", [P, NT, 512], F32),
                 ("a_g", [P, GH, S], F32), ("a_qT", [P, S], F32), ("a_kT", [P, S], F32),
                 ("a_bias", [P, 2, BANDW], F32), ("a_p", [P, 3, BANDW], F32), ("a_pT", [P, 2, BANDW], F32),
                 ("a_o", [P, 512], F32)],
                [("a_ohi", [P, GH, S], F32R), ("a_olo", [P, GH, S], F32R), 32, ("a_x", [P, 4, 512], F32),
                 20, ("a_sq", [P, S], F32)],
                [("l_lat", [P, NT, LATW], F32), ("l_u", [P, 4, PADW], F32), ("l_gp", [P, 4, S], F32),
                 ("l_sum", [P, 2, PADW], F32), ("l_ga", [P, 2, 512], F32), ("l_y", [P, 2, 512], F32),
                 ("l_pw", [P, 4, P], F32), ("l_edge", [P, 4, 2, 8], F32), ("l_e8", [P, 2, 8], F32)],
                [("l_q", [P, NT, LH * LQK], F32), ("l_k", [P, NT, LH * LQK], F32),
                 ("l_v", [P, NT, LH * LV], F32), ("l_tmp", [P, 2, S], F32),
                 ("l_qlhi", [P, 2, S], F32R), ("l_qllo", [P, 2, S], F32R), ("l_klhi", [P, S], F32R),
                 ("l_kllo", [P, S], F32R), ("cos2", [P, NT, HR], F32), ("sin2", [P, NT, HR], F32)],
                [64, ("l_qT", [P, S], F32), ("l_kT", [P, S], F32), ("l_p", [P, 3, S], F32),
                 ("l_pT", [P, 2, S], F32), ("l_sg", [P, 512], F32), ("l_o", [P, 512], F32)],
                [64, ("l_x", [P, 4, 512], F32), ("l_t", [P, 512], F32)])

        (x_in, xn, arow, srow, ngrow, junk, ada_a, ada_b, mod_row, h_hi, h_lo) = (
            b[n] for n in ("x_in", "xn", "arow", "srow", "ngrow", "junk", "ada_a", "ada_b", "mod_row",
                           "h_hi", "h_lo"))
        (r_q, r_k, r_v, r_g, r_ohi, r_olo, r_tmp, r_decay, r_s, r_gn, r_x, cos, sin, ada_c, acc) = (
            b[n] for n in ("r_q", "r_k", "r_v", "r_g", "r_ohi", "r_olo", "r_tmp", "r_decay", "r_s",
                           "r_gn", "r_x", "cos", "sin", "ada_c", "acc"))
        (a_q, a_k, a_v, a_g, a_qT, a_kT, a_bias, a_p, a_pT, a_o, a_ohi, a_olo, a_x, a_sq) = (
            b[n] for n in ("a_q", "a_k", "a_v", "a_g", "a_qT", "a_kT", "a_bias", "a_p", "a_pT", "a_o",
                           "a_ohi", "a_olo", "a_x", "a_sq"))

        (l_lat, l_u, l_gp, l_sum, l_ga, l_y, l_pw, l_edge, l_e8, l_q, l_k, l_v, l_tmp, l_qlhi, l_qllo,
         l_klhi, l_kllo, cos2, sin2, l_qT, l_kT, l_p, l_pT, l_sg, l_o, l_x, l_t) = (
            b[n] for n in ("l_lat", "l_u", "l_gp", "l_sum", "l_ga", "l_y", "l_pw", "l_edge", "l_e8", "l_q",
                           "l_k", "l_v", "l_tmp", "l_qlhi", "l_qllo", "l_klhi", "l_kllo", "cos2", "sin2",
                           "l_qT", "l_kT", "l_p", "l_pT", "l_sg", "l_o", "l_x", "l_t"))

        w_landed = [sem(f"w_landed{n}") for n in range(STAGE)]
        w_rounded = sem("w_rounded")
        w_split = sem("w_split")
        w_used = sem("w_used")
        const_in = sem("const_in")
        ada_in = [sem(f"ada_in{n}") for n in range(PIECES)]
        c_ready = sem("c_ready")
        dve_init = sem("dve_init")
        mod_done = sem("mod_done")
        mod_copied = sem("mod_copied")
        mod_stored = sem("mod_stored")
        pos_in = sem("pos_in")
        res_copied = sem("res_copied")
        rope_chain = sem("rope_chain")
        rope_reduced = sem("rope_reduced")
        rope_tables = sem("rope_tables")
        n_rows = sem("n_rows")
        n_arow = sem("n_arow")
        n_x = [sem(f"n_x{n}") for n in range(2)]
        n_sq = sem("n_sq")
        n_root = sem("n_root")
        n_rr = sem("n_rr")
        n_mul = sem("n_mul")
        n_xn = sem("n_xn")
        n_turned = sem("n_turned")
        n_hi = sem("n_hi")
        n_lo = sem("n_lo")
        dve_r = sem("dve_r")

        bank_done = {l: sem(f"bank_done{l}") for l in "ram"}
        bank_free = {l: sem(f"bank_free{l}") for l in "ram"}
        out_done = {l: sem(f"out_done{l}") for l in "ram"}
        out_free = {l: sem(f"out_free{l}") for l in "ram"}
        out_ready = {l: sem(f"out_ready{l}") for l in "ram"}
        res_in = {l: [sem(f"res_in{l}{n}") for n in range(4)] for l in "ram"}
        res_out = {l: [sem(f"res_out{l}{n}") for n in range(4)] for l in "ram"}

        r_rope = sem("r_rope")
        r_gready = sem("r_gready")
        r_consts = sem("r_consts")
        m_in = sem("m_in")
        m_acc = sem("m_acc")
        m_red = sem("m_red")
        m_row = sem("m_row")
        m_st = sem("m_st")
        r_sdone = sem("r_sdone")
        r_sready = sem("r_sready")
        r_odone = sem("r_odone")
        r_sq = sem("r_sq")
        r_root = sem("r_root")
        r_rinv = sem("r_rinv")
        r_gated = sem("r_gated")
        r_turned = sem("r_turned")
        r_hi = sem("r_hi")
        r_lo = sem("r_lo")

        a_sums = sem("a_sums")
        a_roots = sem("a_roots")
        a_normed = sem("a_normed")
        a_rchain = sem("a_rchain")
        a_biasin = [sem(f"a_biasin{n}") for n in range(2)]
        a_turned = sem("a_turned")
        a_qready = sem("a_qready")
        a_kready = sem("a_kready")
        a_biasok = sem("a_biasok")
        a_sdone = sem("a_sdone")
        a_max = sem("a_max")
        a_neg = sem("a_neg")
        a_exp = sem("a_exp")
        a_rinv = sem("a_rinv")
        a_prob = sem("a_prob")
        a_pdone = sem("a_pdone")
        a_pevac = sem("a_pevac")
        a_odone = sem("a_odone")
        a_gated = sem("a_gated")
        a_hi = sem("a_hi")
        a_lo = sem("a_lo")
        dve_a = sem("dve_a")

        l_consts = sem("l_consts")
        l_chain = sem("l_chain")
        l_angles = sem("l_angles")
        l_tables = sem("l_tables")
        l_pads = sem("l_pads")
        l_sums = sem("l_sums")
        l_roots = sem("l_roots")
        l_latok = sem("l_latok")
        l_gastored = [sem(f"l_gastored{n}") for n in range(2)]
        l_diff = sem("l_diff")
        l_ydone = sem("l_ydone")
        l_yready = sem("l_yready")
        l_yhi = sem("l_yhi")
        l_ylo = sem("l_ylo")
        l_lturned = sem("l_lturned")
        l_lhi = sem("l_lhi")
        l_llo = sem("l_llo")
        l_rcopied = sem("l_rcopied")
        l_updone = sem("l_updone")
        l_upfree = sem("l_upfree")
        l_qsums = sem("l_qsums")
        l_qroots = sem("l_qroots")
        l_qkready = sem("l_qkready")
        l_turned = sem("l_turned")
        l_qready = sem("l_qready")
        l_kready = sem("l_kready")
        l_sdone = sem("l_sdone")
        l_max = sem("l_max")
        l_neg = sem("l_neg")
        l_exp = sem("l_exp")
        l_rinv = sem("l_rinv")
        l_prob = sem("l_prob")
        l_pdone = sem("l_pdone")
        l_pevac = sem("l_pevac")
        l_odone = sem("l_odone")
        l_sgin = sem("l_sgin")
        l_gated = sem("l_gated")
        l_hi = sem("l_hi")
        l_lo = sem("l_lo")

        block = ctx.enter_context(nc.Block())

        @block.sync
        def _(sp):
            for n in range(PIECES):
                buf = ada_a[:, n] if n < 3 else ada_b[:, n - 3]
                sp.dma_start(buf, t["ada"][n]).then_inc(ada_in[n], 16)
            for n in range(STAGE):
                sp.dma_start(stage[:, n], t["w"][n]).then_inc(w_landed[n], 16)
            with sp.Fori(1, slots_run // STAGE) as i:
                for n in range(STAGE):
                    sp.wait_ge(w_split, i * STAGE + (n + 1 - STAGE))
                    sp.dma_start(stage[:, n], t["w"][bass.ds(i * STAGE + n, 1)].rearrange(
                        "a p n -> (a p) n")).then_inc(w_landed[n], 16)

        @block.gpsimd
        def _(pool):
            pool.wait_ge(dve_init, 2)
            with pool.Fori(0, slots_run // RING) as i:
                for n in range(RING):
                    pool.wait_ge(w_landed[n % STAGE], i * (16 * RING // STAGE) + 16 * (n // STAGE + 1))
                    pool.wait_ge(w_used, i * RING + n + 1)
                    pool.tensor_tensor(w_hi[:, n], stage[:, n % STAGE],
                                       ones[:, 0:1].to_broadcast([P, 512]), ALU.mult).then_inc(w_rounded, 1)
                    pool.wait_ge(w_rounded, i * RING + n + 1)
                    pool.tensor_tensor(w_lo[:, n], stage[:, n % STAGE], w_hi[:, n].bitcast(F32),
                                       ALU.subtract).then_inc(w_split, 1)

        @block.tensor
        def _(pe):
            def product(out, a_hi_, a_lo_, b_hi_, b_lo_, first, last):
                pe.matmul(out, a_hi_, b_hi_, start=first, stop=False)
                pe.matmul(out, a_hi_, b_lo_, start=False, stop=False)
                return pe.matmul(out, a_lo_, b_hi_, start=False, stop=last)

            def tokens_first(slot0, l, done0, wait_bank):
                for m in range(NT):
                    wait_bank(m)
                    for k in range(KD):
                        if m == 0:
                            pe.wait_ge(w_split, slot0 + (k + 1))
                        mm = product(ps[:, m % 4], h_hi[:, k, m * P:(m + 1) * P],
                                     h_lo[:, k, m * P:(m + 1) * P], w_hi[:, k], w_lo[:, k],
                                     k == 0, k == KD - 1)
                        if m == NT - 1:
                            mm.then_inc(w_used, 1)
                        elif k == KD - 1:
                            mm.then_inc(bank_done[l], 1)

            def tokens(slot0, l, wait_bank):
                for k in range(KD):
                    pe.wait_ge(w_split, slot0 + (k + 1))
                    for m in range(NT):
                        if k == 0:
                            wait_bank(m)
                        mm = product(ps[:, m], h_hi[:, k, m * P:(m + 1) * P],
                                     h_lo[:, k, m * P:(m + 1) * P], w_hi[:, k], w_lo[:, k],
                                     k == 0, k == KD - 1)
                        if m == NT - 1:
                            mm.then_inc(w_used, 1)
                        elif k == KD - 1:
                            mm.then_inc(bank_done[l], 1)

            def features(slot0, l, wait_bank):
                for k in range(KD):
                    pe.wait_ge(w_split, slot0 + (k + 1))
                    for m in range(4):
                        for a in range(2):
                            if k == 0:
                                wait_bank(2 * m + a)
                            mm = product(ps[:, 2 * m + a], w_hi[:, k, m * P:(m + 1) * P],
                                         w_lo[:, k, m * P:(m + 1) * P], h_hi[:, k, a * 512:(a + 1) * 512],
                                         h_lo[:, k, a * 512:(a + 1) * 512], k == 0, k == KD - 1)
                            if 2 * m + a == 7:
                                mm.then_inc(w_used, 1)
                            elif k == KD - 1:
                                mm.then_inc(bank_done[l], 1)

            def out_unit(l, u, o_hi, o_lo, tok, wait_free, last):
                wait_free(u)
                for k in range(4):
                    mm = product(ps[:, u % 4], o_hi[:, k, tok], o_lo[:, k, tok], w_hi[:, 4 * (u % 2) + k],
                                 w_lo[:, 4 * (u % 2) + k], k == 0, k == 3)
                mm.then_inc(w_used, 8) if last else mm.then_inc(out_done[l], 1)

            def turn_norm(l):
                for m in range(NT):
                    pe.wait_ge(n_xn, l * NT + m + 1)
                    if l or m >= 2:
                        pe.wait_ge(n_lo, l * NT + m - 1)
                    for k in range(KD):
                        tr = pe.transpose(psf[:, (4 + 2 * (m % 2)) * 512 + k * P:][:, 0:P],
                                          xn[:, m % 2, k * P:(k + 1) * P], ident[:, :])
                    tr.then_inc(n_turned, 1)

            pe.sem_inc(w_used, RING)
            for credited in (out_free["r"], out_free["a"], out_ready["r"], out_ready["a"], r_lo, r_sq, a_max,
                             a_lo, *res_out["r"], *res_out["a"]):
                pe.sem_inc(credited, FREE)
            pe.wait_ge(c_ready, 1)
            pe.wait_ge(dve_init, 2)
            for n in range(PIECES):
                pe.wait_ge(ada_in[n], 16)
                buf = ada_a[:, n] if n < 3 else ada_b[:, n - 3]
                for k in range(KD):
                    pe.matmul(ps[0:1, n], ccol[:, 0, k:k + 1], buf[:, k], start=(k == 0), stop=False)
                pe.matmul(ps[0:1, n], ones[:, 0:1], buf[:, KD], start=False, stop=True).then_inc(mod_done, 1)
            pe.wait_ge(const_in, 16 * 3)
            turn_norm(0)

            pe.wait_ge(n_lo, NT)
            with pe.Fori(0, RET_GROUPS) as h:
                w0, f0 = h * RET_SLOTS, h * (3 * NT)
                pe.wait_ge(out_free["r"], h * 16 + FREE)
                tokens_first(w0, "r", 0, lambda m: m >= 4 and pe.wait_ge(bank_free["r"], f0 + (m - 3)))
                features(w0 + 8, "r", lambda n: pe.wait_ge(bank_free["r"], f0 + (n % 4 + 5)))
                tokens(w0 + 16, "r", lambda n: pe.wait_ge(bank_free["r"], f0 + (n + 9)))
                pe.wait_ge(bank_free["r"], f0 + 24)
                pe.wait_ge(r_rope, h + 1)

                def scores(i):
                    if i >= 2:
                        pe.wait_ge(r_sready, h * NT + (i - 1))
                    if i == 4:
                        pe.wait_ge(out_free["r"], h * 16 + 8 + FREE)
                    for j in range(i + 1):
                        for k in range(2):
                            mm = pe.matmul(psf[:, (i % 2) * 1024 + j * P:][:, 0:P], r_k[:, k, j * P:(j + 1) * P],
                                           r_q[:, k, i * P:(i + 1) * P], start=(k == 0), stop=(k == 1))
                    mm.then_inc(r_sdone, 1)

                def values(i):
                    pe.wait_ge(r_sready, h * NT + (i + 1))
                    if i >= 2:
                        pe.wait_ge(r_gated, h * NT + (i - 1))
                    for j in range(i + 1):
                        mm = pe.matmul(ps[:, 4 + i % 2], r_s[:, i % 2, j * P:(j + 1) * P], r_v[:, j],
                                       start=(j == 0), stop=(j == i))
                    mm.then_inc(r_odone, 1)

                def turn(i):
                    pe.wait_ge(r_gated, h * NT + (i + 1))
                    if i:
                        pe.wait_ge(r_lo, h * NT + i + FREE)
                    for e in range(4):
                        tr = pe.transpose(ps[:, 6, e * P:(e + 1) * P], r_g[:, i, e * P:(e + 1) * P], ident[:, :])
                    tr.then_inc(r_turned, 1)

                for a in range(2):
                    scores(4 * a)
                    if a == 0:
                        scores(1)
                        pe.wait_ge(m_acc, h * 3 + 3)
                        for n in range(3):
                            pe.matmul(ps[0:1, 5 + n], ones[:, 0:1], acc[:, n], start=True,
                                      stop=True).then_inc(m_red, 1)
                        pe.wait_ge(m_row, h * 3 + 3)
                    for i in range(4 * a, 4 * a + 4):
                        if i % 4 < 3 and i > 0:
                            scores(i + 1)
                        values(i)
                        if i % 4:
                            turn(i - 1)
                    turn(4 * a + 3)
                    pe.wait_ge(r_lo, h * NT + (4 * a + 4) + FREE)
                    if a == 0:
                        pe.wait_ge(w_split, w0 + RET_SLOTS)
                    for u in range(8 * a, 8 * a + 8):
                        m = (u % 8) // 2
                        out_unit("r", u, r_ohi, r_olo, slice(m * P, (m + 1) * P),
                                 lambda u: u % 8 >= 4 and pe.wait_ge(out_free["r"], h * 16 + (u - 3) + FREE), u == 15)
            if stop_after < 1:
                return
            pe.wait_ge(out_free["r"], RET_GROUPS * 16 + FREE)
            turn_norm(1)

            pe.wait_ge(n_lo, 2 * NT)
            with pe.Fori(0, ATT_GROUPS) as g:
                w0, f0 = g * ATT_SLOTS + ATT0, g * (4 * NT)
                pe.wait_ge(out_free["a"], g * 16 + FREE)
                tokens_first(w0, "a", 0, lambda m: m >= 4 and pe.wait_ge(bank_free["a"], f0 + (m - 3)))
                tokens(w0 + 8, "a", lambda n: pe.wait_ge(bank_free["a"], f0 + (n % 4 + 5)))
                tokens(w0 + 16, "a", lambda n: pe.wait_ge(bank_free["a"], f0 + (n + 9)))
                features(w0 + 24, "a", lambda n: pe.wait_ge(bank_free["a"], f0 + (n + 17)))
                pe.wait_ge(bank_free["a"], f0 + 32)
                pe.wait_ge(a_normed, g * 2 + 2)

                for h in range(GH):
                    e0 = g * (GH * NT) + h * NT

                    if h:
                        pe.wait_ge(a_max, e0 + FREE)
                        pe.wait_ge(a_gated, g * (2 * GH) + 2 * h)
                    for src, bank in ((a_q, 0), (a_k, 2)):
                        for m in range(NT):
                            tr = pe.transpose(psf[:, bank * 512 + m * P:][:, 0:P],
                                              src[:, h, m * P:(m + 1) * P], ident[:, :])
                        tr.then_inc(a_turned, 1)
                    pe.wait_ge(a_qready, g * GH + (h + 1))
                    pe.wait_ge(a_kready, g * GH + (h + 1))

                    def scores(i):
                        if i >= 2:
                            pe.wait_ge(a_max, e0 + (i - 1) + FREE)
                        lo = max(0, i - LEFT) * P
                        width = (i + 1) * P - lo
                        base = (i % 2) * 1024
                        for c in range(0, width, 512):
                            w = min(512, width - c)
                            mm = pe.matmul(psf[:, base + c:base + c + w], a_qT[:, i * P:(i + 1) * P],
                                           a_kT[:, lo + c:lo + c + w], start=True, stop=True)
                        mm.then_inc(a_sdone, 1)

                    def turn(i):
                        pe.wait_ge(a_prob, e0 + (i + 1))
                        if i or h:
                            pe.wait_ge(a_pevac, e0 + i)
                        for n in range(min(i, LEFT) + 1):
                            tr = pe.transpose(psf[:, 4 * 512 + n * P:][:, 0:P],
                                              a_p[:, i % 3, n * P:(n + 1) * P], ident[:, :])
                        tr.then_inc(a_pdone, 1)

                    def values(i):
                        pe.wait_ge(a_pevac, e0 + (i + 1))
                        n = min(i, LEFT) + 1
                        for c in range(n):
                            j = i + 1 - n + c
                            mm = pe.matmul(ps[:, 6 + i // 4, (i % 4) * P:(i % 4 + 1) * P],
                                           a_v[:, j, h * P:(h + 1) * P], a_pT[:, i % 2, c * P:(c + 1) * P],
                                           start=(c == 0), stop=(c == n - 1))
                        mm.then_inc(a_odone, 1)

                    scores(0)
                    scores(1)
                    for i in range(NT):
                        if i + 2 < NT:
                            scores(i + 2)
                        turn(i)
                        if i:
                            values(i - 1)
                    values(NT - 1)
                pe.wait_ge(a_lo, g * (2 * GH) + 2 * GH + FREE)
                pe.wait_ge(w_split, w0 + ATT_SLOTS)
                for u in range(16):
                    m = u // 2
                    out_unit("a", u, a_ohi, a_olo, slice(m * P, (m + 1) * P),
                             lambda u: u >= 4 and pe.wait_ge(out_free["a"], g * 16 + (u - 3) + FREE), u == 15)


            if stop_after < 2:
                return
            pe.wait_ge(out_free["a"], ATT_GROUPS * 16 + FREE)
            turn_norm(2)

            pe.wait_ge(n_lo, 3 * NT)
            tokens_first(MIX0, "m", 0, lambda m: m >= 4 and pe.wait_ge(bank_free["m"], m - 3))
            features(MIX0 + 8, "m", lambda n: pe.wait_ge(bank_free["m"], n % 4 + 5))
            features(MIX0 + 16, "m", lambda n: pe.wait_ge(bank_free["m"], n + 9))
            features(MIX0 + 24, "m", lambda n: pe.wait_ge(bank_free["m"], n + 17))
            pe.wait_ge(bank_free["m"], 32)
            pe.wait_ge(l_consts, 16 * 6)
            for n in range(4):
                pe.wait_ge(l_diff, n + 1)
                for a in range(2):
                    pe.matmul(ps[:, 2 * n + a], l_pw[:, n], l_u[:, n, PAD + 512 * a:PAD + 512 * a + 512],
                              start=True, stop=True).then_inc(l_ydone, 1)
            pe.wait_ge(l_latok, 2)
            for n in range(3):
                pe.wait_ge(l_ylo, 2 * n + 2)
                for m in range(NT):
                    tr = pe.transpose(psf[:, n * 1024 + m * P:][:, 0:P], l_lat[:, m, n * P:(n + 1) * P],
                                      ident[:, :])
                tr.then_inc(l_lturned, 1)
            pe.wait_ge(l_llo, 3)
            pe.wait_ge(l_ylo, 8)
            pe.wait_ge(w_split, MIX0 + 40)
            for m in range(NT):
                if m >= 2:
                    pe.wait_ge(l_upfree, m - 1)
                bank, tok = 4 * (m % 2), slice(m * P, (m + 1) * P)
                for c in range(2):
                    for k in range(2):
                        product(ps[:, bank + c, 0:384], l_qlhi[:, k, tok], l_qllo[:, k, tok],
                                w_hi[:, 2 * c + k, 0:384], w_lo[:, 2 * c + k, 0:384], k == 0, k == 1)
                for c in range(2):
                    mm = product(ps[:, bank + 2 + c], l_klhi[:, tok], l_kllo[:, tok], w_hi[:, 4 + c],
                                 w_lo[:, 4 + c], True, True)
                mm.then_inc(w_used, 8) if m == NT - 1 else mm.then_inc(l_updone, 1)
            pe.wait_ge(l_upfree, NT)
            pe.wait_ge(l_qkready, 2)

            for h in range(LH):
                e0, rows = h * NT, slice(LV * (h % 2), LV * (h % 2) + LV)
                if h:
                    pe.wait_ge(l_exp, e0)
                    pe.wait_ge(l_gated, 2 * h)
                for src, bank in ((l_q, 0), (l_k, 2)):
                    for m in range(NT):
                        tr = pe.transpose(psf[0:LQK, bank * 512 + m * P:][:, 0:P],
                                          src[:, m, h * LQK:(h + 1) * LQK], ident[:, :])
                    tr.then_inc(l_turned, 1)
                pe.wait_ge(l_qready, h + 1)
                pe.wait_ge(l_kready, h + 1)

                def l_scores(i):
                    if i >= 2:
                        pe.wait_ge(l_exp, e0 + i - 1)
                    for c in range(2):
                        mm = pe.matmul(ps[:, 2 * (i % 2) + c], l_qT[0:LQK, i * P:(i + 1) * P],
                                       l_kT[0:LQK, c * 512:(c + 1) * 512], start=True, stop=True)
                    mm.then_inc(l_sdone, 1)

                def l_turn(i):
                    pe.wait_ge(l_prob, e0 + i + 1)
                    if i or h:
                        pe.wait_ge(l_pevac, e0 + i)
                    for n in range(NT):
                        tr = pe.transpose(psf[:, 4 * 512 + n * P:][:, 0:P], l_p[:, i % 3, n * P:(n + 1) * P],
                                          ident[:, :])
                    tr.then_inc(l_pdone, 1)

                def l_values(i):
                    pe.wait_ge(l_pevac, e0 + i + 1)
                    for n in range(NT):
                        mm = pe.matmul(ps[rows, 6 + i // 4, (i % 4) * P:(i % 4 + 1) * P],
                                       l_v[:, n, h * LV:(h + 1) * LV], l_pT[:, i % 2, n * P:(n + 1) * P],
                                       start=(n == 0), stop=(n == NT - 1))
                    mm.then_inc(l_odone, 1)

                l_scores(0)
                l_scores(1)
                for i in range(NT):
                    if i + 2 < NT:
                        l_scores(i + 2)
                    l_turn(i)
                    if i:
                        l_values(i - 1)
                l_values(NT - 1)
            pe.wait_ge(l_lo, 2 * LH)
            for a in range(2):
                for m in range(NT):
                    u = 8 * a + m
                    if u >= 4:
                        pe.wait_ge(out_free["m"], u - 3)
                    for k in range(KD):
                        if m == 0:
                            pe.wait_ge(w_split, MIX0 + 40 + 8 * a + k + 1)
                        mm = product(ps[:, u % 4], h_hi[:, k, m * P:(m + 1) * P], h_lo[:, k, m * P:(m + 1) * P],
                                     w_hi[:, k], w_lo[:, k], k == 0, k == KD - 1)
                        if m == NT - 1:
                            mm.then_inc(w_used, 1)
                        elif k == KD - 1:
                            mm.then_inc(out_done["m"], 1)

        @block.scalar
        def _(act):
            def wait_bank(l, blocks, slots0, done0, blk, n):
                if n < 7:
                    act.wait_ge(bank_done[l], done0 + (7 * blk + n + 1))
                else:
                    act.wait_ge(w_used, slots0 + (RING + 8 * blk + 8))

            def norm_loads(l, m):
                src = t["x"] if l == 0 else t["res"]
                act.dma_start(x_in[:, m % 2], src[m * P:(m + 1) * P, :]).then_inc(n_x[m % 2], 16)

            def norm_layer(l):
                if l:
                    for n in range(4):
                        act.wait_ge(res_out["ra"[l - 1]][n], 16 * 4 * RET_GROUPS + FREE)
                norm_loads(l, 0)
                norm_loads(l, 1)
                if l == 0:
                    act.wait_ge(mod_stored, 16 * 6)
                    act.wait_ge(rope_reduced, 2)
                act.dma_start(arow[:, :], t["mod"][6 * l + 2:6 * l + 4, :].rearrange("a n -> (a n)")
                              .partition_broadcast(P)).then_inc(n_rows, 16)
                act.dma_start(srow[:, :], t["mod"][6 * l:6 * l + 2, :].rearrange("a n -> (a n)")
                              .partition_broadcast(P)).then_inc(n_rows, 16)
                act.dma_start(gate[:, :], t["mod"][6 * l + 4:6 * l + 6, :].rearrange("a n -> (a n)")
                              .partition_broadcast(P)).then_inc(n_rows, 16)
                act.dma_start(ngrow[:, :], t["norm_g"][l].partition_broadcast(P)).then_inc(n_rows, 16)
                for m in range(NT + 1):
                    if m < NT:
                        e = l * NT + m
                        act.wait_ge(n_x[m % 2], 16 * (l * 4 + m // 2 + 1))
                        if e:
                            act.wait_ge(n_sq, e)
                        act.activation(junk[:, :], x_in[:, m % 2], ACT.Square,
                                       accum_out=st[:, m:m + 1]).then_inc(n_sq, 1)
                        act.wait_ge(n_sq, e + 1)
                        act.activation(st[:, 8 + m:9 + m], st[:, m:m + 1], ACT.Sqrt, scale=1.0 / D,
                                       bias=eps[:, 0:1]).then_inc(n_root, 1)
                    if m:
                        e = l * NT + m - 1
                        act.wait_ge(n_turned, e + 1)
                        act.activation(h_hi[:, :, (m - 1) * P:m * P],
                                       psf[:, (4 + 2 * ((m - 1) % 2)) * 512:][:, 0:D].rearrange(
                                           "p (k n) -> p k n", k=KD), ACT.Copy).then_inc(n_hi, 1)
                        if m + 1 < NT:
                            act.wait_ge(n_mul, e + 1)
                            norm_loads(l, m + 1)

            act.dma_start(ident[:, :], t["ident"]).then_inc(const_in, 16)
            act.dma_start(ccol[:, :, :], t["cond"]).then_inc(const_in, 16)
            act.dma_start(gains[:, :], t["gains"]).then_inc(const_in, 16)
            act.dma_start(cos[:, :].bitcast(I32), t["pos"].partition_broadcast(P)).then_inc(pos_in, 16)
            act.dma_start(t["res"], t["x"]).then_inc(res_copied, 16)
            act.wait_ge(const_in, 48)
            act.activation(ccol[:, :, :], ccol[:, :, :], ACT.Silu).then_inc(c_ready, 1)
            act.wait_ge(rope_reduced, 1)
            act.activation(sin[:, :], sin[:, :], ACT.Sin).then_inc(rope_tables, 1)
            act.wait_ge(rope_reduced, 2)
            act.activation(cos[:, :], cos[:, :], ACT.Sin).then_inc(rope_tables, 1)
            for n in range(PIECES):
                act.wait_ge(mod_copied, n + 1)
                act.dma_start(t["mod"][n:n + 1, :], mod_row[:, :]).then_inc(mod_stored, 16)
            norm_layer(0)

            def residual_load(l, j0, u, tok_of):
                m, half = tok_of(u)
                for_unit = t["res"][m * P:(m + 1) * P, half * 512:(half + 1) * 512]
                buf = r_x if l == "r" else a_x
                act.dma_start(buf[:, u % 4], for_unit).then_inc(res_in[l][u % 4], 16)

            def residual_units(l, i, units):
                buf = r_x if l == "r" else a_x
                units = list(units)
                for u in units:
                    m, half = u // 2, u % 2
                    act.wait_ge(out_ready[l], i * 16 + (u + 1) + FREE)
                    act.dma_start(t["res"][m * P:(m + 1) * P, half * 512:(half + 1) * 512],
                                  buf[:, u % 4]).then_inc(res_out[l][u % 4], 16)
                    if u + 3 in units and u + 3 >= units[0] + 4:
                        v = u + 3
                        act.wait_ge(res_out[l][v % 4], i * 64 + 16 * (v // 4) + FREE)
                        residual_load(l, i, v, lambda u: (u // 2, u % 2))

            def first_loads(l, i, units):
                for v in list(units)[0:4]:
                    act.wait_ge(res_out[l][v % 4], i * 64 + 16 * (v // 4) + FREE)
                    residual_load(l, i, v, lambda u: (u // 2, u % 2))

            act.wait_ge(res_copied, 16)
            with act.Fori(0, RET_GROUPS) as h:
                w0, d0 = h * RET_SLOTS, h * 21

                def ada_load(n):
                    act.dma_start(ada_c[:, :, :], t["ada"][bass.ds(h * 3 + (n + PIECES), 1)].rearrange(
                        "a p k n -> (a p) k n")).then_inc(m_in, 16)

                act.wait_ge(w_used, w0 + RING)
                act.wait_ge(r_lo, h * NT + FREE)
                act.wait_ge(out_ready["r"], h * 16 + FREE)
                act.dma_start(r_gn[:, :], t["ret_gn"][bass.ds(h, 1)].rearrange("a n -> (a n)")
                              .partition_broadcast(P)).then_inc(r_consts, 16)
                act.dma_start(r_decay[:, :], t["decay"][bass.ds(h, 1)].rearrange("a p n -> (a p) n"))\
                    .then_inc(r_consts, 16)
                ada_load(0)
                for m in range(NT):
                    wait_bank("r", 3, w0, d0, 0, m)
                    act.activation(r_v[:, m], ps[:, m % 4], ACT.Copy).then_inc(bank_free["r"], 1)
                act.wait_ge(m_acc, h * 3 + 1)
                ada_load(1)
                for n in range(8):
                    wait_bank("r", 3, w0, d0, 1, n)
                    dst = (r_q if n < 4 else r_k)[:, (n // 2) % 2, (n % 2) * 512:(n % 2 + 1) * 512]
                    act.activation(dst, ps[:, n], ACT.Copy).then_inc(bank_free["r"], 1)
                act.wait_ge(m_acc, h * 3 + 2)
                ada_load(2)
                for m in range(NT):
                    wait_bank("r", 3, w0, d0, 2, m)
                    act.activation(r_g[:, m], ps[:, m], ACT.Silu).then_inc(bank_free["r"], 1)

                def squares(i):
                    act.wait_ge(r_odone, h * NT + (i + 1))
                    act.wait_ge(r_sq, h * NT + i + FREE)
                    act.activation(r_tmp[:, :], ps[:, 4 + i % 2], ACT.Square,
                                   accum_out=st[:, 16 + i:17 + i]).then_inc(r_sq, 1)
                    act.wait_ge(r_sq, h * NT + (i + 1) + FREE)
                    act.activation(st[:, 24 + i:25 + i], st[:, 16 + i:17 + i], ACT.Sqrt, scale=1.0 / 512,
                                   bias=eps[:, 0:1]).then_inc(r_root, 1)

                def high(i):
                    act.wait_ge(r_turned, h * NT + (i + 1))
                    act.activation(r_ohi[:, :, (i % 4) * P:(i % 4 + 1) * P],
                                   ps[:, 6].rearrange("p (e n) -> p e n", e=4), ACT.Copy).then_inc(r_hi, 1)

                for n in range(3):
                    act.wait_ge(m_row, h * 3 + (n + 1))
                    act.dma_start(t["mod"][bass.ds(h * 3 + (n + PIECES), 1)], acc[0:1, n]).then_inc(m_st, 16)
                for a in range(2):
                    for i in range(4 * a, 4 * a + 4):
                        squares(i)
                        if i % 4:
                            high(i - 1)
                        if i % 4 == 2:
                            if a == 0:
                                act.wait_ge(m_st, h * 48 + 48)
                            first_loads("r", h, range(8 * a, 8 * a + 8))
                    high(4 * a + 3)
                    residual_units("r", h, range(8 * a, 8 * a + 8))
            if stop_after < 1:
                for n in range(4):
                    act.wait_ge(res_out["r"][n], 64 * RET_GROUPS + FREE)
                return
            norm_layer(1)

            with act.Fori(0, ATT_GROUPS) as g:
                w0, d0 = g * ATT_SLOTS + ATT0, g * 28

                def bias_load(h):
                    act.dma_start(a_bias[:, h % 2], t["band"][bass.ds(g * GH + h, 1)].rearrange(
                        "a p n -> (a p) n")).then_inc(a_biasin[h % 2], 16)

                act.wait_ge(a_max, g * (GH * NT) + FREE)
                act.wait_ge(a_lo, g * (2 * GH) + FREE)
                act.wait_ge(out_ready["a"], g * 16 + FREE)
                bias_load(0)
                for m in range(NT):
                    wait_bank("a", 4, w0, d0, 0, m)
                    act.activation(a_v[:, m], ps[:, m % 4], ACT.Copy).then_inc(bank_free["a"], 1)
                for blk, dst in ((1, a_q), (2, a_k)):
                    for m in range(NT):
                        wait_bank("a", 4, w0, d0, blk, m)
                        act.activation(dst[:, :, m * P:(m + 1) * P],
                                       ps[:, m].rearrange("p (h n) -> p h n", h=GH), ACT.Copy)\
                            .then_inc(bank_free["a"], 1)
                    act.wait_ge(a_sums, g * 2 + blk)
                    c = 32 + 64 * (blk - 1)
                    act.activation(st[:, c + 32:c + 64], st[:, c:c + 32], ACT.Sqrt, scale=1.0 / P,
                                   bias=eps[:, 0:1]).then_inc(a_roots, 1)
                for n in range(8):
                    wait_bank("a", 4, w0, d0, 3, n)
                    act.activation(a_g[:, n // 2, (n % 2) * 512:(n % 2 + 1) * 512], ps[:, n],
                                   ACT.Silu).then_inc(bank_free["a"], 1)
                for h in range(GH):
                    e0 = g * (GH * NT) + h * NT
                    if h + 1 < GH:
                        if h:
                            act.wait_ge(a_max, e0 + FREE)
                        bias_load(h + 1)
                    if h == 0:
                        for n in range(4):
                            act.wait_ge(res_out["a"][n], g * 64 + FREE)
                    act.wait_ge(a_turned, g * (2 * GH) + (2 * h + 1))
                    act.activation(a_qT[:, :], psf[:, 0:S], ACT.Identity,
                                   scale=gains[:, 0:1]).then_inc(a_qready, 1)

                    def exps(i):
                        w = min(i + 1, LEFT + 1) * P
                        act.wait_ge(a_neg, e0 + (i + 1))
                        act.activation(a_p[:, i % 3, 0:w], a_p[:, i % 3, 0:w], ACT.Exp,
                                       bias=st[:, 168 + i % 4:169 + i % 4],
                                       accum_out=st[:, 172 + i % 4:173 + i % 4]).then_inc(a_exp, 1)

                    def evac(i):
                        w = min(i + 1, LEFT + 1) * P
                        act.wait_ge(a_pdone, e0 + (i + 1))
                        if i >= 2:
                            act.wait_ge(a_odone, e0 + (i - 1))
                        act.activation(a_pT[:, i % 2, 0:w], psf[:, 4 * 512:4 * 512 + w], ACT.Copy)\
                            .then_inc(a_pevac, 1)

                    def high(a):
                        act.wait_ge(a_gated, g * (2 * GH) + (2 * h + a + 1))
                        act.activation(a_ohi[:, h, a * 512:(a + 1) * 512], a_o[:, :], ACT.Copy)\
                            .then_inc(a_hi, 1)

                    exps(0)
                    for i in range(NT):
                        if i + 1 < NT:
                            exps(i + 1)
                        evac(i)
                        if i == 5:
                            high(0)
                    high(1)
                first_loads("a", g, range(16))
                residual_units("a", g, range(16))
            if stop_after < 2:
                for n in range(4):
                    act.wait_ge(res_out["a"][n], 64 * ATT_GROUPS + FREE)
                return

            norm_layer(2)

            act.dma_start(l_pw[:, :, :], t["pool_w"]).then_inc(l_consts, 16)
            act.dma_start(l_edge[:, :, :, :], t["edge"]).then_inc(l_consts, 16)
            act.dma_start(st[:, 184:192].bitcast(I32), t["pos2"]).then_inc(l_consts, 16)
            act.dma_start(cos2[:, :, :], t["inv2"].partition_broadcast(P)).then_inc(l_consts, 16)
            act.dma_start(qk_rows[:, 0], t["g_qnorm"].partition_broadcast(P)).then_inc(l_consts, 16)
            act.dma_start(qk_rows[:, 1], t["g_knorm"].partition_broadcast(P)).then_inc(l_consts, 16)
            for m in range(NT):
                wait_bank("m", 4, MIX0, 0, 0, m)
                act.activation(l_lat[:, m], ps[:, m % 4, 0:LATW], ACT.Copy).then_inc(bank_free["m"], 1)
            act.wait_ge(l_angles, 2)
            act.activation(sin2[:, :, :], sin2[:, :, :], ACT.Sin).then_inc(l_tables, 1)
            act.activation(cos2[:, :, :], cos2[:, :, :], ACT.Sin).then_inc(l_tables, 1)
            act.wait_ge(l_sums, 2)
            act.activation(st[:, 16:24], st[:, 0:8], ACT.Sqrt, scale=1.0 / QLAT, bias=eps[:, 0:1])
            act.activation(st[:, 24:32], st[:, 8:16], ACT.Sqrt, scale=1.0 / KVLAT,
                           bias=eps[:, 0:1]).then_inc(l_roots, 1)
            for n in range(8):
                wait_bank("m", 4, MIX0, 0, 1, n)
                act.activation(l_u[:, n // 2, PAD + 512 * (n % 2):PAD + 512 * (n % 2) + 512], ps[:, n],
                               ACT.Copy).then_inc(bank_free["m"], 1)
            for n in range(8):
                wait_bank("m", 4, MIX0, 0, 2, n)
                act.activation(l_gp[:, n // 2, (n % 2) * 512:(n % 2 + 1) * 512], ps[:, n],
                               ACT.Silu).then_inc(bank_free["m"], 1)
            for n in range(8):
                wait_bank("m", 4, MIX0, 0, 3, n)
                if n >= 2:
                    act.wait_ge(l_gastored[n % 2], 16 * (n // 2))
                act.activation(l_ga[:, n % 2], ps[:, n], ACT.Silu).then_inc(bank_free["m"], 1)
                act.wait_ge(bank_free["m"], 24 + n + 1)
                act.dma_start(t["sg"][(n // 2) * P:(n // 2 + 1) * P, (n % 2) * 512:(n % 2 + 1) * 512],
                              l_ga[:, n % 2]).then_inc(l_gastored[n % 2], 16)
            for n in range(8):
                act.wait_ge(l_yready, n + 1)
                act.activation(h_hi[:, n // 2, (n % 2) * 512:(n % 2 + 1) * 512], l_y[:, n % 2],
                               ACT.Copy).then_inc(l_yhi, 1)
            for n in range(3):
                act.wait_ge(l_lturned, n + 1)
                act.activation(l_qlhi[:, n] if n < 2 else l_klhi[:, :], psf[:, n * 1024:(n + 1) * 1024],
                               ACT.Identity, scale=gains[:, 7 + n:8 + n]).then_inc(l_lhi, 1)
            act.wait_ge(l_rcopied, 1)
            for n in range(2):
                act.wait_ge(l_gastored[n], 64)
            for m in range(NT):
                bank = 4 * (m % 2)
                if m < NT - 1:
                    act.wait_ge(l_updone, m + 1)
                else:
                    act.wait_ge(w_used, MIX0 + 40 + RING)
                act.activation(l_q[:, m].rearrange("p (c n) -> p c n", c=2), ps[:, bank:bank + 2, 0:384],
                               ACT.Copy)
                kv = ps[:, bank + 2:bank + 4].rearrange("p c n -> p (c n)").rearrange(
                    "p (h n) -> p h n", h=LH)
                act.activation(l_k[:, m].rearrange("p (h n) -> p h n", h=LH)[:, :, 0:LNOPE],
                               kv[:, :, 0:LNOPE], ACT.Copy)
                act.activation(l_v[:, m].rearrange("p (h n) -> p h n", h=LH), kv[:, :, LNOPE:],
                               ACT.Copy).then_inc(l_upfree, 1)
            for n in range(2):
                act.wait_ge(l_qsums, n + 1)
                act.activation(st[:, 64 + 64 * n:128 + 64 * n], st[:, 64 * n:64 * n + 64], ACT.Sqrt,
                               scale=1.0 / LQK, bias=eps[:, 0:1]).then_inc(l_qroots, 1)

            def gate_load(n):
                h, a = n // 2, n % 2
                rows = slice(LV * (h % 2), LV * (h % 2) + LV)
                act.dma_start(l_sg[rows, :], t["sg"][h * LV:(h + 1) * LV, a * 512:(a + 1) * 512])\
                   .then_inc(l_sgin, 16)

            act.wait_ge(l_llo, 3)
            act.wait_ge(w_used, MIX0 + 40 + RING)
            gate_load(0)
            for h in range(LH):
                e0 = h * NT
                rows = slice(LV * (h % 2), LV * (h % 2) + LV)
                act.wait_ge(l_turned, 2 * h + 1)
                act.activation(l_qT[0:LQK, :], psf[0:LQK, 0:S], ACT.Copy,
                               scale=LQK ** -0.5).then_inc(l_qready, 1)

                def l_exps(i):
                    act.wait_ge(l_neg, e0 + i + 1)
                    if i >= 3 or h:
                        act.wait_ge(l_pdone, e0 + i - 2)
                    act.activation(l_p[:, i % 3], psf[:, (i % 2) * 1024:(i % 2) * 1024 + S], ACT.Exp,
                                   bias=st[:, 4 + i % 4:5 + i % 4], accum_out=st[:, 8 + i % 4:9 + i % 4])\
                       .then_inc(l_exp, 1)

                def l_evac(i):
                    act.wait_ge(l_pdone, e0 + i + 1)
                    if i >= 2 or h:
                        act.wait_ge(l_odone, e0 + i - 1)
                    act.activation(l_pT[:, i % 2], psf[:, 4 * 512:4 * 512 + S], ACT.Copy).then_inc(l_pevac, 1)

                def l_high(a):
                    act.wait_ge(l_gated, 2 * h + a + 1)
                    act.activation(h_hi[rows, 4 + h // 2, a * 512:(a + 1) * 512], l_o[rows, :],
                                   ACT.Copy).then_inc(l_hi, 1)
                    if 2 * h + a + 1 < 2 * LH:
                        gate_load(2 * h + a + 1)

                l_exps(0)
                for i in range(NT):
                    if i + 1 < NT:
                        l_exps(i + 1)
                    l_evac(i)
                    if i == 5:
                        l_high(0)
                l_high(1)
            def unit(u):
                return slice((u % 8) * P, (u % 8 + 1) * P), slice((u // 8) * 512, (u // 8 + 1) * 512)

            for u in range(19):
                if 3 <= u:
                    v = u - 3
                    act.wait_ge(out_ready["m"], v + 1)
                    act.dma_start(t["out"][unit(v)], l_x[:, v % 4]).then_inc(res_out["m"][v % 4], 16)
                if u < 16:
                    if u >= 4:
                        act.wait_ge(res_out["m"][u % 4], 16 * (u // 4))
                    act.dma_start(l_x[:, u % 4], t["res"][unit(u)]).then_inc(res_in["m"][u % 4], 16)
            for n in range(4):
                act.wait_ge(res_out["m"][n], 64)

        @block.vector
        def _(dve):
            links = [0]

            def link(ins, chain, base=0):
                links[0] += 1
                ins.then_inc(chain, 1)
                dve.wait_ge(chain, base + links[0])

            dve.memset(eps[:, :], EPS).then_inc(dve_init, 1)
            dve.memset(ones[:, :], 1.0).then_inc(dve_init, 1)
            dve.wait_ge(dve_init, 2)
            ang, turns = xn[:, 0], xn[:, 1]
            dve.wait_ge(pos_in, 16)
            dve.wait_ge(const_in, 48)
            link(dve.tensor_copy(ang, cos[:, :].bitcast(I32)), rope_chain)
            link(dve.tensor_scalar(ang, ang, gains[:, 2:3], None, ALU.mult), rope_chain)
            for table, quarter in ((sin, 0.0), (cos, 0.25)):
                link(dve.tensor_scalar(turns, ang, 1.0 / TWO_PI, quarter, ALU.mult, ALU.add), rope_chain)
                link(dve.tensor_scalar(turns, turns, MAGIC, MAGIC, ALU.add, ALU.subtract), rope_chain)
                link(dve.scalar_tensor_tensor(table[:, :], turns, -C1, ang, ALU.mult, ALU.add), rope_chain)
                link(dve.scalar_tensor_tensor(table[:, :], turns, -C2, table[:, :], ALU.mult, ALU.add),
                     rope_chain)
                link(dve.scalar_tensor_tensor(table[:, :], turns, -C3, table[:, :], ALU.mult, ALU.add),
                     rope_chain)
                link(dve.tensor_scalar(table[:, :], table[:, :], quarter * TWO_PI, math.pi, ALU.add, ALU.min),
                     rope_chain)
                dve.tensor_scalar(table[:, :], table[:, :], -math.pi, None, ALU.max).then_inc(rope_reduced, 1)
            link(dve.tensor_scalar(gains[:, 0:1], gains[:, 0:1], P ** -0.5, None, ALU.mult), rope_chain)
            for n in range(PIECES):
                dve.wait_ge(mod_done, n + 1)
                if n:
                    dve.wait_ge(mod_stored, 16 * n)
                dve.tensor_copy(mod_row[:, :], ps[0:1, n]).then_inc(mod_copied, 1)

            def norm_layer(l):
                dve.wait_ge(n_rows, 64 * (l + 1))
                dve.scalar_tensor_tensor(arow[:, :], arow[:, :], 1.0, ngrow[:, :], ALU.add,
                                         ALU.mult).then_inc(n_arow, 1)
                dve.wait_ge(n_arow, l + 1)
                for m in range(NT + 1):
                    if m < NT:
                        e = l * NT + m
                        dve.wait_ge(n_root, e + 1)
                        dve.reciprocal(st[:, 8 + m:9 + m], st[:, 8 + m:9 + m]).then_inc(n_rr, 1)
                        dve.wait_ge(n_rr, e + 1)
                        if m >= 2 or l:
                            dve.wait_ge(n_turned, e - 1 if m >= 2 else l * NT)
                        dve.scalar_tensor_tensor(xn[:, m % 2], x_in[:, m % 2], st[:, 8 + m:9 + m], arow[:, :],
                                                 ALU.mult, ALU.mult).then_inc(n_mul, 1)
                        dve.wait_ge(n_mul, e + 1)
                        dve.tensor_tensor(xn[:, m % 2], xn[:, m % 2], srow[:, :], ALU.add).then_inc(n_xn, 1)
                    if m:
                        e = l * NT + m - 1
                        sl = slice((m - 1) * P, m * P)
                        dve.wait_ge(n_hi, e + 1)
                        dve.tensor_tensor(h_lo[:, :, sl], psf[:, (4 + 2 * ((m - 1) % 2)) * 512:][:, 0:D]
                                          .rearrange("p (k n) -> p k n", k=KD), h_hi[:, :, sl].bitcast(F32),
                                          ALU.subtract).then_inc(n_lo, 1)

            norm_layer(0)

            def residual(l, i, units, tmp, chain, base):
                buf = r_x if l == "r" else a_x
                for u in units:
                    if u == 15:
                        slots = (RET_SLOTS, 0) if l == "r" else (ATT_SLOTS, ATT0)
                        dve.wait_ge(w_used, i * slots[0] + (slots[0] + slots[1] + RING))
                    else:
                        dve.wait_ge(out_done[l], i * 15 + (u + 1))
                    if u:
                        dve.wait_ge(out_ready[l], i * 16 + u + FREE)
                    dve.tensor_tensor(tmp, ps[:, u % 4], gate[:, (u % 2) * 512:(u % 2 + 1) * 512],
                                      ALU.mult).then_inc(out_free[l], 1)
                    dve.wait_ge(out_free[l], i * 16 + (u + 1) + FREE)
                    dve.wait_ge(res_in[l][u % 4], i * 64 + 16 * (u // 4 + 1))
                    dve.tensor_tensor(buf[:, u % 4], buf[:, u % 4], tmp, ALU.add).then_inc(out_ready[l], 1)

            RL = 1 + 3 * (KD - 1) + 5
            dve.wait_ge(rope_tables, 2)
            with dve.Fori(0, RET_GROUPS) as h:
                links[0] = 0
                base = h * RL

                def modulation(n):
                    dve.wait_ge(m_in, h * 48 + 16 * (n + 1))
                    for k in range(KD):
                        other = ada_c[:, KD] if k == 0 else acc[:, n]
                        ins = dve.scalar_tensor_tensor(acc[:, n], ada_c[:, k], cnext[:, k:k + 1], other,
                                                       ALU.mult, ALU.add)
                        if k < KD - 1:
                            link(ins, dve_r, base)
                        else:
                            ins.then_inc(m_acc, 1)

                for n in range(4):
                    dve.wait_ge(res_out["r"][n], h * 64 + FREE)
                dve.wait_ge(w_used, h * RET_SLOTS + RING)
                cnext = st[:, 176:176 + KD]
                link(dve.tensor_copy(cnext, ccol[:, :, :].rearrange("p l k -> p (l k)")[
                    :, bass.ds(h * KD + KD, KD)]), dve_r, base)
                modulation(0)
                modulation(1)
                dve.wait_ge(bank_free["r"], h * 24 + 16)
                for src in (r_q, r_k):
                    first, second = src[:, 0], src[:, 1]
                    dve.tensor_tensor(r_s[:, 0], first, sin[:, :], ALU.mult)
                    link(dve.tensor_tensor(r_s[:, 1], second, sin[:, :], ALU.mult), dve_r, base)
                    dve.tensor_tensor(first, first, cos[:, :], ALU.mult)
                    link(dve.tensor_tensor(second, second, cos[:, :], ALU.mult), dve_r, base)
                    dve.tensor_tensor(first, first, r_s[:, 1], ALU.subtract)
                    ins = dve.tensor_tensor(second, second, r_s[:, 0], ALU.add)
                    if src is r_q:
                        link(ins, dve_r, base)
                    else:
                        ins.then_inc(r_rope, 1)
                modulation(2)
                dve.wait_ge(r_consts, h * 32 + 32)
                for m in range(NT):
                    dve.wait_ge(bank_free["r"], h * 24 + (17 + m))
                    dve.tensor_tensor(r_g[:, m], r_g[:, m], r_gn[:, :], ALU.mult).then_inc(r_gready, 1)
                dve.wait_ge(r_rope, h + 1)

                def decay(i):
                    dve.wait_ge(r_sdone, h * NT + (i + 1))
                    if i >= 2:
                        dve.wait_ge(r_odone, h * NT + (i - 1))
                    w = (i + 1) * P
                    dve.tensor_tensor(r_s[:, i % 2, 0:w], psf[:, (i % 2) * 1024:(i % 2) * 1024 + w],
                                      r_decay[:, (NT - 1 - i) * P:], ALU.mult).then_inc(r_sready, 1)

                def gated(i):
                    dve.wait_ge(r_root, h * NT + (i + 1))
                    dve.reciprocal(st[:, 24 + i:25 + i], st[:, 24 + i:25 + i]).then_inc(r_rinv, 1)
                    dve.wait_ge(r_rinv, h * NT + (i + 1))
                    dve.wait_ge(r_gready, h * NT + (i + 1))
                    dve.scalar_tensor_tensor(r_g[:, i], ps[:, 4 + i % 2], st[:, 24 + i:25 + i], r_g[:, i],
                                             ALU.mult, ALU.mult).then_inc(r_gated, 1)

                def low(i):
                    sl = slice((i % 4) * P, (i % 4 + 1) * P)
                    dve.wait_ge(r_hi, h * NT + (i + 1))
                    dve.tensor_tensor(r_olo[:, :, sl], ps[:, 6].rearrange("p (e n) -> p e n", e=4),
                                      r_ohi[:, :, sl].bitcast(F32), ALU.subtract).then_inc(r_lo, 1)

                for a in range(2):
                    decay(4 * a)
                    if a == 0:
                        decay(1)
                        for n in range(3):
                            dve.wait_ge(m_red, h * 3 + (n + 1))
                            dve.tensor_copy(acc[0:1, n], ps[0:1, 5 + n]).then_inc(m_row, 1)
                    for i in range(4 * a, 4 * a + 4):
                        if i % 4 < 3 and i > 0:
                            decay(i + 1)
                        gated(i)
                        if i % 4:
                            low(i - 1)
                    low(4 * a + 3)
                    residual("r", h, range(8 * a, 8 * a + 8), r_tmp[:, :], dve_r, base)
            assert links[0] == RL, links
            if stop_after < 1:
                return
            norm_layer(1)

            AL = 2 * (2 * GH - 1)
            with dve.Fori(0, ATT_GROUPS) as g:
                links[0] = 0
                base = g * AL
                for blk, src in ((1, a_q), (2, a_k)):
                    dve.wait_ge(bank_free["a"], g * 32 + 8 * (blk + 1))
                    c = 32 + 64 * (blk - 1)
                    for h in range(GH):
                        link(dve.tensor_tensor(a_sq[:, :], src[:, h], src[:, h], ALU.mult), dve_a, base)
                        ins = dve.tensor_reduce(st[:, c + 8 * h:c + 8 * h + 8],
                                                a_sq[:, :].rearrange("p (m n) -> p m n", m=NT), AX.X, ALU.add)
                        if h < GH - 1:
                            link(ins, dve_a, base)
                        else:
                            ins.then_inc(a_sums, 1)
                    dve.wait_ge(a_sums, g * 2 + blk)
                    dve.wait_ge(a_roots, g * 2 + blk)
                    r = st[:, c + 32:c + 64]
                    dve.reciprocal(r, r).then_inc(a_rchain, 1)
                    dve.wait_ge(a_rchain, g * 2 + blk)
                    whole = src[:, :, :].rearrange("p h (m n) -> p (h m) n", m=NT)
                    dve.tensor_tensor(whole, whole, r.unsqueeze(2).to_broadcast([P, GH * NT, P]),
                                      ALU.mult).then_inc(a_normed, 1)
                for h in range(GH):
                    e0 = g * (GH * NT) + h * NT
                    dve.wait_ge(a_biasin[h % 2], g * 32 + 16 * (h // 2 + 1))
                    dve.memset(a_bias[64:128, h % 2, 0:64], NEG).then_inc(a_biasok, 1)
                    dve.memset(a_bias[0:64, h % 2, BANDW - 64:BANDW], NEG).then_inc(a_biasok, 1)
                    if h == 0:
                        for n in range(4):
                            dve.wait_ge(res_out["a"][n], g * 64 + FREE)
                    dve.wait_ge(a_turned, g * (2 * GH) + (2 * h + 2))
                    dve.tensor_scalar(a_kT[:, :], psf[:, 1024:1024 + S], gains[:, 1:2], None,
                                      ALU.mult).then_inc(a_kready, 1)
                    dve.wait_ge(a_biasok, g * (2 * GH) + (2 * h + 2))

                    def maxima(i):
                        w = min(i + 1, LEFT + 1) * P
                        dve.wait_ge(a_sdone, e0 + (i + 1))
                        if i >= 3:
                            dve.wait_ge(a_pdone, e0 + (i - 2))
                        dve.memset(st[:, 160:161], 0.0)
                        dve.tensor_tensor_reduce(a_p[:, i % 3, 0:w], psf[:, (i % 2) * 1024:(i % 2) * 1024 + w],
                                                 a_bias[:, h % 2, BANDW - w:], 1.0, -3.0e38, ALU.add, ALU.max,
                                                 st[:, 164 + i % 4:165 + i % 4]).then_inc(a_max, 1)
                        dve.wait_ge(a_max, e0 + (i + 1) + FREE)
                        dve.tensor_scalar(st[:, 168 + i % 4:169 + i % 4], st[:, 164 + i % 4:165 + i % 4], -1.0,
                                          None, ALU.mult).then_inc(a_neg, 1)

                    def normed(i):
                        w = min(i + 1, LEFT + 1) * P
                        dve.wait_ge(a_exp, e0 + (i + 1))
                        r = st[:, 172 + i % 4:173 + i % 4]
                        dve.reciprocal(r, r).then_inc(a_rinv, 1)
                        dve.wait_ge(a_rinv, e0 + (i + 1))
                        dve.tensor_scalar(a_p[:, i % 3, 0:w], a_p[:, i % 3, 0:w], r, None,
                                          ALU.mult).then_inc(a_prob, 1)

                    def gated(a):
                        n = 2 * h + a
                        dve.wait_ge(a_odone, e0 + (4 * a + 4))
                        dve.tensor_tensor(a_o[:, :], ps[:, 6 + a], a_g[:, h, a * 512:(a + 1) * 512],
                                          ALU.mult).then_inc(a_gated, 1)

                    def low(a):
                        dve.wait_ge(a_hi, g * (2 * GH) + (2 * h + a + 1))
                        dve.tensor_tensor(a_olo[:, h, a * 512:(a + 1) * 512], a_o[:, :],
                                          a_ohi[:, h, a * 512:(a + 1) * 512].bitcast(F32),
                                          ALU.subtract).then_inc(a_lo, 1)

                    maxima(0)
                    for i in range(NT):
                        if i + 1 < NT:
                            maxima(i + 1)
                        normed(i)
                        if i == 4:
                            gated(0)
                        if i == 6:
                            low(0)
                    gated(1)
                    low(1)
                residual("a", g, range(16), a_o[:, :], dve_a, base)
            assert links[0] == AL, links
            if stop_after < 2:
                return
            norm_layer(2)

            links[0] = 0
            for n in range(4):
                dve.memset(l_u[:, n, 0:PAD], 0.0)
                dve.memset(l_u[:, n, PAD + S:PADW], 0.0).then_inc(l_pads, 1)
            dve.wait_ge(l_consts, 16 * 6)
            fr, ang, turns = l_tmp[:, 0, 0:P], l_tmp[:, 0, P:2 * P], l_tmp[:, 0, 2 * P:3 * P]
            fr, ang, turns = (v.rearrange("p (m n) -> p m n", m=NT) for v in (fr, ang, turns))
            link(dve.tensor_copy(fr[:, :, 0], st[:, 184:192].bitcast(I32)), l_chain)
            link(dve.tensor_tensor(ang, cos2[:, :, :], fr[:, :, 0:1].to_broadcast([P, NT, HR]), ALU.mult), l_chain)
            for table, quarter in ((sin2, 0.0), (cos2, 0.25)):
                link(dve.tensor_scalar(turns, ang, 1.0 / TWO_PI, quarter, ALU.mult, ALU.add), l_chain)
                link(dve.tensor_scalar(turns, turns, MAGIC, MAGIC, ALU.add, ALU.subtract), l_chain)
                link(dve.scalar_tensor_tensor(table[:, :, :], turns, -C1, ang, ALU.mult, ALU.add), l_chain)
                link(dve.scalar_tensor_tensor(table[:, :, :], turns, -C2, table[:, :, :], ALU.mult, ALU.add),
                     l_chain)
                link(dve.scalar_tensor_tensor(table[:, :, :], turns, -C3, table[:, :, :], ALU.mult, ALU.add),
                     l_chain)
                link(dve.tensor_scalar(table[:, :, :], table[:, :, :], quarter * TWO_PI, math.pi, ALU.add,
                                       ALU.min), l_chain)
                dve.tensor_scalar(table[:, :, :], table[:, :, :], -math.pi, None, ALU.max).then_inc(l_angles, 1)
            dve.wait_ge(bank_free["m"], 8)
            for n, (lo, width) in enumerate(((0, QLAT), (QLAT, KVLAT))):
                part = l_lat[:, :, lo:lo + width]
                sq = l_tmp[:, :, :].rearrange("p a n -> p (a n)")[:, 0:NT * width].rearrange(
                    "p (m n) -> p m n", m=NT)
                link(dve.tensor_tensor(sq, part, part, ALU.mult), l_chain)
                dve.tensor_reduce(st[:, 8 * n:8 * n + 8], sq, AX.X, ALU.add).then_inc(l_sums, 1)
                dve.wait_ge(l_sums, n + 1)
            dve.wait_ge(l_roots, 1)
            link(dve.reciprocal(st[:, 16:32], st[:, 16:32]), l_chain)
            for n, (lo, width) in enumerate(((0, QLAT), (QLAT, KVLAT))):
                part = l_lat[:, :, lo:lo + width]
                r = st[:, 16 + 8 * n:24 + 8 * n].unsqueeze(2).to_broadcast([P, NT, width])
                dve.tensor_tensor(part, part, r, ALU.mult).then_inc(l_latok, 1)
            dve.wait_ge(l_pads, 4)
            for n, window in enumerate(POOLS):
                dve.wait_ge(bank_free["m"], 8 + 2 * n + 2)
                src, step, lo = l_u[:, n], 1, 1
                link(dve.tensor_tensor(l_sum[:, 0, 1:PADW], l_u[:, n, 1:PADW], l_u[:, n, 0:PADW - 1],
                                       ALU.add), l_chain)
                cur, reach, lo, hi = 0, 1, 1, PADW
                while 2 * reach < window:
                    lo, hi = lo + reach, hi - reach
                    link(dve.tensor_tensor(l_sum[:, 1 - cur, lo:hi], l_sum[:, cur, lo - reach:hi - reach],
                                           l_sum[:, cur, lo + reach:hi + reach], ALU.add), l_chain)
                    cur, reach = 1 - cur, 2 * reach
                sums = l_sum[:, cur]
                for e, c in enumerate((PAD, PAD + S - 8)):
                    link(dve.tensor_tensor(l_e8[:, e], sums[:, c:c + 8], l_edge[:, n, e], ALU.mult), l_chain)
                for e, c in enumerate((PAD, PAD + S - 8)):
                    link(dve.tensor_tensor(l_u[:, n, c:c + 8], l_e8[:, e], l_u[:, n, c:c + 8],
                                           ALU.subtract), l_chain)
                inner = slice(PAD + 8, PAD + S - 8)
                dve.scalar_tensor_tensor(l_u[:, n, inner], sums[:, inner], 1.0 / window, l_u[:, n, inner],
                                         ALU.mult, ALU.subtract).then_inc(l_diff, 1)
                dve.wait_ge(l_diff, n + 1)
            for n in range(9):
                if n < 8:
                    dve.wait_ge(l_ydone, n + 1)
                    if n >= 2:
                        dve.wait_ge(l_ylo, n - 1)
                    dve.scalar_tensor_tensor(l_y[:, n % 2], ps[:, n], gains[:, 3 + n // 2:4 + n // 2],
                                             l_gp[:, n // 2, (n % 2) * 512:(n % 2 + 1) * 512], ALU.mult,
                                             ALU.mult).then_inc(l_yready, 1)
                if n:
                    v = n - 1
                    sl = slice((v % 2) * 512, (v % 2 + 1) * 512)
                    dve.wait_ge(l_yhi, v + 1)
                    dve.tensor_tensor(h_lo[:, v // 2, sl], l_y[:, v % 2], h_hi[:, v // 2, sl].bitcast(F32),
                                      ALU.subtract).then_inc(l_ylo, 1)
            for n in range(3):
                dve.wait_ge(l_lhi, n + 1)
                hi, lo = (l_qlhi[:, n], l_qllo[:, n]) if n < 2 else (l_klhi[:, :], l_kllo[:, :])
                dve.scalar_tensor_tensor(lo, psf[:, n * 1024:(n + 1) * 1024], gains[:, 7 + n:8 + n],
                                         hi.bitcast(F32), ALU.mult, ALU.subtract).then_inc(l_llo, 1)
            def heads(x):
                return x[:, :, :].rearrange("p m (h n) -> p m h n", h=LH)

            dve.wait_ge(l_ydone, 8)
            dve.tensor_copy(heads(l_k)[:, :, :, LNOPE:], l_lat[:, :, QLAT + KVLAT:].unsqueeze(2)
                            .to_broadcast([P, NT, LH, LROPE])).then_inc(l_rcopied, 1)
            dve.wait_ge(l_rcopied, 1)
            dve.wait_ge(l_tables, 2)
            dve.wait_ge(l_upfree, NT)
            for n, src in enumerate((l_q, l_k)):
                flat = src[:, :, :].rearrange("p m (h n) -> p (m h) n", h=LH)
                for m in range(0, NT, 2):
                    sq = l_tmp[:, :, :].rearrange("p a n -> p (a n)")[:, 0:2 * LH * LQK].rearrange(
                        "p (e n) -> p e n", n=LQK)
                    part = flat[:, m * LH:(m + 2) * LH]
                    link(dve.tensor_tensor(sq, part, part, ALU.mult), l_chain)
                    c = 64 * n + m * LH
                    ins = dve.tensor_reduce(st[:, c:c + 2 * LH], sq, AX.X, ALU.add)
                    if m < NT - 2:
                        link(ins, l_chain)
                    else:
                        ins.then_inc(l_qsums, 1)
                dve.wait_ge(l_qroots, n + 1)
                r = st[:, 64 + 64 * n:128 + 64 * n]
                link(dve.reciprocal(r, r), l_chain)
                link(dve.tensor_tensor(flat, flat, r.unsqueeze(2).to_broadcast([P, NT * LH, LQK]), ALU.mult),
                     l_chain)
                link(dve.tensor_tensor(flat, flat, qk_rows[:, n].unsqueeze(1).to_broadcast(
                    [P, NT * LH, LQK]), ALU.mult), l_chain)
                x1 = heads(src)[:, :, :, LNOPE:LNOPE + HR]
                x2 = heads(src)[:, :, :, LNOPE + HR:]
                cs = cos2[:, :, :].unsqueeze(2).to_broadcast([P, NT, LH, HR])
                sn = sin2[:, :, :].unsqueeze(2).to_broadcast([P, NT, LH, HR])
                t1, t2 = (l_tmp[:, a].rearrange("p (m h n) -> p m h n", m=NT, h=LH) for a in range(2))
                link(dve.tensor_tensor(t1, x1, sn, ALU.mult), l_chain)
                link(dve.tensor_tensor(t2, x2, sn, ALU.mult), l_chain)
                link(dve.tensor_tensor(x1, x1, cs, ALU.mult), l_chain)
                link(dve.tensor_tensor(x2, x2, cs, ALU.mult), l_chain)
                link(dve.tensor_tensor(x1, x1, t2, ALU.subtract), l_chain)
                dve.tensor_tensor(x2, x2, t1, ALU.add).then_inc(l_qkready, 1)
                dve.wait_ge(l_qkready, n + 1)

            for h in range(LH):
                e0 = h * NT
                rows = slice(LV * (h % 2), LV * (h % 2) + LV)
                dve.wait_ge(l_turned, 2 * h + 2)
                dve.tensor_copy(l_kT[0:LQK, :], psf[0:LQK, 1024:1024 + S]).then_inc(l_kready, 1)

                def l_maxima(i):
                    dve.wait_ge(l_sdone, e0 + i + 1)
                    dve.tensor_reduce(st[:, i % 4:i % 4 + 1], psf[:, (i % 2) * 1024:(i % 2) * 1024 + S], AX.X,
                                      ALU.max).then_inc(l_max, 1)
                    dve.wait_ge(l_max, e0 + i + 1)
                    dve.tensor_scalar(st[:, 4 + i % 4:5 + i % 4], st[:, i % 4:i % 4 + 1], -1.0, None,
                                      ALU.mult).then_inc(l_neg, 1)

                def l_normed(i):
                    dve.wait_ge(l_exp, e0 + i + 1)
                    r = st[:, 8 + i % 4:9 + i % 4]
                    dve.reciprocal(r, r).then_inc(l_rinv, 1)
                    dve.wait_ge(l_rinv, e0 + i + 1)
                    dve.tensor_scalar(l_p[:, i % 3], l_p[:, i % 3], r, None, ALU.mult).then_inc(l_prob, 1)

                def l_gate(a):
                    dve.wait_ge(l_odone, e0 + 4 * a + 4)
                    dve.wait_ge(l_sgin, 16 * (2 * h + a + 1))
                    dve.tensor_tensor(l_o[rows, :], ps[rows, 6 + a], l_sg[rows, :], ALU.mult)\
                       .then_inc(l_gated, 1)

                def l_low(a):
                    sl = slice(a * 512, (a + 1) * 512)
                    dve.wait_ge(l_hi, 2 * h + a + 1)
                    dve.tensor_tensor(h_lo[rows, 4 + h // 2, sl], l_o[rows, :],
                                      h_hi[rows, 4 + h // 2, sl].bitcast(F32), ALU.subtract).then_inc(l_lo, 1)

                l_maxima(0)
                for i in range(NT):
                    if i + 1 < NT:
                        l_maxima(i + 1)
                    l_normed(i)
                    if i == 4:
                        l_gate(0)
                    if i == 6:
                        l_low(0)
                l_gate(1)
                l_low(1)
            for u in range(16):
                if u % 8 == 7:
                    dve.wait_ge(w_used, MIX0 + 40 + u + 1 + RING)
                else:
                    dve.wait_ge(out_done["m"], u - u // 8 + 1)
                if u:
                    dve.wait_ge(out_ready["m"], u)
                dve.tensor_tensor(l_t[:, :], ps[:, u % 4], gate[:, (u // 8) * 512:(u // 8 + 1) * 512],
                                  ALU.mult).then_inc(out_free["m"], 1)
                dve.wait_ge(out_free["m"], u + 1)
                dve.wait_ge(res_in["m"][u % 4], 16 * (u // 4 + 1))
                dve.tensor_tensor(l_x[:, u % 4], l_x[:, u % 4], l_t[:, :], ALU.add).then_inc(out_ready["m"], 1)


SCRATCH = {"sg": (512, 1024)}


def lay_out(inputs):
    f = {k: np.asarray(v) for k, v in inputs.items()}
    w = []

    def slots(m):
        w.extend(m.reshape(-1, P, 512))

    def halves(m):
        slots(m[:, :512])
        slots(m[:, 512:])

    wi, wo = f["ret_w_in"][0], f["ret_w_out"][0]
    for h in range(4):
        slots(wi[:, 2048 + 512 * h:2560 + 512 * h])
        slots(np.concatenate([wi[:, 256 * h:256 * h + 256], wi[:, 1024 + 256 * h:1280 + 256 * h]], 1))
        slots(wi[:, 4096 + 512 * h:4608 + 512 * h])
        halves(wo[512 * h:512 * h + 512])
    wi, wo = f["att_w_in"][0], f["att_w_out"][0]
    for g in range(4):
        for part in (2, 0, 1, 3):
            slots(wi[:, 2048 * part + 512 * g:2048 * part + 512 * g + 512])
        halves(wo[512 * g:512 * g + 512])
    wi = f["w_in_2"][0]
    slots(np.pad(wi[:, 1024:1440], ((0, 0), (0, 96))))
    slots(wi[:, 0:512])
    slots(wi[:, 512:1024])
    slots(wi[:, 1440:1952])
    uq = f["w_uq_2"][0]
    for c in range(2):
        slots(np.pad(uq[:, 384 * c:384 * c + 384], ((0, 0), (0, 128))))
    uk = f["w_ukv_2"][0]
    slots(uk[:, :512])
    slots(uk[:, 512:])
    w.extend([np.zeros((P, 512), np.float32)] * 2)
    halves(f["w_out_2"][0])
    w = np.stack(w)
    assert w.shape[0] == SLOTS, w.shape

    aw = np.concatenate([f["ada_w"], f["ada_w_2"]])
    ab = np.concatenate([f["ada_b"], f["ada_b_2"]])
    aw = aw.reshape(3, KD, P, PIECES, 512).transpose(0, 3, 2, 1, 4).reshape(18, P, KD, 512)
    bias = np.concatenate([ab.reshape(18, 1, 1, 512), np.zeros((18, P - 1, 1, 512), np.float32)], 1)
    ada = np.concatenate([aw, bias], 2)

    c1, c2 = f["c"].reshape(KD, P).T, f["c_2"].reshape(KD, P).T
    cond = np.stack([c1, c1, c1, c2, c2], 1)
    i = np.arange(0, 256, 2, dtype=np.float32)
    inv = (1.0 / (np.float32(10000.0) ** (i / np.float32(256.0)))).astype(np.float32)
    col = lambda v: v.reshape(-1, P).T
    gains = np.concatenate([col(f["att_q_g"]), col(f["att_k_g"]), col(inv), col(f["pool_scale_2"]),
                            col(f["g_q_lat_2"]), col(f["g_kv_lat_2"]), np.zeros((P, 6), np.float32)], 1)

    lg = np.log(1.0 - 2.0 ** (-5.0 - np.arange(4)))
    j, q = np.arange(P)[:, None], np.arange(P)[None, :]
    far = np.stack([q - j + P * n for n in range(NT - 1, 0, -1)])
    near = np.abs(q - j)[None]
    power = np.exp(lg[:, None, None, None] * np.concatenate([far, near])[None])
    power[:, -1][:, (j // 64) > (q // 64)] = 0.0
    decay = (power / 16.0).transpose(0, 2, 1, 3).reshape(4, P, NT * P).astype(np.float32)

    rel = f["att_rel_bias"][0]
    diag = np.concatenate([np.repeat(rel[:, 256:257], 511, 1), rel[:, ::-1][:, :256]], 1)
    band = np.stack([diag[:, 127 - n:127 - n + BANDW] for n in range(P)], 1)

    edge = np.zeros((P, 4, 2, 8), np.float32)
    for n, window in enumerate(POOLS):
        for e, c in enumerate((0, S - 8)):
            tt = np.arange(c, c + 8)
            edge[:, n, e] = 1.0 / (np.clip(tt + window // 2, 0, S) - np.clip(tt - window // 2, 0, S))
    inv2 = (np.float32(10000.0) ** (-np.arange(0, LROPE, 2, dtype=np.float32) / np.float32(LROPE)))

    return {
        "w": w, "ada": ada, "cond": cond, "gains": gains, "x": f["x"][0], "pos": f["positions"][0],
        "norm_g": np.concatenate([f["norm_g"], f["norm_g_2"]]), "ret_gn": f["ret_gn_g"].reshape(4, 512),
        "pool_w": f["pool_w_2"][0].transpose(1, 0, 2), "edge": edge, "pos2": f["positions_2"].reshape(NT, P).T,
        "inv2": np.repeat(inv2[None], NT, 0), "g_qnorm": f["g_qnorm_2"][0], "g_knorm": f["g_knorm_2"][0],
        "decay": decay, "ident": np.eye(P, dtype=np.float32), "band": band,
    }


def kernel(**inputs):
    import concourse.bacc as bacc
    from concourse.bass_utils import run_bass_kernel_spmd

    nc = bacc.Bacc("TRN2", target_bir_lowering=False, num_devices=1)
    arrays = {f"in_{k}": np.ascontiguousarray(v) for k, v in lay_out(inputs).items()}
    t = {k[3:]: nc.dram_tensor(k, v.shape, mybir.dt.from_np(v.dtype), kind="ExternalInput").ap()
         for k, v in arrays.items()}
    t["out"] = nc.dram_tensor("out", (S, D), F32, kind="ExternalOutput").ap()
    t["res"] = nc.dram_tensor("res", (S, D), F32, kind="Internal").ap()
    t["mod"] = nc.dram_tensor("mod", (18, 512), F32, kind="Internal").ap()
    for name, shape in SCRATCH.items():
        t[name] = nc.dram_tensor(name, shape, F32, kind="Internal").ap()
    build_program(nc, t)
    result = run_bass_kernel_spmd(nc, [arrays], core_ids=[0])
    return np.asarray(result.results[0]["out"]).reshape(1, S, D)
```

```python
from contextlib import ExitStack
import math

import numpy as np

import concourse.bass as bass
from concourse import mybir

F32 = mybir.dt.float32
F32R = mybir.dt.float32r
I32 = mybir.dt.int32
ALU = mybir.AluOpType
ACT = mybir.ActivationFunctionType
AX = mybir.AxisListType

P = 128
D = 1024
S = 1024
NT = S // P
KD = D // P
EPS = 1e-6
NEG = -1e30

RING = 8
STAGE = 4
RET_GROUPS, RET_SLOTS = 4, 32
ATT_GROUPS, ATT_SLOTS = 4, 40
GH = 4
MIX_SLOTS = 56
ATT0 = RET_GROUPS * RET_SLOTS
MIX0 = ATT0 + ATT_GROUPS * ATT_SLOTS
SLOTS = MIX0 + MIX_SLOTS

ADA = KD + 1
PIECES = 6
LEFT = 4
BANDW = (LEFT + 1) * P
POOLS = (2, 4, 8, 16)
LH, LQK, LNOPE, LROPE, LV = 8, 96, 64, 32, 64
QLAT, KVLAT = 256, 128
LATW = QLAT + KVLAT + LROPE
HR = LROPE // 2
PAD = 8
PADW = S + 2 * PAD

FREE = 1

TWO_PI = 2.0 * math.pi
C1 = 6.28125
C2 = round((TWO_PI - C1) * 2**20) / 2**20
C3 = TWO_PI - C1 - C2
MAGIC = 1.5 * 2**23


def build_program(nc, t, stop_after=3):
    with ExitStack() as ctx:
        def sb(name, shape, dt=F32, where=None):
            return (where or ctx).enter_context(nc.sbuf_tensor(name, shape, dt))

        def sem(name):
            return ctx.enter_context(nc.semaphore(name))

        def overlay(region, size, *sets):
            for n, tensors in enumerate(sets):
                with ExitStack() as own:
                    total = 0
                    for m, tensor in enumerate(tensors):
                        if isinstance(tensor, (int, float)):
                            tensor = (f"{region}_gap{n}_{m}", [P, int(tensor * 256)], F32)
                        name, shape, dt = tensor
                        b[name] = sb(name, shape, dt, own)
                        total += 4 * int(np.prod(shape[1:]))
                    assert total <= size * 1024, (region, n, total)
            sb(region, [P, int(size * 256)])

        slots_run = (ATT0, MIX0, SLOTS, SLOTS)[stop_after]
        b = {}
        w_hi = sb("w_hi", [P, RING, 512], F32R)
        w_lo = sb("w_lo", [P, RING, 512], F32R)
        stage = sb("stage", [P, STAGE, 512])
        ident = sb("ident", [P, P])
        ones = sb("ones", [P, 2])
        eps = sb("eps", [P, 1])
        ccol = sb("ccol", [P, 5, KD])
        gate = sb("gate", [P, D])
        st = sb("st", [P, 192])
        gains = sb("gains", [P, 16])
        qk_rows = sb("qk_rows", [P, 2, LROPE])
        ps = ctx.enter_context(nc.psum_tensor("ps", [P, 8, 512], F32))
        psf = ps[:, :, :].rearrange("p b n -> p (b n)")

        overlay("region_h", 64,
                [("ada_a", [P, 3, ADA, 512], F32)],
                [("h_hi", [P, KD, S], F32R), ("h_lo", [P, KD, S], F32R)],
                [24, ("k_scratch", [P, 2, LH, HR], F32), 3, ("turned_q", [P, S], F32),
                 20, ("k_squares", [P, 2, S], F32), ("turned_k", [P, S], F32)])
        norm = [("x_in", [P, 3, D]), ("xn", [P, 2, D]), ("arow", [P, D]), ("srow", [P, D]), ("ngrow", [P, D])]
        overlay("region_w", 97,
                [(f"{n}0", shape, F32) for n, shape in norm]
                + [("ada_b", [P, 3, ADA, 512], F32), ("mod_row", [1, 512], F32)],
                [40] + [(f"{n}2", shape, F32) for n, shape in norm],
                [("r_q", [P, 2, S], F32), ("r_k", [P, 2, S], F32), ("r_g", [P, NT, 512], F32),
                 ("r_v", [P, NT, 512], F32), ("r_ohi", [P, 4, 512], F32R), ("r_olo", [P, 4, 512], F32R),
                 ("r_tmp", [P, 512], F32), ("r_decay", [P, NT * P], F32), ("r_s", [P, 2, S], F32),
                 ("r_gn", [P, 512], F32), ("r_x", [P, 4, 512], F32),
                 1, ("cos", [P, S], F32), ("sin", [P, S], F32)],
                [48, ("ada_c", [P, ADA, 512], F32), 14, ("acc", [P, 3, 512], F32)],
                [4, ("a_q", [P, GH, S], F32), 4, ("a_k", [P, GH, S], F32), ("a_v", [P, NT, 512], F32),
                 ("a_g", [P, GH, S], F32), ("a_bias", [P, 2, BANDW], F32), ("a_p", [P, 3, BANDW], F32),
                 ("a_pT", [P, 2, BANDW], F32), ("a_o", [P, 512], F32), 0.5, ("a_sq", [P, S], F32)],
                [("a_ohi", [P, GH, S], F32R), 4, ("a_olo", [P, GH, S], F32R), 41, ("a_x", [P, 4, 512], F32)],
                [("l_lat", [P, NT, LATW], F32), ("l_u", [P, 4, PADW], F32), ("l_gp", [P, 4, S], F32),
                 ("l_sum", [P, 2, PADW], F32), ("l_ga", [P, 2, 512], F32), ("l_y", [P, 2, 512], F32),
                 ("l_pw", [P, 4, P], F32), ("l_edge", [P, 4, 2, 8], F32), ("l_e8", [P, 2, 8], F32)],
                [("l_q", [P, NT, LH * LQK], F32), ("l_k", [P, NT, LH * LQK], F32),
                 ("l_v", [P, NT, LH * LV], F32), ("l_tmp", [P, 2, S], F32),
                 ("l_qlhi", [P, 2, S], F32R), ("l_qllo", [P, 2, S], F32R), ("l_klhi", [P, S], F32R),
                 ("l_kllo", [P, S], F32R), ("cos2", [P, NT, HR], F32), ("sin2", [P, NT, HR], F32)],
                [64, ("l_qT", [P, S], F32), ("l_kT", [P, S], F32), ("l_p", [P, 3, S], F32),
                 ("l_pT", [P, 2, S], F32), ("l_sg", [P, 512], F32), ("l_o", [P, 512], F32)],
                [64, ("l_x", [P, 4, 512], F32), ("l_t", [P, 512], F32)])

        ada_a, ada_b, mod_row, h_hi, h_lo = (b[n] for n in ("ada_a", "ada_b", "mod_row", "h_hi", "h_lo"))
        x_in, xn, arow, srow, ngrow = ([b[f"{n}{l}"] for l in (0, 0, 2)] for n, _ in norm)
        (r_q, r_k, r_v, r_g, r_ohi, r_olo, r_tmp, r_decay, r_s, r_gn, r_x, cos, sin, ada_c, acc) = (
            b[n] for n in ("r_q", "r_k", "r_v", "r_g", "r_ohi", "r_olo", "r_tmp", "r_decay", "r_s",
                           "r_gn", "r_x", "cos", "sin", "ada_c", "acc"))
        (a_q, a_k, a_v, a_g, a_bias, a_p, a_pT, a_o, a_ohi, a_olo, a_x, a_sq) = (
            b[n] for n in ("a_q", "a_k", "a_v", "a_g", "a_bias", "a_p", "a_pT", "a_o",
                           "a_ohi", "a_olo", "a_x", "a_sq"))

        (l_lat, l_u, l_gp, l_sum, l_ga, l_y, l_pw, l_edge, l_e8, l_q, l_k, l_v, l_tmp, l_qlhi, l_qllo,
         l_klhi, l_kllo, cos2, sin2, l_qT, l_kT, l_p, l_pT, l_sg, l_o, l_x, l_t) = (
            b[n] for n in ("l_lat", "l_u", "l_gp", "l_sum", "l_ga", "l_y", "l_pw", "l_edge", "l_e8", "l_q",
                           "l_k", "l_v", "l_tmp", "l_qlhi", "l_qllo", "l_klhi", "l_kllo", "cos2", "sin2",
                           "l_qT", "l_kT", "l_p", "l_pT", "l_sg", "l_o", "l_x", "l_t"))

        w_landed = [sem(f"w_landed{n}") for n in range(STAGE)]
        w_rounded = sem("w_rounded")
        w_split = sem("w_split")
        w_used = sem("w_used")
        const_in = sem("const_in")
        ada_in = [sem(f"ada_in{n}") for n in range(PIECES)]
        c_ready = sem("c_ready")
        dve_init = sem("dve_init")
        mod_done = sem("mod_done")
        mod_copied = sem("mod_copied")
        mod_stored = sem("mod_stored")
        pos_in = sem("pos_in")
        res_copied = sem("res_copied")
        rope_chain = sem("rope_chain")
        rope_reduced = sem("rope_reduced")
        rope_tables = sem("rope_tables")
        n_rows = sem("n_rows")
        n_arow = sem("n_arow")
        n_x = [sem(f"n_x{n}") for n in range(3)]
        n_gate = sem("n_gate")
        n_sq = sem("n_sq")
        n_root = sem("n_root")
        n_rr = sem("n_rr")
        n_mul = sem("n_mul")
        n_xn = sem("n_xn")
        n_turned = sem("n_turned")
        n_hi = sem("n_hi")
        n_lo = sem("n_lo")
        dve_r = sem("dve_r")

        bank_done = {l: sem(f"bank_done{l}") for l in "ram"}
        bank_free = {l: sem(f"bank_free{l}") for l in "ram"}
        out_done = {l: sem(f"out_done{l}") for l in "ram"}
        out_free = {l: sem(f"out_free{l}") for l in "ram"}
        out_ready = {l: sem(f"out_ready{l}") for l in "ram"}
        res_in = {l: [sem(f"res_in{l}{n}") for n in range(4)] for l in "ram"}
        res_out = {l: [sem(f"res_out{l}{n}") for n in range(4)] for l in "ram"}

        r_rope = sem("r_rope")
        r_gready = sem("r_gready")
        r_consts = sem("r_consts")
        m_in = sem("m_in")
        m_acc = sem("m_acc")
        m_red = sem("m_red")
        m_row = sem("m_row")
        m_st = sem("m_st")
        r_sdone = sem("r_sdone")
        r_sready = sem("r_sready")
        r_odone = sem("r_odone")
        r_sq = sem("r_sq")
        r_root = sem("r_root")
        r_rinv = sem("r_rinv")
        r_gated = sem("r_gated")
        r_turned = sem("r_turned")
        r_hi = sem("r_hi")
        r_lo = sem("r_lo")

        a_sums = sem("a_sums")
        a_roots = sem("a_roots")
        a_normed = sem("a_normed")
        a_rchain = sem("a_rchain")
        a_biasin = [sem(f"a_biasin{n}") for n in range(2)]
        a_biasok = sem("a_biasok")
        a_sdone = sem("a_sdone")
        a_max = sem("a_max")
        a_neg = sem("a_neg")
        a_exp = sem("a_exp")
        a_rinv = sem("a_rinv")
        a_prob = sem("a_prob")
        a_pdone = sem("a_pdone")
        a_pevac = sem("a_pevac")
        a_odone = sem("a_odone")
        a_gated = sem("a_gated")
        a_hi = sem("a_hi")
        a_lo = sem("a_lo")
        dve_a = sem("dve_a")

        l_consts = sem("l_consts")
        l_chain = sem("l_chain")
        l_angles = sem("l_angles")
        l_tables = sem("l_tables")
        l_pads = sem("l_pads")
        l_sums = sem("l_sums")
        l_roots = sem("l_roots")
        l_latok = sem("l_latok")
        l_gastored = [sem(f"l_gastored{n}") for n in range(2)]
        l_diff = sem("l_diff")
        l_ydone = sem("l_ydone")
        l_yready = sem("l_yready")
        l_yhi = sem("l_yhi")
        l_ylo = sem("l_ylo")
        l_lturned = sem("l_lturned")
        l_lhi = sem("l_lhi")
        l_llo = sem("l_llo")
        l_rcopied = sem("l_rcopied")
        l_updone = sem("l_updone")
        l_upfree = sem("l_upfree")
        l_sq = sem("l_sq")
        l_rr = sem("l_rr")
        l_qdone = sem("l_qdone")
        l_kdone = sem("l_kdone")
        l_kchain = sem("l_kchain")
        l_sdone = sem("l_sdone")
        l_max = sem("l_max")
        l_neg = sem("l_neg")
        l_exp = sem("l_exp")
        l_rinv = sem("l_rinv")
        l_prob = sem("l_prob")
        l_pdone = sem("l_pdone")
        l_pevac = sem("l_pevac")
        l_odone = sem("l_odone")
        l_sgin = sem("l_sgin")
        l_gated = sem("l_gated")
        l_hi = sem("l_hi")
        l_lo = sem("l_lo")

        def unit_of(l, u):
            return (4 * (u // 8) + u % 4, (u // 4) % 2) if l == "r" else (u % 8, u // 8)

        qk_tables = b["turned_k"][:, :].rearrange("p (s e c m n) -> p s e c m n", s=2, e=2, c=2, m=NT)
        k_squares = [b["k_squares"][:, n, 0:LH * LQK] for n in range(2)]
        k_scratch = b["k_scratch"]

        qk_stats = st[:, 0:2 * NT * LH].rearrange("p (s m h) -> p s m h", s=2, m=NT)

        def l_turned(h, k):
            if h == LH - 1:
                return (l_k if k else l_q)[:, :, 0:P]
            flat = (l_kT if k else l_qT)[:, :] if h % 2 == 0 else b["turned_k" if k else "turned_q"][:, :]
            return flat.rearrange("p (m n) -> p m n", m=NT)

        def rope_parts(src, m):
            x = src[:, m].rearrange("p (h n) -> p h n", h=LH)
            return x[:, :, LNOPE:LNOPE + HR], x[:, :, LNOPE + HR:]

        def head_unit(h, k):
            return k if h == 0 else (NT + 2) * (h - 1) + 2 + (6 if k else 3)

        def prob_unit(e, heads=GH):
            h, i = divmod(e, NT)
            return (NT + 2) * h + 2 + i + ((i > 2) + (i > 4) if h + 1 < heads else 0)

        block = ctx.enter_context(nc.Block())

        @block.sync
        def _(sp):
            for n in range(PIECES):
                buf = ada_a[:, n] if n < 3 else ada_b[:, n - 3]
                sp.dma_start(buf, t["ada"][n]).then_inc(ada_in[n], 16)
            for n in range(STAGE):
                sp.dma_start(stage[:, n], t["w"][n]).then_inc(w_landed[n], 16)
            with sp.Fori(1, slots_run // STAGE) as i:
                for n in range(STAGE):
                    sp.wait_ge(w_split, i * STAGE + (n + 1 - STAGE))
                    sp.dma_start(stage[:, n], t["w"][bass.ds(i * STAGE + n, 1)].rearrange(
                        "a p n -> (a p) n")).then_inc(w_landed[n], 16)

        @block.gpsimd
        def _(pool):
            pool.wait_ge(dve_init, 2)
            def stream(first, count):
                with pool.Fori(first // RING, (first + count) // RING) as i:
                    for n in range(RING):
                        pool.wait_ge(w_landed[n % STAGE], i * (16 * RING // STAGE) + 16 * (n // STAGE + 1))
                        pool.wait_ge(w_used, i * RING + n + 1)
                        pool.tensor_tensor(w_hi[:, n], stage[:, n % STAGE],
                                           ones[:, 0:1].to_broadcast([P, 512]), ALU.mult).then_inc(w_rounded, 1)
                        pool.wait_ge(w_rounded, i * RING + n + 1)
                        pool.tensor_tensor(w_lo[:, n], stage[:, n % STAGE], w_hi[:, n].bitcast(F32),
                                           ALU.subtract).then_inc(w_split, 1)

            if stop_after < 2:
                return stream(0, slots_run)
            before_out = MIX0 + 5 * RING
            stream(0, before_out)
            for m in range(NT):
                def chained(ins, n):
                    ins.then_inc(l_kchain, 1)
                    pool.wait_ge(l_kchain, 4 * m + n)

                pool.wait_ge(l_rr, m + 1)
                x = l_k[:, m].rearrange("p (h n) -> p h n", h=LH)
                chained(pool.tensor_tensor(x, x, st[:, 64 + m * LH:64 + (m + 1) * LH].unsqueeze(2)
                                           .to_broadcast([P, LH, LQK]), ALU.mult), 1)
                x1, x2 = rope_parts(l_k, m)
                (cos1, sin1), (cos2_, sin2_) = (
                    [qk_tables[:, 1, e, c, m].unsqueeze(1).to_broadcast([P, LH, HR]) for c in range(2)]
                    for e in range(2))
                pool.tensor_tensor(k_scratch[:, 0], x1, sin1, ALU.mult)
                chained(pool.tensor_tensor(k_scratch[:, 1], x2, sin2_, ALU.mult), 2)
                pool.tensor_tensor(x1, x1, cos1, ALU.mult)
                chained(pool.tensor_tensor(x2, x2, cos2_, ALU.mult), 3)
                pool.tensor_tensor(x1, x1, k_scratch[:, 1], ALU.subtract)
                chained(pool.tensor_tensor(x2, x2, k_scratch[:, 0], ALU.add), 4)
            pool.sem_inc(l_kdone, 1)
            stream(before_out, SLOTS - before_out)

        @block.tensor
        def _(pe):
            def product(out, a_hi_, a_lo_, b_hi_, b_lo_, first, last):
                pe.matmul(out, a_hi_, b_hi_, start=first, stop=False)
                pe.matmul(out, a_hi_, b_lo_, start=False, stop=False)
                return pe.matmul(out, a_lo_, b_hi_, start=False, stop=last)

            def token_tile(m, slot0, l, wait_bank):
                wait_bank(m)
                for k in range(KD):
                    if m == 0:
                        pe.wait_ge(w_split, slot0 + (k + 1))
                    mm = product(ps[:, m % 4], h_hi[:, k, m * P:(m + 1) * P],
                                 h_lo[:, k, m * P:(m + 1) * P], w_hi[:, k], w_lo[:, k],
                                 k == 0, k == KD - 1)
                    if m == NT - 1:
                        mm.then_inc(w_used, 1)
                    elif k == KD - 1:
                        mm.then_inc(bank_done[l], 1)

            def tokens(slot0, l, wait_bank):
                for k in range(KD):
                    pe.wait_ge(w_split, slot0 + (k + 1))
                    for m in range(NT):
                        if k == 0:
                            wait_bank(m)
                        mm = product(ps[:, m], h_hi[:, k, m * P:(m + 1) * P],
                                     h_lo[:, k, m * P:(m + 1) * P], w_hi[:, k], w_lo[:, k],
                                     k == 0, k == KD - 1)
                        if m == NT - 1:
                            mm.then_inc(w_used, 1)
                        elif k == KD - 1:
                            mm.then_inc(bank_done[l], 1)

            def features(slot0, l, wait_bank):
                for k in range(KD):
                    pe.wait_ge(w_split, slot0 + (k + 1))
                    for m in range(4):
                        for a in range(2):
                            if k == 0:
                                wait_bank(2 * m + a)
                            mm = product(ps[:, 2 * m + a], w_hi[:, k, m * P:(m + 1) * P],
                                         w_lo[:, k, m * P:(m + 1) * P], h_hi[:, k, a * 512:(a + 1) * 512],
                                         h_lo[:, k, a * 512:(a + 1) * 512], k == 0, k == KD - 1)
                            if 2 * m + a == 7:
                                mm.then_inc(w_used, 1)
                            elif k == KD - 1:
                                mm.then_inc(bank_done[l], 1)

            def out_unit(l, u, o_hi, o_lo, tok, wait_free):
                wait_free(u)
                first_half = 4 * unit_of(l, u)[1]
                for k in range(4):
                    mm = product(ps[:, u % 4], o_hi[:, k, tok], o_lo[:, k, tok], w_hi[:, first_half + k],
                                 w_lo[:, first_half + k], k == 0, k == 3)
                    if k == 0 and u == (12 if l == "r" else 8):
                        mm.then_inc(w_used, 4)
                mm.then_inc(w_used, 4) if u == 15 else mm.then_inc(out_done[l], 1)

            def turn_norm(l, m):
                pe.wait_ge(n_xn, l * NT + m + 1)
                if l or m >= 2:
                    pe.wait_ge(n_lo, l * NT + m - 1)
                for k in range(KD):
                    tr = pe.transpose(psf[:, (4 + 2 * (m % 2)) * 512 + k * P:][:, 0:P],
                                      xn[l][:, m % 2, k * P:(k + 1) * P], ident[:, :])
                tr.then_inc(n_turned, 1)

            def norm_and_first(l, slot0, loop):
                turn_norm(l, 0)
                for m in range(NT):
                    if m + 1 < NT:
                        turn_norm(l, m + 1)
                    pe.wait_ge(n_lo, l * NT + m + 1)
                    token_tile(m, slot0, loop, lambda m: m >= 4 and pe.wait_ge(bank_free[loop], m - 3))

            pe.sem_inc(w_used, RING)
            for credited in (out_free["r"], out_free["a"], out_ready["r"], out_ready["a"], r_lo, r_sq, a_max,
                             a_lo, *res_out["r"], *res_out["a"]):
                pe.sem_inc(credited, FREE)
            pe.wait_ge(c_ready, 1)
            pe.wait_ge(dve_init, 2)
            for n in range(PIECES):
                pe.wait_ge(ada_in[n], 16)
                buf = ada_a[:, n] if n < 3 else ada_b[:, n - 3]
                for k in range(KD):
                    pe.matmul(ps[0:1, n], ccol[:, 0, k:k + 1], buf[:, k], start=(k == 0), stop=False)
                pe.matmul(ps[0:1, n], ones[:, 0:1], buf[:, KD], start=False, stop=True).then_inc(mod_done, 1)
            pe.wait_ge(const_in, 16 * 3)
            norm_and_first(0, 0, "r")

            def retention(h, last):
                w0, f0 = h * RET_SLOTS, h * (3 * NT)
                features(w0 + 8, "r", lambda n: pe.wait_ge(bank_free["r"], f0 + (n % 4 + 5)))
                tokens(w0 + 16, "r", lambda n: pe.wait_ge(bank_free["r"], f0 + (n + 9)))
                pe.wait_ge(bank_free["r"], f0 + 24)
                pe.wait_ge(r_rope, h + 1)

                def scores(i):
                    if i >= 2:
                        pe.wait_ge(r_sready, h * NT + (i - 1))
                    if i == 4:
                        pe.wait_ge(out_free["r"], h * 16 + 8 + FREE)
                    for j in range(i + 1):
                        for k in range(2):
                            mm = pe.matmul(psf[:, (i % 2) * 1024 + j * P:][:, 0:P], r_k[:, k, j * P:(j + 1) * P],
                                           r_q[:, k, i * P:(i + 1) * P], start=(k == 0), stop=(k == 1))
                    mm.then_inc(r_sdone, 1)

                def values(i):
                    pe.wait_ge(r_sready, h * NT + (i + 1))
                    if i >= 2:
                        pe.wait_ge(r_gated, h * NT + (i - 1))
                    for j in range(i + 1):
                        mm = pe.matmul(ps[:, 4 + i % 2], r_s[:, i % 2, j * P:(j + 1) * P], r_v[:, j],
                                       start=(j == 0), stop=(j == i))
                    mm.then_inc(r_odone, 1)

                def turn(i):
                    pe.wait_ge(r_gated, h * NT + (i + 1))
                    if i:
                        pe.wait_ge(r_lo, h * NT + i + FREE)
                    for e in range(4):
                        tr = pe.transpose(ps[:, 6, e * P:(e + 1) * P], r_g[:, i, e * P:(e + 1) * P], ident[:, :])
                    tr.then_inc(r_turned, 1)

                for a in range(2):
                    scores(4 * a)
                    if a == 0:
                        scores(1)
                        pe.wait_ge(m_acc, h * 3 + 3)
                        for n in range(3):
                            pe.matmul(ps[0:1, 5 + n], ones[:, 0:1], acc[:, n], start=True,
                                      stop=True).then_inc(m_red, 1)
                        pe.wait_ge(m_row, h * 3 + 3)
                    for i in range(4 * a, 4 * a + 4):
                        if i % 4 < 3 and i > 0:
                            scores(i + 1)
                        values(i)
                        if i % 4:
                            turn(i - 1)
                    turn(4 * a + 3)
                    pe.wait_ge(r_lo, h * NT + (4 * a + 4) + FREE)
                    if a == 0:
                        pe.wait_ge(w_split, w0 + RET_SLOTS)
                    for u in range(8 * a, 8 * a + 8):
                        m = unit_of("r", u)[0] % 4
                        out_unit("r", u, r_ohi, r_olo, slice(m * P, (m + 1) * P),
                                 lambda u: u % 8 >= 4 and pe.wait_ge(out_free["r"], h * 16 + (u - 3) + FREE))
                if not last:
                    pe.wait_ge(out_free["r"], h * 16 + 16 + FREE)
                    for m in range(NT):
                        token_tile(m, w0 + RET_SLOTS, "r",
                                   lambda m: m >= 4 and pe.wait_ge(bank_free["r"], f0 + (3 * NT + m - 3)))

            with pe.Fori(0, RET_GROUPS - 1) as h:
                retention(h, False)
            retention(RET_GROUPS - 1, True)
            if stop_after < 1:
                return
            pe.wait_ge(out_free["r"], RET_GROUPS * 16 + FREE)
            norm_and_first(1, ATT0, "a")

            def attention(g, last):
                w0, f0 = g * ATT_SLOTS + ATT0, g * (4 * NT)
                tokens(w0 + 8, "a", lambda n: pe.wait_ge(bank_free["a"], f0 + (n % 4 + 5)))
                tokens(w0 + 16, "a", lambda n: pe.wait_ge(bank_free["a"], f0 + (n + 9)))
                features(w0 + 24, "a", lambda n: pe.wait_ge(bank_free["a"], f0 + (n + 17)))
                pe.wait_ge(bank_free["a"], f0 + 32)
                pe.wait_ge(a_normed, g * 2 + 2)

                e0, t0 = g * (GH * NT), g * (GH * (NT + 2))

                def turn_head(h, k):
                    n = head_unit(h, k)
                    if n > 1:
                        pe.wait_ge(a_pevac, t0 + n)
                    for m in range(NT):
                        tr = pe.transpose(psf[:, (6 if n == 1 else 4) * 512 + m * P:][:, 0:P],
                                          (a_k if k else a_q)[:, h, m * P:(m + 1) * P], ident[:, :])
                    tr.then_inc(a_pdone, 1)

                def scores(e):
                    h, i = divmod(e, NT)
                    if i == 0:
                        pe.wait_ge(a_pevac, t0 + (head_unit(h, 1) + 1))
                    if e >= 2:
                        pe.wait_ge(a_max, e0 + (e - 1) + FREE)
                    lo = max(0, i - LEFT) * P
                    width = (i + 1) * P - lo
                    base = (e % 2) * 1024
                    for c in range(0, width, 512):
                        w = min(512, width - c)
                        mm = pe.matmul(psf[:, base + c:base + c + w], a_q[:, h, i * P:(i + 1) * P],
                                       a_k[:, h, lo + c:lo + c + w], start=True, stop=True)
                    mm.then_inc(a_sdone, 1)

                def turn(e):
                    pe.wait_ge(a_prob, e0 + (e + 1))
                    pe.wait_ge(a_pevac, t0 + prob_unit(e))
                    for n in range(min(e % NT, LEFT) + 1):
                        tr = pe.transpose(psf[:, 4 * 512 + n * P:][:, 0:P],
                                          a_p[:, e % 3, n * P:(n + 1) * P], ident[:, :])
                    tr.then_inc(a_pdone, 1)

                def values(e):
                    h, i = divmod(e, NT)
                    pe.wait_ge(a_pevac, t0 + (prob_unit(e) + 1))
                    if h and i % 4 == 0:
                        pe.wait_ge(a_gated, g * (2 * GH) + (2 * h - 1 + i // 4))
                    n = min(i, LEFT) + 1
                    for c in range(n):
                        j = i + 1 - n + c
                        mm = pe.matmul(ps[:, 6 + i // 4, (i % 4) * P:(i % 4 + 1) * P],
                                       a_v[:, j, h * P:(h + 1) * P], a_pT[:, e % 2, c * P:(c + 1) * P],
                                       start=(c == 0), stop=(c == n - 1))
                    mm.then_inc(a_odone, 1)

                turn_head(0, 0)
                turn_head(0, 1)
                scores(0)
                scores(1)
                for e in range(GH * NT):
                    h, i = divmod(e, NT)
                    if e + 2 < GH * NT:
                        scores(e + 2)
                    turn(e)
                    if e:
                        values(e - 1)
                    if h + 1 < GH and i in (2, 4):
                        turn_head(h + 1, i == 4)
                values(GH * NT - 1)
                pe.wait_ge(a_lo, g * (2 * GH) + 2 * GH + FREE)
                pe.wait_ge(w_split, w0 + ATT_SLOTS)
                for u in range(16):
                    m = unit_of("a", u)[0]
                    out_unit("a", u, a_ohi, a_olo, slice(m * P, (m + 1) * P),
                             lambda u: u >= 4 and pe.wait_ge(out_free["a"], g * 16 + (u - 3) + FREE))
                if not last:
                    pe.wait_ge(out_free["a"], g * 16 + 16 + FREE)
                    for m in range(NT):
                        token_tile(m, w0 + ATT_SLOTS, "a",
                                   lambda m: m >= 4 and pe.wait_ge(bank_free["a"], f0 + (4 * NT + m - 3)))

            with pe.Fori(0, ATT_GROUPS - 1) as g:
                attention(g, False)
            attention(ATT_GROUPS - 1, True)
            if stop_after < 2:
                return
            pe.wait_ge(out_free["a"], ATT_GROUPS * 16 + FREE)

            norm_and_first(2, MIX0, "m")
            features(MIX0 + 8, "m", lambda n: pe.wait_ge(bank_free["m"], n % 4 + 5))
            features(MIX0 + 16, "m", lambda n: pe.wait_ge(bank_free["m"], n + 9))
            features(MIX0 + 24, "m", lambda n: pe.wait_ge(bank_free["m"], n + 17))
            pe.wait_ge(bank_free["m"], 32)
            pe.wait_ge(l_consts, 16 * 6)
            for n in range(4):
                pe.wait_ge(l_diff, n + 1)
                for a in range(2):
                    pe.matmul(ps[:, 2 * n + a], l_pw[:, n], l_u[:, n, PAD + 512 * a:PAD + 512 * a + 512],
                              start=True, stop=True).then_inc(l_ydone, 1)
            pe.wait_ge(l_latok, 2)
            for n in range(3):
                pe.wait_ge(l_ylo, 2 * n + 2)
                for m in range(NT):
                    tr = pe.transpose(psf[:, n * 1024 + m * P:][:, 0:P], l_lat[:, m, n * P:(n + 1) * P],
                                      ident[:, :])
                tr.then_inc(l_lturned, 1)
            pe.wait_ge(l_llo, 3)
            pe.wait_ge(l_ylo, 8)
            pe.wait_ge(w_split, MIX0 + 40)
            for m in range(NT):
                if m >= 2:
                    pe.wait_ge(l_upfree, m - 1)
                bank, tok = 4 * (m % 2), slice(m * P, (m + 1) * P)
                for c in range(2):
                    for k in range(2):
                        product(ps[:, bank + c, 0:384], l_qlhi[:, k, tok], l_qllo[:, k, tok],
                                w_hi[:, 2 * c + k, 0:384], w_lo[:, 2 * c + k, 0:384], k == 0, k == 1)
                for c in range(2):
                    mm = product(ps[:, bank + 2 + c], l_klhi[:, tok], l_kllo[:, tok], w_hi[:, 4 + c],
                                 w_lo[:, 4 + c], True, True)
                mm.then_inc(w_used, 8) if m == NT - 1 else mm.then_inc(l_updone, 1)
            pe.wait_ge(l_upfree, NT)
            pe.wait_ge(l_qdone, NT)
            pe.wait_ge(l_kdone, 1)

            def l_turn_head(h, k):
                n = head_unit(h, k)
                if n > 1:
                    pe.wait_ge(l_pevac, n)
                for m in range(NT):
                    tr = pe.transpose(psf[0:LQK, (6 if n == 1 else 4) * 512 + m * P:][:, 0:P],
                                      (l_k if k else l_q)[:, m, h * LQK:(h + 1) * LQK], ident[:, :])
                tr.then_inc(l_pdone, 1)

            def l_scores(e):
                h, i = divmod(e, NT)
                if i == 0:
                    pe.wait_ge(l_pevac, head_unit(h, 1) + 1)
                if e >= 2:
                    pe.wait_ge(l_exp, e - 1)
                q, k = l_turned(h, 0), l_turned(h, 1)
                for c in range(2):
                    mm = pe.matmul(ps[:, 2 * (e % 2) + c].rearrange("p (m n) -> p m n", m=4), q[0:LQK, i],
                                   k[0:LQK, 4 * c:4 * c + 4], start=True, stop=True)
                mm.then_inc(l_sdone, 1)

            def l_turn(e):
                pe.wait_ge(l_prob, e + 1)
                pe.wait_ge(l_pevac, prob_unit(e, LH))
                for n in range(NT):
                    tr = pe.transpose(psf[:, 4 * 512 + n * P:][:, 0:P], l_p[:, e % 3, n * P:(n + 1) * P],
                                      ident[:, :])
                tr.then_inc(l_pdone, 1)

            def l_values(e):
                h, i = divmod(e, NT)
                rows = slice(LV * (h % 2), LV * (h % 2) + LV)
                pe.wait_ge(l_pevac, prob_unit(e, LH) + 1)
                if h and i % 4 == 0:
                    pe.wait_ge(l_gated, 2 * h - 1 + i // 4)
                for n in range(NT):
                    mm = pe.matmul(ps[rows, 6 + i // 4, (i % 4) * P:(i % 4 + 1) * P],
                                   l_v[:, n, h * LV:(h + 1) * LV], l_pT[:, e % 2, n * P:(n + 1) * P],
                                   start=(n == 0), stop=(n == NT - 1))
                mm.then_inc(l_odone, 1)

            l_turn_head(0, 0)
            l_turn_head(0, 1)
            l_scores(0)
            l_scores(1)
            for e in range(LH * NT):
                h, i = divmod(e, NT)
                if e + 2 < LH * NT:
                    l_scores(e + 2)
                l_turn(e)
                if e:
                    l_values(e - 1)
                if h + 1 < LH and i in (2, 4):
                    l_turn_head(h + 1, int(i == 4))
            l_values(LH * NT - 1)
            pe.wait_ge(l_lo, 2 * LH)
            for a in range(2):
                for m in range(NT):
                    u = 8 * a + m
                    if u >= 4:
                        pe.wait_ge(out_free["m"], u - 3)
                    for k in range(KD):
                        if m == 0:
                            pe.wait_ge(w_split, MIX0 + 40 + 8 * a + k + 1)
                        mm = product(ps[:, u % 4], h_hi[:, k, m * P:(m + 1) * P], h_lo[:, k, m * P:(m + 1) * P],
                                     w_hi[:, k], w_lo[:, k], k == 0, k == KD - 1)
                        if m == NT - 1:
                            mm.then_inc(w_used, 1)
                        elif k == KD - 1:
                            mm.then_inc(out_done["m"], 1)

        @block.scalar
        def _(act):
            def wait_bank(l, slots0, done0, blk, n):
                if n < 7:
                    act.wait_ge(bank_done[l], done0 + (7 * blk + n + 1))
                else:
                    act.wait_ge(w_used, slots0 + (RING + 8 * blk + 8))

            def norm_load(l, m):
                src = t["x"] if l == 0 else t["res"]
                act.dma_start(x_in[l][:, m % 3], src[m * P:(m + 1) * P, :]).then_inc(n_x[m % 3], 16)

            def norm_rows(l):
                act.dma_start(arow[l][:, :], t["mod"][6 * l + 2:6 * l + 4, :].rearrange("a n -> (a n)")
                              .partition_broadcast(P)).then_inc(n_rows, 16)
                act.dma_start(ngrow[l][:, :], t["norm_g"][l].partition_broadcast(P)).then_inc(n_rows, 16)
                act.dma_start(srow[l][:, :], t["mod"][6 * l:6 * l + 2, :].rearrange("a n -> (a n)")
                              .partition_broadcast(P)).then_inc(n_rows, 16)

            def norm_stats(l, m):
                e = l * NT + m
                act.wait_ge(n_x[m % 3], 16 * (l * (3, 3, 2)[m % 3] + m // 3 + 1))
                if e >= 2:
                    act.wait_ge(n_turned, e - 1)
                act.activation(xn[l][:, m % 2], x_in[l][:, m % 3], ACT.Square,
                               accum_out=st[:, m:m + 1]).then_inc(n_sq, 1)
                act.wait_ge(n_sq, e + 1)
                act.activation(st[:, 8 + m:9 + m], st[:, m:m + 1], ACT.Sqrt, scale=1.0 / D,
                               bias=eps[:, 0:1]).then_inc(n_root, 1)

            def norm_layer(l, done, first_copy):
                act.dma_start(gate[:, :], t["mod"][6 * l + 4:6 * l + 6, :].rearrange("a n -> (a n)")
                              .partition_broadcast(P)).then_inc(n_gate, 16)
                for m in range(NT + 2):
                    if done <= m < NT:
                        norm_stats(l, m)
                    if 1 <= m <= NT:
                        e = l * NT + m - 1
                        act.wait_ge(n_turned, e + 1)
                        act.activation(h_hi[:, :, (m - 1) * P:m * P],
                                       psf[:, (4 + 2 * ((m - 1) % 2)) * 512:][:, 0:D].rearrange(
                                           "p (k n) -> p k n", k=KD), ACT.Copy).then_inc(n_hi, 1)
                        if m + 2 < NT:
                            act.wait_ge(n_mul, e + 1)
                            norm_load(l, m + 2)
                    if m >= 2:
                        first_copy(m - 2)

            act.dma_start(ident[:, :], t["ident"]).then_inc(const_in, 16)
            act.dma_start(ccol[:, :, :], t["cond"]).then_inc(const_in, 16)
            act.dma_start(gains[:, :], t["gains"]).then_inc(const_in, 16)
            act.dma_start(cos[:, :].bitcast(I32), t["pos"].partition_broadcast(P)).then_inc(pos_in, 16)
            act.dma_start(t["res"], t["x"]).then_inc(res_copied, 16)
            act.wait_ge(const_in, 48)
            act.activation(ccol[:, :, :], ccol[:, :, :], ACT.Silu).then_inc(c_ready, 1)
            act.wait_ge(rope_reduced, 1)
            act.activation(sin[:, :], sin[:, :], ACT.Sin).then_inc(rope_tables, 1)
            act.wait_ge(rope_reduced, 2)
            act.activation(cos[:, :], cos[:, :], ACT.Sin).then_inc(rope_tables, 1)
            for n in range(PIECES):
                act.wait_ge(mod_copied, n + 1)
                act.dma_start(t["mod"][n:n + 1, :], mod_row[:, :]).then_inc(mod_stored, 16)

            def unit_rows(l, u):
                m, half = unit_of(l, u)
                return t["res"][m * P:(m + 1) * P, half * 512:(half + 1) * 512]

            def residual_load(l, u):
                buf = r_x if l == "r" else a_x
                act.dma_start(buf[:, u % 4], unit_rows(l, u)).then_inc(res_in[l][u % 4], 16)

            def residual_units(l, i, units, meanwhile=None):
                buf = r_x if l == "r" else a_x
                units = list(units)
                for u in units:
                    act.wait_ge(out_ready[l], i * 16 + (u + 1) + FREE)
                    act.dma_start(unit_rows(l, u), buf[:, u % 4]).then_inc(res_out[l][u % 4], 16)
                    if u + 3 in units and u + 3 >= units[0] + 4:
                        v = u + 3
                        act.wait_ge(res_out[l][v % 4], i * 64 + 16 * (v // 4) + FREE)
                        residual_load(l, v)
                    if meanwhile:
                        meanwhile(u)

            def first_loads(l, i, units):
                for v in list(units)[0:4]:
                    act.wait_ge(res_out[l][v % 4], i * 64 + 16 * (v // 4) + FREE)
                    residual_load(l, v)

            def ada_load(n):
                act.dma_start(ada_c[:, :, :], t["ada"][bass.ds(n + PIECES, 1)].rearrange(
                    "a p k n -> (a p) k n")).then_inc(m_in, 16)

            def retention_loads(h):
                act.wait_ge(w_used, h * RET_SLOTS + RING)
                act.wait_ge(r_lo, h * NT + FREE)
                act.wait_ge(out_ready["r"], h * 16 + FREE)
                act.dma_start(r_gn[:, :], t["ret_gn"][bass.ds(h, 1)].rearrange("a n -> (a n)")
                              .partition_broadcast(P)).then_inc(r_consts, 16)
                act.dma_start(r_decay[:, :], t["decay"][bass.ds(h, 1)].rearrange("a p n -> (a p) n"))\
                    .then_inc(r_consts, 16)
                ada_load(h * 3)

            def retention_values(h, m):
                wait_bank("r", h * RET_SLOTS, h * 21, 0, m)
                act.activation(r_v[:, m], ps[:, m % 4], ACT.Copy).then_inc(bank_free["r"], 1)

            def retention(h, last):
                w0, d0 = h * RET_SLOTS, h * 21
                act.wait_ge(m_acc, h * 3 + 1)
                ada_load(h * 3 + 1)
                for n in range(8):
                    wait_bank("r", w0, d0, 1, n)
                    dst = (r_q if n < 4 else r_k)[:, (n // 2) % 2, (n % 2) * 512:(n % 2 + 1) * 512]
                    act.activation(dst, ps[:, n], ACT.Copy).then_inc(bank_free["r"], 1)
                act.wait_ge(m_acc, h * 3 + 2)
                ada_load(h * 3 + 2)
                for m in range(NT):
                    wait_bank("r", w0, d0, 2, m)
                    act.activation(r_g[:, m], ps[:, m], ACT.Silu).then_inc(bank_free["r"], 1)

                def squares(i):
                    act.wait_ge(r_odone, h * NT + (i + 1))
                    act.wait_ge(r_sq, h * NT + i + FREE)
                    act.activation(r_tmp[:, :], ps[:, 4 + i % 2], ACT.Square,
                                   accum_out=st[:, 16 + i:17 + i]).then_inc(r_sq, 1)
                    act.wait_ge(r_sq, h * NT + (i + 1) + FREE)
                    act.activation(st[:, 24 + i:25 + i], st[:, 16 + i:17 + i], ACT.Sqrt, scale=1.0 / 512,
                                   bias=eps[:, 0:1]).then_inc(r_root, 1)

                def high(i):
                    act.wait_ge(r_turned, h * NT + (i + 1))
                    act.activation(r_ohi[:, :, (i % 4) * P:(i % 4 + 1) * P],
                                   ps[:, 6].rearrange("p (e n) -> p e n", e=4), ACT.Copy).then_inc(r_hi, 1)

                for n in range(3):
                    act.wait_ge(m_row, h * 3 + (n + 1))
                    act.dma_start(t["mod"][bass.ds(h * 3 + (n + PIECES), 1)], acc[0:1, n]).then_inc(m_st, 16)
                for a in range(2):
                    for i in range(4 * a, 4 * a + 4):
                        squares(i)
                        if i % 4:
                            high(i - 1)
                        if i % 4 == 2:
                            if a == 0:
                                act.wait_ge(m_st, h * 48 + 48)
                            first_loads("r", h, range(8 * a, 8 * a + 8))
                    high(4 * a + 3)
                    if a and last:
                        norm_rows(1)
                        for m in range(3):
                            norm_load(1, m)
                        residual_units("r", h, range(8, 16), lambda u: u == 12 and norm_stats(1, 0))
                    else:
                        residual_units("r", h, range(8 * a, 8 * a + 8))
                if not last:
                    retention_loads(h + 1)
                    for m in range(NT):
                        retention_values(h + 1, m)

            act.wait_ge(res_copied, 16)
            act.wait_ge(mod_stored, 16 * 6)
            act.wait_ge(rope_reduced, 2)
            norm_rows(0)
            for m in range(3):
                norm_load(0, m)
            retention_loads(0)
            norm_layer(0, 0, lambda m: retention_values(0, m))
            with act.Fori(0, RET_GROUPS - 1) as h:
                retention(h, False)
            retention(RET_GROUPS - 1, True)
            for n in range(4):
                act.wait_ge(res_out["r"][n], 64 * RET_GROUPS + FREE)
            if stop_after < 1:
                return

            def bias_load(g, h):
                act.dma_start(a_bias[:, h % 2], t["band"][bass.ds(g * GH + h, 1)].rearrange(
                    "a p n -> (a p) n")).then_inc(a_biasin[h % 2], 16)

            def attention_loads(g):
                act.wait_ge(a_max, g * (GH * NT) + FREE)
                act.wait_ge(a_lo, g * (2 * GH) + FREE)
                act.wait_ge(out_ready["a"], g * 16 + FREE)
                bias_load(g, 0)

            def attention_values(g, m):
                wait_bank("a", g * ATT_SLOTS + ATT0, g * 28, 0, m)
                act.activation(a_v[:, m], ps[:, m % 4], ACT.Copy).then_inc(bank_free["a"], 1)

            def attention(g, last):
                w0, d0 = g * ATT_SLOTS + ATT0, g * 28
                for blk, dst in ((1, a_q), (2, a_k)):
                    for m in range(NT):
                        wait_bank("a", w0, d0, blk, m)
                        act.activation(dst[:, :, m * P:(m + 1) * P],
                                       ps[:, m].rearrange("p (h n) -> p h n", h=GH), ACT.Copy)\
                            .then_inc(bank_free["a"], 1)
                    act.wait_ge(a_sums, g * 2 + blk)
                    c = 32 + 64 * (blk - 1)
                    act.activation(st[:, c + 32:c + 64], st[:, c:c + 32], ACT.Sqrt, scale=1.0 / P,
                                   bias=eps[:, 0:1]).then_inc(a_roots, 1)
                for n in range(8):
                    wait_bank("a", w0, d0, 3, n)
                    act.activation(a_g[:, n // 2, (n % 2) * 512:(n % 2 + 1) * 512], ps[:, n],
                                   ACT.Silu).then_inc(bank_free["a"], 1)
                e0, t0 = g * (GH * NT), g * (GH * (NT + 2))
                for n in range(4):
                    act.wait_ge(res_out["a"][n], g * 64 + FREE)

                def head_turned(h, k):
                    n = head_unit(h, k)
                    act.wait_ge(a_pdone, t0 + (n + 1))
                    bank = 6 if n == 1 else 4
                    act.activation((a_k if k else a_q)[:, h], psf[:, bank * 512:bank * 512 + S], ACT.Identity,
                                   scale=gains[:, k:k + 1]).then_inc(a_pevac, 1)

                def exps(e):
                    w = min(e % NT + 1, LEFT + 1) * P
                    act.wait_ge(a_neg, e0 + (e + 1))
                    act.activation(a_p[:, e % 3, 0:w], a_p[:, e % 3, 0:w], ACT.Exp,
                                   bias=st[:, 168 + e % 4:169 + e % 4],
                                   accum_out=st[:, 172 + e % 4:173 + e % 4]).then_inc(a_exp, 1)

                def prob_turned(e):
                    w = min(e % NT + 1, LEFT + 1) * P
                    act.wait_ge(a_pdone, t0 + (prob_unit(e) + 1))
                    if e >= 2:
                        act.wait_ge(a_odone, e0 + (e - 1))
                    act.activation(a_pT[:, e % 2, 0:w], psf[:, 4 * 512:4 * 512 + w], ACT.Copy)\
                        .then_inc(a_pevac, 1)

                def high(h, a):
                    act.wait_ge(a_gated, g * (2 * GH) + (2 * h + a + 1))
                    act.activation(a_ohi[:, h, a * 512:(a + 1) * 512], a_o[:, :], ACT.Copy)\
                        .then_inc(a_hi, 1)

                head_turned(0, 0)
                head_turned(0, 1)
                exps(0)
                for e in range(GH * NT):
                    h, i = divmod(e, NT)
                    if i == 1 and h + 1 < GH:
                        if h:
                            act.wait_ge(a_max, e0 + h * NT + FREE)
                        bias_load(g, h + 1)
                    if e + 1 < GH * NT:
                        exps(e + 1)
                    prob_turned(e)
                    if h + 1 < GH and i in (2, 4):
                        head_turned(h + 1, int(i == 4))
                    if i == 2 and h:
                        high(h - 1, 1)
                    if i == 6:
                        high(h, 0)
                high(GH - 1, 1)
                first_loads("a", g, range(16))

                def next_norm(u):
                    if 9 <= u <= 11:
                        act.wait_ge(res_out["a"][(u - 1) % 4], g * 64 + 16 * ((u - 1) // 4 + 1) + FREE)
                        norm_load(2, u - 9)
                    if u == 13:
                        norm_stats(2, 0)

                if last:
                    act.wait_ge(a_lo, ATT_GROUPS * 2 * GH + FREE)
                    norm_rows(2)
                    residual_units("a", g, range(16), next_norm)
                else:
                    residual_units("a", g, range(16))
                    attention_loads(g + 1)
                    for m in range(NT):
                        attention_values(g + 1, m)

            attention_loads(0)
            norm_layer(1, 1, lambda m: attention_values(0, m))
            with act.Fori(0, ATT_GROUPS - 1) as g:
                attention(g, False)
            attention(ATT_GROUPS - 1, True)
            for n in range(4):
                act.wait_ge(res_out["a"][n], 64 * ATT_GROUPS + FREE)
            if stop_after < 2:
                return

            def latents(m):
                wait_bank("m", MIX0, 0, 0, m)
                act.activation(l_lat[:, m], ps[:, m % 4, 0:LATW], ACT.Copy).then_inc(bank_free["m"], 1)

            norm_layer(2, 1, latents)
            act.dma_start(l_pw[:, :, :], t["pool_w"]).then_inc(l_consts, 16)
            act.dma_start(l_edge[:, :, :, :], t["edge"]).then_inc(l_consts, 16)
            act.dma_start(st[:, 184:192].bitcast(I32), t["pos2"]).then_inc(l_consts, 16)
            act.dma_start(cos2[:, :, :], t["inv2"].partition_broadcast(P)).then_inc(l_consts, 16)
            act.dma_start(qk_rows[:, 0], t["g_qnorm"][LNOPE:].partition_broadcast(P)).then_inc(l_consts, 16)
            act.dma_start(qk_rows[:, 1], t["g_knorm"][LNOPE:].partition_broadcast(P)).then_inc(l_consts, 16)
            act.wait_ge(l_angles, 2)
            act.activation(sin2[:, :, :], sin2[:, :, :], ACT.Sin).then_inc(l_tables, 1)
            act.activation(cos2[:, :, :], cos2[:, :, :], ACT.Sin).then_inc(l_tables, 1)
            act.wait_ge(l_sums, 2)
            act.activation(st[:, 16:24], st[:, 0:8], ACT.Sqrt, scale=1.0 / QLAT, bias=eps[:, 0:1])
            act.activation(st[:, 24:32], st[:, 8:16], ACT.Sqrt, scale=1.0 / KVLAT,
                           bias=eps[:, 0:1]).then_inc(l_roots, 1)
            for n in range(8):
                wait_bank("m", MIX0, 0, 1, n)
                act.activation(l_u[:, n // 2, PAD + 512 * (n % 2):PAD + 512 * (n % 2) + 512], ps[:, n],
                               ACT.Copy).then_inc(bank_free["m"], 1)
            for n in range(8):
                wait_bank("m", MIX0, 0, 2, n)
                act.activation(l_gp[:, n // 2, (n % 2) * 512:(n % 2 + 1) * 512], ps[:, n],
                               ACT.Silu).then_inc(bank_free["m"], 1)
            for n in range(8):
                wait_bank("m", MIX0, 0, 3, n)
                if n >= 2:
                    act.wait_ge(l_gastored[n % 2], 16 * (n // 2))
                act.activation(l_ga[:, n % 2], ps[:, n], ACT.Silu).then_inc(bank_free["m"], 1)
                act.wait_ge(bank_free["m"], 24 + n + 1)
                act.dma_start(t["sg"][(n // 2) * P:(n // 2 + 1) * P, (n % 2) * 512:(n % 2 + 1) * 512],
                              l_ga[:, n % 2]).then_inc(l_gastored[n % 2], 16)
            for n in range(8):
                act.wait_ge(l_yready, n + 1)
                act.activation(h_hi[:, n // 2, (n % 2) * 512:(n % 2 + 1) * 512], l_y[:, n % 2],
                               ACT.Copy).then_inc(l_yhi, 1)
            for n in range(3):
                act.wait_ge(l_lturned, n + 1)
                act.activation(l_qlhi[:, n] if n < 2 else l_klhi[:, :], psf[:, n * 1024:(n + 1) * 1024],
                               ACT.Identity, scale=gains[:, 7 + n:8 + n]).then_inc(l_lhi, 1)
            act.wait_ge(l_rcopied, 1)
            for n in range(2):
                act.wait_ge(l_gastored[n], 64)

            def roots(m):
                act.wait_ge(l_sums, 2 + m + 1)
                sums = qk_stats[:, :, m]
                act.activation(sums, sums, ACT.Sqrt, scale=1.0 / LQK, bias=eps[:, 0:1]).then_inc(l_roots, 1)

            for m in range(NT):
                bank = 4 * (m % 2)
                if m < NT - 1:
                    act.wait_ge(l_updone, m + 1)
                else:
                    act.wait_ge(w_used, MIX0 + 40 + RING)
                act.activation(l_q[:, m].rearrange("p (c n) -> p c n", c=2), ps[:, bank:bank + 2, 0:384],
                               ACT.Copy)
                kv = ps[:, bank + 2:bank + 4].rearrange("p c n -> p (c n)").rearrange(
                    "p (h n) -> p h n", h=LH)
                act.activation(l_k[:, m].rearrange("p (h n) -> p h n", h=LH)[:, :, 0:LNOPE],
                               kv[:, :, 0:LNOPE], ACT.Copy)
                act.activation(l_v[:, m].rearrange("p (h n) -> p h n", h=LH), kv[:, :, LNOPE:],
                               ACT.Copy).then_inc(l_upfree, 1)
                act.wait_ge(l_upfree, m + 1)
                if m >= 2:
                    act.wait_ge(l_sums, 2 + m - 1)
                act.activation(k_squares[m % 2], l_k[:, m], ACT.Square).then_inc(l_sq, 1)
                if m:
                    roots(m - 1)
            roots(NT - 1)
            def gate_load(n):
                h, a = n // 2, n % 2
                rows = slice(LV * (h % 2), LV * (h % 2) + LV)
                act.dma_start(l_sg[rows, :], t["sg"][h * LV:(h + 1) * LV, a * 512:(a + 1) * 512])\
                   .then_inc(l_sgin, 16)

            act.wait_ge(l_llo, 3)
            act.wait_ge(w_used, MIX0 + 40 + RING)
            gate_load(0)
            def l_head_turned(h, k):
                n = head_unit(h, k)
                act.wait_ge(l_pdone, n + 1)
                bank = 6 if n == 1 else 4
                act.activation(l_turned(h, k)[0:LQK], psf[0:LQK, bank * 512:bank * 512 + S].rearrange(
                    "p (m n) -> p m n", m=NT), ACT.Identity, scale=gains[0:LQK, 10 + k:11 + k]).then_inc(l_pevac, 1)

            def l_exps(e):
                h, i = divmod(e, NT)
                act.wait_ge(l_neg, e + 1)
                if e >= 3:
                    act.wait_ge(l_pdone, prob_unit(e - 3, LH) + 1)
                act.activation(l_p[:, e % 3], psf[:, (e % 2) * 1024:(e % 2) * 1024 + S], ACT.Exp,
                               scale=qk_stats[:, 0, i, h:h + 1], bias=st[:, 132 + e % 4:133 + e % 4],
                               accum_out=st[:, 136 + e % 4:137 + e % 4]).then_inc(l_exp, 1)

            def l_prob_turned(e):
                act.wait_ge(l_pdone, prob_unit(e, LH) + 1)
                if e >= 2:
                    act.wait_ge(l_odone, e - 1)
                act.activation(l_pT[:, e % 2], psf[:, 4 * 512:4 * 512 + S], ACT.Copy).then_inc(l_pevac, 1)

            def l_high(h, a):
                rows = slice(LV * (h % 2), LV * (h % 2) + LV)
                act.wait_ge(l_gated, 2 * h + a + 1)
                act.activation(h_hi[rows, 4 + h // 2, a * 512:(a + 1) * 512], l_o[rows, :],
                               ACT.Copy).then_inc(l_hi, 1)
                if 2 * h + a + 1 < 2 * LH:
                    gate_load(2 * h + a + 1)

            l_head_turned(0, 0)
            l_head_turned(0, 1)
            l_exps(0)
            for e in range(LH * NT):
                h, i = divmod(e, NT)
                if e + 1 < LH * NT:
                    l_exps(e + 1)
                l_prob_turned(e)
                if h + 1 < LH and i in (2, 4):
                    l_head_turned(h + 1, int(i == 4))
                if h and i == 2:
                    l_high(h - 1, 1)
                if i == 6:
                    l_high(h, 0)
            l_high(LH - 1, 1)
            def unit(u):
                return slice((u % 8) * P, (u % 8 + 1) * P), slice((u // 8) * 512, (u // 8 + 1) * 512)

            for u in range(19):
                if 3 <= u:
                    v = u - 3
                    act.wait_ge(out_ready["m"], v + 1)
                    act.dma_start(t["out"][unit(v)], l_x[:, v % 4]).then_inc(res_out["m"][v % 4], 16)
                if u < 16:
                    if u >= 4:
                        act.wait_ge(res_out["m"][u % 4], 16 * (u // 4))
                    act.dma_start(l_x[:, u % 4], t["res"][unit(u)]).then_inc(res_in["m"][u % 4], 16)
            for n in range(4):
                act.wait_ge(res_out["m"][n], 64)

        @block.vector
        def _(dve):
            links = [0]

            def link(ins, chain, base=0):
                links[0] += 1
                ins.then_inc(chain, 1)
                dve.wait_ge(chain, base + links[0])

            dve.memset(eps[:, :], EPS).then_inc(dve_init, 1)
            dve.memset(ones[:, :], 1.0).then_inc(dve_init, 1)
            dve.wait_ge(dve_init, 2)
            ang, turns = xn[0][:, 0], xn[0][:, 1]
            dve.wait_ge(pos_in, 16)
            dve.wait_ge(const_in, 48)
            link(dve.tensor_copy(ang, cos[:, :].bitcast(I32)), rope_chain)
            link(dve.tensor_scalar(ang, ang, gains[:, 2:3], None, ALU.mult), rope_chain)
            for table, quarter in ((sin, 0.0), (cos, 0.25)):
                link(dve.tensor_scalar(turns, ang, 1.0 / TWO_PI, quarter, ALU.mult, ALU.add), rope_chain)
                link(dve.tensor_scalar(turns, turns, MAGIC, MAGIC, ALU.add, ALU.subtract), rope_chain)
                link(dve.scalar_tensor_tensor(table[:, :], turns, -C1, ang, ALU.mult, ALU.add), rope_chain)
                link(dve.scalar_tensor_tensor(table[:, :], turns, -C2, table[:, :], ALU.mult, ALU.add),
                     rope_chain)
                link(dve.scalar_tensor_tensor(table[:, :], turns, -C3, table[:, :], ALU.mult, ALU.add),
                     rope_chain)
                link(dve.tensor_scalar(table[:, :], table[:, :], quarter * TWO_PI, math.pi, ALU.add, ALU.min),
                     rope_chain)
                dve.tensor_scalar(table[:, :], table[:, :], -math.pi, None, ALU.max).then_inc(rope_reduced, 1)
            link(dve.tensor_scalar(gains[:, 0:1], gains[:, 0:1], P ** -0.5, None, ALU.mult), rope_chain)
            for n in range(PIECES):
                dve.wait_ge(mod_done, n + 1)
                if n:
                    dve.wait_ge(mod_stored, 16 * n)
                dve.tensor_copy(mod_row[:, :], ps[0:1, n]).then_inc(mod_copied, 1)

            def norm_layer(l):
                dve.wait_ge(n_rows, 48 * (l + 1))
                dve.scalar_tensor_tensor(arow[l][:, :], arow[l][:, :], 1.0, ngrow[l][:, :], ALU.add,
                                         ALU.mult).then_inc(n_arow, 1)
                dve.wait_ge(n_arow, l + 1)
                for m in range(NT + 1):
                    if m < NT:
                        e = l * NT + m
                        tile = xn[l][:, m % 2]
                        dve.wait_ge(n_root, e + 1)
                        dve.reciprocal(st[:, 8 + m:9 + m], st[:, 8 + m:9 + m]).then_inc(n_rr, 1)
                        dve.wait_ge(n_rr, e + 1)
                        dve.scalar_tensor_tensor(tile, x_in[l][:, m % 3], st[:, 8 + m:9 + m], arow[l][:, :],
                                                 ALU.mult, ALU.mult).then_inc(n_mul, 1)
                        dve.wait_ge(n_mul, e + 1)
                        dve.tensor_tensor(tile, tile, srow[l][:, :], ALU.add).then_inc(n_xn, 1)
                    if m:
                        e = l * NT + m - 1
                        sl = slice((m - 1) * P, m * P)
                        dve.wait_ge(n_hi, e + 1)
                        dve.tensor_tensor(h_lo[:, :, sl], psf[:, (4 + 2 * ((m - 1) % 2)) * 512:][:, 0:D]
                                          .rearrange("p (k n) -> p k n", k=KD), h_hi[:, :, sl].bitcast(F32),
                                          ALU.subtract).then_inc(n_lo, 1)
                dve.wait_ge(n_gate, 16 * (l + 1))

            norm_layer(0)

            def residual(l, i, units, tmp, chain, base):
                buf = r_x if l == "r" else a_x
                for u in units:
                    half = unit_of(l, u)[1]
                    if u == 15:
                        slots = (RET_SLOTS, 0) if l == "r" else (ATT_SLOTS, ATT0)
                        dve.wait_ge(w_used, i * slots[0] + (slots[0] + slots[1] + RING))
                    else:
                        dve.wait_ge(out_done[l], i * 15 + (u + 1))
                    if u:
                        dve.wait_ge(out_ready[l], i * 16 + u + FREE)
                    dve.tensor_tensor(tmp, ps[:, u % 4], gate[:, half * 512:(half + 1) * 512],
                                      ALU.mult).then_inc(out_free[l], 1)
                    dve.wait_ge(out_free[l], i * 16 + (u + 1) + FREE)
                    dve.wait_ge(res_in[l][u % 4], i * 64 + 16 * (u // 4 + 1))
                    dve.tensor_tensor(buf[:, u % 4], buf[:, u % 4], tmp, ALU.add).then_inc(out_ready[l], 1)

            RL = 1 + 3 * (KD - 1) + 5
            dve.wait_ge(rope_tables, 2)
            with dve.Fori(0, RET_GROUPS) as h:
                links[0] = 0
                base = h * RL

                def modulation(n):
                    dve.wait_ge(m_in, h * 48 + 16 * (n + 1))
                    for k in range(KD):
                        other = ada_c[:, KD] if k == 0 else acc[:, n]
                        ins = dve.scalar_tensor_tensor(acc[:, n], ada_c[:, k], cnext[:, k:k + 1], other,
                                                       ALU.mult, ALU.add)
                        if k < KD - 1:
                            link(ins, dve_r, base)
                        else:
                            ins.then_inc(m_acc, 1)

                for n in range(4):
                    dve.wait_ge(res_out["r"][n], h * 64 + FREE)
                dve.wait_ge(w_used, h * RET_SLOTS + RING)
                cnext = st[:, 176:176 + KD]
                link(dve.tensor_copy(cnext, ccol[:, :, :].rearrange("p l k -> p (l k)")[
                    :, bass.ds(h * KD + KD, KD)]), dve_r, base)
                modulation(0)
                modulation(1)
                dve.wait_ge(bank_free["r"], h * 24 + 16)
                for src in (r_q, r_k):
                    first, second = src[:, 0], src[:, 1]
                    dve.tensor_tensor(r_s[:, 0], first, sin[:, :], ALU.mult)
                    link(dve.tensor_tensor(r_s[:, 1], second, sin[:, :], ALU.mult), dve_r, base)
                    dve.tensor_tensor(first, first, cos[:, :], ALU.mult)
                    link(dve.tensor_tensor(second, second, cos[:, :], ALU.mult), dve_r, base)
                    dve.tensor_tensor(first, first, r_s[:, 1], ALU.subtract)
                    ins = dve.tensor_tensor(second, second, r_s[:, 0], ALU.add)
                    if src is r_q:
                        link(ins, dve_r, base)
                    else:
                        ins.then_inc(r_rope, 1)
                modulation(2)
                dve.wait_ge(r_consts, h * 32 + 32)
                for m in range(NT):
                    dve.wait_ge(bank_free["r"], h * 24 + (17 + m))
                    dve.tensor_tensor(r_g[:, m], r_g[:, m], r_gn[:, :], ALU.mult).then_inc(r_gready, 1)
                dve.wait_ge(r_rope, h + 1)

                def decay(i):
                    dve.wait_ge(r_sdone, h * NT + (i + 1))
                    if i >= 2:
                        dve.wait_ge(r_odone, h * NT + (i - 1))
                    w = (i + 1) * P
                    dve.tensor_tensor(r_s[:, i % 2, 0:w], psf[:, (i % 2) * 1024:(i % 2) * 1024 + w],
                                      r_decay[:, (NT - 1 - i) * P:], ALU.mult).then_inc(r_sready, 1)

                def gated(i):
                    dve.wait_ge(r_root, h * NT + (i + 1))
                    dve.reciprocal(st[:, 24 + i:25 + i], st[:, 24 + i:25 + i]).then_inc(r_rinv, 1)
                    dve.wait_ge(r_rinv, h * NT + (i + 1))
                    dve.wait_ge(r_gready, h * NT + (i + 1))
                    dve.scalar_tensor_tensor(r_g[:, i], ps[:, 4 + i % 2], st[:, 24 + i:25 + i], r_g[:, i],
                                             ALU.mult, ALU.mult).then_inc(r_gated, 1)

                def low(i):
                    sl = slice((i % 4) * P, (i % 4 + 1) * P)
                    dve.wait_ge(r_hi, h * NT + (i + 1))
                    dve.tensor_tensor(r_olo[:, :, sl], ps[:, 6].rearrange("p (e n) -> p e n", e=4),
                                      r_ohi[:, :, sl].bitcast(F32), ALU.subtract).then_inc(r_lo, 1)

                for a in range(2):
                    decay(4 * a)
                    if a == 0:
                        decay(1)
                        for n in range(3):
                            dve.wait_ge(m_red, h * 3 + (n + 1))
                            dve.tensor_copy(acc[0:1, n], ps[0:1, 5 + n]).then_inc(m_row, 1)
                    for i in range(4 * a, 4 * a + 4):
                        if i % 4 < 3 and i > 0:
                            decay(i + 1)
                        gated(i)
                        if i % 4:
                            low(i - 1)
                    low(4 * a + 3)
                    residual("r", h, range(8 * a, 8 * a + 8), r_tmp[:, :], dve_r, base)
            assert links[0] == RL, links
            if stop_after < 1:
                return
            norm_layer(1)

            AL = 2 * (2 * GH - 1)
            with dve.Fori(0, ATT_GROUPS) as g:
                links[0] = 0
                base = g * AL
                for blk, src in ((1, a_q), (2, a_k)):
                    dve.wait_ge(bank_free["a"], g * 32 + 8 * (blk + 1))
                    c = 32 + 64 * (blk - 1)
                    for h in range(GH):
                        link(dve.tensor_tensor(a_sq[:, :], src[:, h], src[:, h], ALU.mult), dve_a, base)
                        ins = dve.tensor_reduce(st[:, c + 8 * h:c + 8 * h + 8],
                                                a_sq[:, :].rearrange("p (m n) -> p m n", m=NT), AX.X, ALU.add)
                        if h < GH - 1:
                            link(ins, dve_a, base)
                        else:
                            ins.then_inc(a_sums, 1)
                    dve.wait_ge(a_sums, g * 2 + blk)
                    dve.wait_ge(a_roots, g * 2 + blk)
                    r = st[:, c + 32:c + 64]
                    dve.reciprocal(r, r).then_inc(a_rchain, 1)
                    dve.wait_ge(a_rchain, g * 2 + blk)
                    whole = src[:, :, :].rearrange("p h (m n) -> p (h m) n", m=NT)
                    dve.tensor_tensor(whole, whole, r.unsqueeze(2).to_broadcast([P, GH * NT, P]),
                                      ALU.mult).then_inc(a_normed, 1)
                e0, t0 = g * (GH * NT), g * (GH * (NT + 2))
                for n in range(4):
                    dve.wait_ge(res_out["a"][n], g * 64 + FREE)

                def bias_masked(h):
                    dve.wait_ge(a_biasin[h % 2], g * 32 + 16 * (h // 2 + 1))
                    dve.memset(a_bias[64:128, h % 2, 0:64], NEG).then_inc(a_biasok, 1)
                    dve.memset(a_bias[0:64, h % 2, BANDW - 64:BANDW], NEG).then_inc(a_biasok, 1)
                    dve.wait_ge(a_biasok, g * (2 * GH) + (2 * h + 2))

                def maxima(e):
                    h, i = divmod(e, NT)
                    w = min(i + 1, LEFT + 1) * P
                    if i == 0:
                        bias_masked(h)
                    dve.wait_ge(a_sdone, e0 + (e + 1))
                    if e >= 3:
                        dve.wait_ge(a_pdone, t0 + (prob_unit(e - 3) + 1))
                    dve.memset(st[:, 160:161], 0.0)
                    dve.tensor_tensor_reduce(a_p[:, e % 3, 0:w], psf[:, (e % 2) * 1024:(e % 2) * 1024 + w],
                                             a_bias[:, h % 2, BANDW - w:], 1.0, -3.0e38, ALU.add, ALU.max,
                                             st[:, 164 + e % 4:165 + e % 4]).then_inc(a_max, 1)
                    dve.wait_ge(a_max, e0 + (e + 1) + FREE)
                    dve.tensor_scalar(st[:, 168 + e % 4:169 + e % 4], st[:, 164 + e % 4:165 + e % 4], -1.0,
                                      None, ALU.mult).then_inc(a_neg, 1)

                def normed(e):
                    w = min(e % NT + 1, LEFT + 1) * P
                    dve.wait_ge(a_exp, e0 + (e + 1))
                    r = st[:, 172 + e % 4:173 + e % 4]
                    dve.reciprocal(r, r).then_inc(a_rinv, 1)
                    dve.wait_ge(a_rinv, e0 + (e + 1))
                    dve.tensor_scalar(a_p[:, e % 3, 0:w], a_p[:, e % 3, 0:w], r, None,
                                      ALU.mult).then_inc(a_prob, 1)

                def gated(h, a):
                    dve.wait_ge(a_odone, e0 + (h * NT + 4 * a + 4))
                    if h or a:
                        dve.wait_ge(a_lo, g * (2 * GH) + (2 * h + a) + FREE)
                    dve.tensor_tensor(a_o[:, :], ps[:, 6 + a], a_g[:, h, a * 512:(a + 1) * 512],
                                      ALU.mult).then_inc(a_gated, 1)

                def low(h, a):
                    dve.wait_ge(a_hi, g * (2 * GH) + (2 * h + a + 1))
                    dve.tensor_tensor(a_olo[:, h, a * 512:(a + 1) * 512], a_o[:, :],
                                      a_ohi[:, h, a * 512:(a + 1) * 512].bitcast(F32),
                                      ALU.subtract).then_inc(a_lo, 1)

                maxima(0)
                for e in range(GH * NT):
                    h, i = divmod(e, NT)
                    if e + 1 < GH * NT:
                        maxima(e + 1)
                    normed(e)
                    if h and i == 1:
                        gated(h - 1, 1)
                    if h and i == 3:
                        low(h - 1, 1)
                    if i == 5:
                        gated(h, 0)
                    if i == 7:
                        low(h, 0)
                gated(GH - 1, 1)
                low(GH - 1, 1)
                residual("a", g, range(16), a_o[:, :], dve_a, base)
            assert links[0] == AL, links
            if stop_after < 2:
                return
            norm_layer(2)

            links[0] = 0
            for n in range(4):
                dve.memset(l_u[:, n, 0:PAD], 0.0)
                dve.memset(l_u[:, n, PAD + S:PADW], 0.0).then_inc(l_pads, 1)
            dve.wait_ge(l_consts, 16 * 6)
            fr, ang, turns = l_tmp[:, 0, 0:P], l_tmp[:, 0, P:2 * P], l_tmp[:, 0, 2 * P:3 * P]
            fr, ang, turns = (v.rearrange("p (m n) -> p m n", m=NT) for v in (fr, ang, turns))
            link(dve.tensor_copy(fr[:, :, 0], st[:, 184:192].bitcast(I32)), l_chain)
            link(dve.tensor_tensor(ang, cos2[:, :, :], fr[:, :, 0:1].to_broadcast([P, NT, HR]), ALU.mult), l_chain)
            for table, quarter in ((sin2, 0.0), (cos2, 0.25)):
                link(dve.tensor_scalar(turns, ang, 1.0 / TWO_PI, quarter, ALU.mult, ALU.add), l_chain)
                link(dve.tensor_scalar(turns, turns, MAGIC, MAGIC, ALU.add, ALU.subtract), l_chain)
                link(dve.scalar_tensor_tensor(table[:, :, :], turns, -C1, ang, ALU.mult, ALU.add), l_chain)
                link(dve.scalar_tensor_tensor(table[:, :, :], turns, -C2, table[:, :, :], ALU.mult, ALU.add),
                     l_chain)
                link(dve.scalar_tensor_tensor(table[:, :, :], turns, -C3, table[:, :, :], ALU.mult, ALU.add),
                     l_chain)
                link(dve.tensor_scalar(table[:, :, :], table[:, :, :], quarter * TWO_PI, math.pi, ALU.add,
                                       ALU.min), l_chain)
                dve.tensor_scalar(table[:, :, :], table[:, :, :], -math.pi, None, ALU.max).then_inc(l_angles, 1)
            dve.wait_ge(bank_free["m"], 8)
            for n, (lo, width) in enumerate(((0, QLAT), (QLAT, KVLAT))):
                part = l_lat[:, :, lo:lo + width]
                sq = l_tmp[:, :, :].rearrange("p a n -> p (a n)")[:, 0:NT * width].rearrange(
                    "p (m n) -> p m n", m=NT)
                link(dve.tensor_tensor(sq, part, part, ALU.mult), l_chain)
                dve.tensor_reduce(st[:, 8 * n:8 * n + 8], sq, AX.X, ALU.add).then_inc(l_sums, 1)
                dve.wait_ge(l_sums, n + 1)
            dve.wait_ge(l_roots, 1)
            link(dve.reciprocal(st[:, 16:32], st[:, 16:32]), l_chain)
            for n, (lo, width) in enumerate(((0, QLAT), (QLAT, KVLAT))):
                part = l_lat[:, :, lo:lo + width]
                r = st[:, 16 + 8 * n:24 + 8 * n].unsqueeze(2).to_broadcast([P, NT, width])
                dve.tensor_tensor(part, part, r, ALU.mult).then_inc(l_latok, 1)
            dve.wait_ge(l_pads, 4)
            for n, window in enumerate(POOLS):
                dve.wait_ge(bank_free["m"], 8 + 2 * n + 2)
                src, step, lo = l_u[:, n], 1, 1
                link(dve.tensor_tensor(l_sum[:, 0, 1:PADW], l_u[:, n, 1:PADW], l_u[:, n, 0:PADW - 1],
                                       ALU.add), l_chain)
                cur, reach, lo, hi = 0, 1, 1, PADW
                while 2 * reach < window:
                    lo, hi = lo + reach, hi - reach
                    link(dve.tensor_tensor(l_sum[:, 1 - cur, lo:hi], l_sum[:, cur, lo - reach:hi - reach],
                                           l_sum[:, cur, lo + reach:hi + reach], ALU.add), l_chain)
                    cur, reach = 1 - cur, 2 * reach
                sums = l_sum[:, cur]
                for e, c in enumerate((PAD, PAD + S - 8)):
                    link(dve.tensor_tensor(l_e8[:, e], sums[:, c:c + 8], l_edge[:, n, e], ALU.mult), l_chain)
                for e, c in enumerate((PAD, PAD + S - 8)):
                    link(dve.tensor_tensor(l_u[:, n, c:c + 8], l_e8[:, e], l_u[:, n, c:c + 8],
                                           ALU.subtract), l_chain)
                inner = slice(PAD + 8, PAD + S - 8)
                dve.scalar_tensor_tensor(l_u[:, n, inner], sums[:, inner], 1.0 / window, l_u[:, n, inner],
                                         ALU.mult, ALU.subtract).then_inc(l_diff, 1)
                dve.wait_ge(l_diff, n + 1)
            for n in range(9):
                if n < 8:
                    dve.wait_ge(l_ydone, n + 1)
                    if n >= 2:
                        dve.wait_ge(l_ylo, n - 1)
                    dve.scalar_tensor_tensor(l_y[:, n % 2], ps[:, n], gains[:, 3 + n // 2:4 + n // 2],
                                             l_gp[:, n // 2, (n % 2) * 512:(n % 2 + 1) * 512], ALU.mult,
                                             ALU.mult).then_inc(l_yready, 1)
                if n:
                    v = n - 1
                    sl = slice((v % 2) * 512, (v % 2 + 1) * 512)
                    dve.wait_ge(l_yhi, v + 1)
                    dve.tensor_tensor(h_lo[:, v // 2, sl], l_y[:, v % 2], h_hi[:, v // 2, sl].bitcast(F32),
                                      ALU.subtract).then_inc(l_ylo, 1)
            for n in range(3):
                dve.wait_ge(l_lhi, n + 1)
                hi, lo = (l_qlhi[:, n], l_qllo[:, n]) if n < 2 else (l_klhi[:, :], l_kllo[:, :])
                dve.scalar_tensor_tensor(lo, psf[:, n * 1024:(n + 1) * 1024], gains[:, 7 + n:8 + n],
                                         hi.bitcast(F32), ALU.mult, ALU.subtract).then_inc(l_llo, 1)
            def heads(x):
                return x[:, :, :].rearrange("p m (h n) -> p m h n", h=LH)

            dve.wait_ge(l_ydone, 8)
            dve.wait_ge(l_tables, 2)
            for n in range(2):
                for e in range(2):
                    row = qk_rows[:, n, e * HR:(e + 1) * HR].unsqueeze(1).to_broadcast([P, NT, HR])
                    for c, table in enumerate((cos2, sin2)):
                        dve.tensor_tensor(qk_tables[:, n, e, c], table[:, :, :], row, ALU.mult)
            link(dve.tensor_scalar(gains[:, 10:11], gains[:, 10:11], LQK ** -0.5, None, ALU.mult), l_chain)
            dve.tensor_copy(heads(l_k)[:, :, :, LNOPE:], l_lat[:, :, QLAT + KVLAT:].unsqueeze(2)
                            .to_broadcast([P, NT, LH, LROPE])).then_inc(l_rcopied, 1)
            dve.wait_ge(l_rcopied, 1)
            def qk_sums(m):
                dve.wait_ge(l_upfree, m + 1)
                sq = l_tmp[:, 0, 0:LH * LQK]
                link(dve.tensor_tensor(sq, l_q[:, m], l_q[:, m], ALU.mult), l_chain)
                dve.tensor_reduce(qk_stats[:, 0, m], sq.rearrange("p (h n) -> p h n", h=LH), AX.X, ALU.add)
                dve.wait_ge(l_sq, m + 1)
                dve.tensor_reduce(qk_stats[:, 1, m], k_squares[m % 2].rearrange("p (h n) -> p h n", h=LH), AX.X,
                                  ALU.add).then_inc(l_sums, 1)
                dve.wait_ge(l_sums, 2 + m + 1)

            def q_rope(m):
                dve.wait_ge(l_roots, m + 2)
                dve.reciprocal(qk_stats[:, :, m], qk_stats[:, :, m]).then_inc(l_rr, 1)
                x1, x2 = rope_parts(l_q, m)
                (cos1, sin1), (cos2_, sin2_) = (
                    [qk_tables[:, 0, e, c, m].unsqueeze(1).to_broadcast([P, LH, HR]) for c in range(2)]
                    for e in range(2))
                t1, t2 = (l_tmp[:, 0, LH * LQK + a * P:][:, 0:P].rearrange("p (h n) -> p h n", h=LH)
                          for a in range(2))
                dve.tensor_tensor(t1, x1, sin1, ALU.mult)
                link(dve.tensor_tensor(t2, x2, sin2_, ALU.mult), l_chain)
                dve.tensor_tensor(x1, x1, cos1, ALU.mult)
                link(dve.tensor_tensor(x2, x2, cos2_, ALU.mult), l_chain)
                dve.tensor_tensor(x1, x1, t2, ALU.subtract)
                dve.tensor_tensor(x2, x2, t1, ALU.add).then_inc(l_qdone, 1)
                dve.wait_ge(l_qdone, m + 1)

            for m in range(NT + 1):
                if m < NT:
                    qk_sums(m)
                if m:
                    q_rope(m - 1)

            def l_maxima(e):
                h, i = divmod(e, NT)
                dve.wait_ge(l_sdone, e + 1)
                dve.tensor_reduce(st[:, 128 + e % 4:129 + e % 4], psf[:, (e % 2) * 1024:(e % 2) * 1024 + S],
                                  AX.X, ALU.max).then_inc(l_max, 1)
                dve.wait_ge(l_max, e + 1)
                dve.tensor_scalar(st[:, 132 + e % 4:133 + e % 4], st[:, 128 + e % 4:129 + e % 4],
                                  qk_stats[:, 0, i, h:h + 1], -1.0, ALU.mult, ALU.mult).then_inc(l_neg, 1)

            def l_normed(e):
                dve.wait_ge(l_exp, e + 1)
                r = st[:, 136 + e % 4:137 + e % 4]
                dve.reciprocal(r, r).then_inc(l_rinv, 1)
                dve.wait_ge(l_rinv, e + 1)
                dve.tensor_scalar(l_p[:, e % 3], l_p[:, e % 3], r, None, ALU.mult).then_inc(l_prob, 1)

            def l_gate(h, a):
                rows, n = slice(LV * (h % 2), LV * (h % 2) + LV), 2 * h + a
                dve.wait_ge(l_odone, h * NT + 4 * a + 4)
                dve.wait_ge(l_sgin, 16 * (n + 1))
                if n:
                    dve.wait_ge(l_lo, n)
                dve.tensor_tensor(l_o[rows, :], ps[rows, 6 + a], l_sg[rows, :], ALU.mult).then_inc(l_gated, 1)

            def l_low(h, a):
                rows, sl = slice(LV * (h % 2), LV * (h % 2) + LV), slice(a * 512, (a + 1) * 512)
                dve.wait_ge(l_hi, 2 * h + a + 1)
                dve.tensor_tensor(h_lo[rows, 4 + h // 2, sl], l_o[rows, :],
                                  h_hi[rows, 4 + h // 2, sl].bitcast(F32), ALU.subtract).then_inc(l_lo, 1)

            l_maxima(0)
            for e in range(LH * NT):
                h, i = divmod(e, NT)
                if e + 1 < LH * NT:
                    l_maxima(e + 1)
                l_normed(e)
                if h and i == 1:
                    l_gate(h - 1, 1)
                if h and i == 3:
                    l_low(h - 1, 1)
                if i == 5:
                    l_gate(h, 0)
                if i == 7:
                    l_low(h, 0)
            l_gate(LH - 1, 1)
            l_low(LH - 1, 1)
            for u in range(16):
                if u % 8 == 7:
                    dve.wait_ge(w_used, MIX0 + 40 + u + 1 + RING)
                else:
                    dve.wait_ge(out_done["m"], u - u // 8 + 1)
                if u:
                    dve.wait_ge(out_ready["m"], u)
                dve.tensor_tensor(l_t[:, :], ps[:, u % 4], gate[:, (u // 8) * 512:(u // 8 + 1) * 512],
                                  ALU.mult).then_inc(out_free["m"], 1)
                dve.wait_ge(out_free["m"], u + 1)
                dve.wait_ge(res_in["m"][u % 4], 16 * (u // 4 + 1))
                dve.tensor_tensor(l_x[:, u % 4], l_x[:, u % 4], l_t[:, :], ALU.add).then_inc(out_ready["m"], 1)


SCRATCH = {"sg": (512, 1024)}


def lay_out(inputs):
    f = {k: np.asarray(v) for k, v in inputs.items()}
    w = []

    def slots(m):
        w.extend(m.reshape(-1, P, 512))

    def halves(m):
        slots(m[:, :512])
        slots(m[:, 512:])

    wi, wo = f["ret_w_in"][0], f["ret_w_out"][0]
    for h in range(4):
        slots(wi[:, 2048 + 512 * h:2560 + 512 * h])
        slots(np.concatenate([wi[:, 256 * h:256 * h + 256], wi[:, 1024 + 256 * h:1280 + 256 * h]], 1))
        slots(wi[:, 4096 + 512 * h:4608 + 512 * h])
        halves(wo[512 * h:512 * h + 512])
    wi, wo = f["att_w_in"][0], f["att_w_out"][0]
    for g in range(4):
        for part in (2, 0, 1, 3):
            slots(wi[:, 2048 * part + 512 * g:2048 * part + 512 * g + 512])
        halves(wo[512 * g:512 * g + 512])
    wi = f["w_in_2"][0]
    slots(np.pad(wi[:, 1024:1440], ((0, 0), (0, 96))))
    slots(wi[:, 0:512])
    slots(wi[:, 512:1024])
    slots(wi[:, 1440:1952])
    uq = f["w_uq_2"][0]
    for c in range(2):
        slots(np.pad(uq[:, 384 * c:384 * c + 384], ((0, 0), (0, 128))))
    uk = f["w_ukv_2"][0]
    slots(uk[:, :512])
    slots(uk[:, 512:])
    w.extend([np.zeros((P, 512), np.float32)] * 2)
    halves(f["w_out_2"][0])
    w = np.stack(w)
    assert w.shape[0] == SLOTS, w.shape

    aw = np.concatenate([f["ada_w"], f["ada_w_2"]])
    ab = np.concatenate([f["ada_b"], f["ada_b_2"]])
    aw = aw.reshape(3, KD, P, PIECES, 512).transpose(0, 3, 2, 1, 4).reshape(18, P, KD, 512)
    bias = np.concatenate([ab.reshape(18, 1, 1, 512), np.zeros((18, P - 1, 1, 512), np.float32)], 1)
    ada = np.concatenate([aw, bias], 2)

    c1, c2 = f["c"].reshape(KD, P).T, f["c_2"].reshape(KD, P).T
    cond = np.stack([c1, c1, c1, c2, c2], 1)
    i = np.arange(0, 256, 2, dtype=np.float32)
    inv = (1.0 / (np.float32(10000.0) ** (i / np.float32(256.0)))).astype(np.float32)
    col = lambda v: v.reshape(-1, P).T
    nope = [np.concatenate([f[n][0, :LNOPE], np.ones(P - LNOPE, np.float32)])[:, None]
            for n in ("g_qnorm_2", "g_knorm_2")]
    gains = np.concatenate([col(f["att_q_g"]), col(f["att_k_g"]), col(inv), col(f["pool_scale_2"]),
                            col(f["g_q_lat_2"]), col(f["g_kv_lat_2"]), *nope, np.zeros((P, 4), np.float32)], 1)

    lg = np.log(1.0 - 2.0 ** (-5.0 - np.arange(4)))
    j, q = np.arange(P)[:, None], np.arange(P)[None, :]
    far = np.stack([q - j + P * n for n in range(NT - 1, 0, -1)])
    near = np.abs(q - j)[None]
    power = np.exp(lg[:, None, None, None] * np.concatenate([far, near])[None])
    power[:, -1][:, (j // 64) > (q // 64)] = 0.0
    decay = (power / 16.0).transpose(0, 2, 1, 3).reshape(4, P, NT * P).astype(np.float32)

    rel = f["att_rel_bias"][0]
    diag = np.concatenate([np.repeat(rel[:, 256:257], 511, 1), rel[:, ::-1][:, :256]], 1)
    band = np.stack([diag[:, 127 - n:127 - n + BANDW] for n in range(P)], 1)

    edge = np.zeros((P, 4, 2, 8), np.float32)
    for n, window in enumerate(POOLS):
        for e, c in enumerate((0, S - 8)):
            tt = np.arange(c, c + 8)
            edge[:, n, e] = 1.0 / (np.clip(tt + window // 2, 0, S) - np.clip(tt - window // 2, 0, S))
    inv2 = (np.float32(10000.0) ** (-np.arange(0, LROPE, 2, dtype=np.float32) / np.float32(LROPE)))

    return {
        "w": w, "ada": ada, "cond": cond, "gains": gains, "x": f["x"][0], "pos": f["positions"][0],
        "norm_g": np.concatenate([f["norm_g"], f["norm_g_2"]]), "ret_gn": f["ret_gn_g"].reshape(4, 512),
        "pool_w": f["pool_w_2"][0].transpose(1, 0, 2), "edge": edge, "pos2": f["positions_2"].reshape(NT, P).T,
        "inv2": np.repeat(inv2[None], NT, 0), "g_qnorm": f["g_qnorm_2"][0], "g_knorm": f["g_knorm_2"][0],
        "decay": decay, "ident": np.eye(P, dtype=np.float32), "band": band,
    }


def kernel(**inputs):
    import concourse.bacc as bacc
    from concourse.bass_utils import run_bass_kernel_spmd

    nc = bacc.Bacc("TRN2", target_bir_lowering=False, num_devices=1)
    arrays = {f"in_{k}": np.ascontiguousarray(v) for k, v in lay_out(inputs).items()}
    t = {k[3:]: nc.dram_tensor(k, v.shape, mybir.dt.from_np(v.dtype), kind="ExternalInput").ap()
         for k, v in arrays.items()}
    t["out"] = nc.dram_tensor("out", (S, D), F32, kind="ExternalOutput").ap()
    t["res"] = nc.dram_tensor("res", (S, D), F32, kind="Internal").ap()
    t["mod"] = nc.dram_tensor("mod", (18, 512), F32, kind="Internal").ap()
    for name, shape in SCRATCH.items():
        t[name] = nc.dram_tensor(name, shape, F32, kind="Internal").ap()
    build_program(nc, t)
    result = run_bass_kernel_spmd(nc, [arrays], core_ids=[0])
    return np.asarray(result.results[0]["out"]).reshape(1, S, D)
```

```python
from contextlib import ExitStack
import math

import numpy as np

import concourse.bass as bass
from concourse import mybir

F32 = mybir.dt.float32
F32R = mybir.dt.float32r
I32 = mybir.dt.int32
ALU = mybir.AluOpType
ACT = mybir.ActivationFunctionType
AX = mybir.AxisListType

P = 128
D = 1024
S = 1024
NT = S // P
KD = D // P
EPS = 1e-6
NEG = -1e30

RING = 8
STAGE = 4
RET_GROUPS, RET_SLOTS = 4, 32
ATT_GROUPS, ATT_SLOTS = 4, 40
GH = 4
MIX_SLOTS = 56
ATT0 = RET_GROUPS * RET_SLOTS
MIX0 = ATT0 + ATT_GROUPS * ATT_SLOTS
SLOTS = MIX0 + MIX_SLOTS

ADA = KD + 1
PIECES = 6
LEFT = 4
BANDW = (LEFT + 1) * P
POOLS = (2, 4, 8, 16)
LH, LQK, LNOPE, LROPE, LV = 8, 96, 64, 32, 64
QLAT, KVLAT = 256, 128
LATW = QLAT + KVLAT + LROPE
HR = LROPE // 2
PAD = 8
PADW = S + 2 * PAD

FREE = 1

TWO_PI = 2.0 * math.pi
C1 = 6.28125
C2 = round((TWO_PI - C1) * 2**20) / 2**20
C3 = TWO_PI - C1 - C2
MAGIC = 1.5 * 2**23


def build_program(nc, t):
    with ExitStack() as ctx:
        def sb(name, shape, dt=F32, where=None):
            return (where or ctx).enter_context(nc.sbuf_tensor(name, shape, dt))

        def sem(name):
            return ctx.enter_context(nc.semaphore(name))

        def overlay(region, size, *sets):
            for n, tensors in enumerate(sets):
                with ExitStack() as own:
                    total = 0
                    for m, tensor in enumerate(tensors):
                        if isinstance(tensor, (int, float)):
                            tensor = (f"{region}_gap{n}_{m}", [P, int(tensor * 256)], F32)
                        name, shape, dt = tensor
                        b[name] = sb(name, shape, dt, own)
                        total += 4 * int(np.prod(shape[1:]))
                    assert total <= size * 1024, (region, n, total)
            sb(region, [P, int(size * 256)])

        b = {}
        w_hi = sb("w_hi", [P, RING, 512], F32R)
        w_lo = sb("w_lo", [P, RING, 512], F32R)
        stage = sb("stage", [P, STAGE, 512])
        ident = sb("ident", [P, P])
        ones = sb("ones", [P, 2])
        eps = sb("eps", [P, 1])
        ccol = sb("ccol", [P, 5, KD])
        gate = sb("gate", [P, D])
        st = sb("st", [P, 192])
        gains = sb("gains", [P, 16])
        qk_rows = sb("qk_rows", [P, 2, LROPE])
        ps = ctx.enter_context(nc.psum_tensor("ps", [P, 8, 512], F32))
        psf = ps[:, :, :].rearrange("p b n -> p (b n)")

        overlay("region_h", 64,
                [("ada_a", [P, 3, ADA, 512], F32)],
                [("h_hi", [P, KD, S], F32R), ("h_lo", [P, KD, S], F32R)],
                [24, ("k_scratch", [P, 2, LH, HR], F32), 27, ("squares", [P, 2, S], F32), ("qk_tables", [P, S], F32)])
        norm = [("x_in", [P, 3, D]), ("xn", [P, 2, D]), ("arow", [P, D]), ("srow", [P, D]), ("ngrow", [P, D])]
        overlay("region_w", 97,
                [(f"{n}0", shape, F32) for n, shape in norm]
                + [("ada_b", [P, 3, ADA, 512], F32)],
                [40] + [(f"{n}2", shape, F32) for n, shape in norm],
                [("r_q", [P, 2, S], F32), ("r_k", [P, 2, S], F32), ("r_g", [P, NT, 512], F32),
                 ("r_v", [P, NT, 512], F32), ("r_ohi", [P, 4, 512], F32R), ("r_olo", [P, 4, 512], F32R),
                 ("r_tmp", [P, 512], F32), ("r_decay", [P, NT * P], F32), ("r_s", [P, 2, S], F32),
                 ("r_gn", [P, 512], F32), ("r_x", [P, 4, 512], F32),
                 1, ("cos", [P, S], F32), ("sin", [P, S], F32)],
                [48, ("ada_c", [P, ADA, 512], F32), 14, ("acc", [P, 3, 512], F32)],
                [4, ("a_q", [P, GH, S], F32), 4, ("a_k", [P, GH, S], F32), ("a_v", [P, NT, 512], F32),
                 ("a_g", [P, GH, S], F32), ("a_bias", [P, 2, BANDW], F32), ("a_p", [P, 3, BANDW], F32),
                 ("a_pT", [P, 2, BANDW], F32), ("a_o", [P, 2, 512], F32)],
                [("a_ohi", [P, GH, S], F32R), 4, ("a_olo", [P, GH, S], F32R),
                 41, ("a_x", [P, 4, 512], F32), 7, ("a_sq", [P, S], F32)],
                [("l_lat", [P, NT, LATW], F32), ("l_u", [P, 4, PADW], F32), ("l_gp", [P, 4, S], F32),
                 ("l_sum", [P, 2, PADW], F32), ("l_ga", [P, 2, 512], F32), ("l_y", [P, 2, 512], F32),
                 ("l_pw", [P, 4, P], F32), ("l_edge", [P, 4, 2, 8], F32), ("l_e8", [P, 2, 8], F32)],
                [("l_q", [P, NT, LH * LQK], F32), ("l_k", [P, NT, LH * LQK], F32),
                 ("l_v", [P, NT, LH * LV], F32), ("l_tmp", [P, 2, S], F32),
                 ("l_qlhi", [P, 2, S], F32R), ("l_qllo", [P, 2, S], F32R), ("l_klhi", [P, S], F32R),
                 ("l_kllo", [P, S], F32R), ("cos2", [P, NT, HR], F32), ("sin2", [P, NT, HR], F32)],
                [("l_q_spare", [P, NT, LH * LQK], F32R), ("l_k_spare", [P, NT, LH * LQK], F32R),
                 16, ("l_qT", [P, S], F32R), ("l_kT", [P, S], F32R), ("l_p", [P, 3, S], F32),
                 ("l_pT", [P, 2, S], F32), ("l_sg", [P, 512], F32), ("l_o", [P, 512], F32)],
                [64, ("l_x", [P, 4, 512], F32), ("l_t", [P, 512], F32)])

        ada_a, ada_b, h_hi, h_lo = (b[n] for n in ("ada_a", "ada_b", "h_hi", "h_lo"))
        x_in, xn, arow, srow, ngrow = ([b[f"{n}{l}"] for l in (0, 0, 2)] for n, _ in norm)
        (r_q, r_k, r_v, r_g, r_ohi, r_olo, r_tmp, r_decay, r_s, r_gn, r_x, cos, sin, ada_c, acc) = (
            b[n] for n in ("r_q", "r_k", "r_v", "r_g", "r_ohi", "r_olo", "r_tmp", "r_decay", "r_s",
                           "r_gn", "r_x", "cos", "sin", "ada_c", "acc"))
        (a_q, a_k, a_v, a_g, a_bias, a_p, a_pT, a_o, a_ohi, a_olo, a_x, a_sq) = (
            b[n] for n in ("a_q", "a_k", "a_v", "a_g", "a_bias", "a_p", "a_pT", "a_o",
                           "a_ohi", "a_olo", "a_x", "a_sq"))

        (l_lat, l_u, l_gp, l_sum, l_ga, l_y, l_pw, l_edge, l_e8, l_q, l_k, l_v, l_tmp, l_qlhi, l_qllo,
         l_klhi, l_kllo, cos2, sin2, l_qT, l_kT, l_p, l_pT, l_sg, l_o, l_x, l_t) = (
            b[n] for n in ("l_lat", "l_u", "l_gp", "l_sum", "l_ga", "l_y", "l_pw", "l_edge", "l_e8", "l_q",
                           "l_k", "l_v", "l_tmp", "l_qlhi", "l_qllo", "l_klhi", "l_kllo", "cos2", "sin2",
                           "l_qT", "l_kT", "l_p", "l_pT", "l_sg", "l_o", "l_x", "l_t"))

        w_landed = [sem(f"w_landed{n}") for n in range(STAGE)]
        w_rounded = sem("w_rounded")
        w_split = sem("w_split")
        w_used = sem("w_used")
        const_in = sem("const_in")
        ada_in = [sem(f"ada_in{n}") for n in range(PIECES)]
        ada_first = [sem(f"ada_first{n}") for n in range(2)]
        c_ready = sem("c_ready")
        dve_init = sem("dve_init")
        mod_done = sem("mod_done")
        mod_copied = sem("mod_copied")
        mod_stored = sem("mod_stored")
        pos_in = sem("pos_in")
        res_copied = sem("res_copied")
        rope_chain = sem("rope_chain")
        rope_reduced = sem("rope_reduced")
        rope_tables = sem("rope_tables")
        n_rows = sem("n_rows")
        n_arow = sem("n_arow")
        n_x = [sem(f"n_x{n}") for n in range(3)]
        n_gate = sem("n_gate")
        n_sq = sem("n_sq")
        n_root = sem("n_root")
        n_rr = sem("n_rr")
        n_mul = sem("n_mul")
        n_xn = sem("n_xn")
        n_turned = sem("n_turned")
        n_hi = sem("n_hi")
        n_lo = sem("n_lo")
        dve_r = sem("dve_r")

        bank_done = {l: sem(f"bank_done{l}") for l in "ram"}
        bank_free = {l: sem(f"bank_free{l}") for l in "ram"}
        first_free = sem("first_free")
        out_done = {l: sem(f"out_done{l}") for l in "ram"}
        out_free = {l: sem(f"out_free{l}") for l in "ram"}
        out_ready = {l: sem(f"out_ready{l}") for l in "ram"}
        res_in = {l: [sem(f"res_in{l}{n}") for n in range(4)] for l in "ram"}
        res_out = {l: [sem(f"res_out{l}{n}") for n in range(4)] for l in "ram"}

        r_rope = sem("r_rope")
        r_gready = sem("r_gready")
        r_consts = sem("r_consts")
        m_in = sem("m_in")
        m_acc = sem("m_acc")
        m_red = sem("m_red")
        m_row = sem("m_row")
        m_st = sem("m_st")
        r_sdone = sem("r_sdone")
        r_sready = sem("r_sready")
        r_odone = sem("r_odone")
        r_sq = sem("r_sq")
        r_root = sem("r_root")
        r_rinv = sem("r_rinv")
        r_gated = sem("r_gated")
        r_turned = sem("r_turned")
        r_hi = sem("r_hi")
        r_lo = sem("r_lo")

        a_sums = sem("a_sums")
        a_roots = sem("a_roots")
        a_normed = sem("a_normed")
        a_biasin = [sem(f"a_biasin{n}") for n in range(2)]
        a_biasok = sem("a_biasok")
        a_sdone = sem("a_sdone")
        a_max = sem("a_max")
        a_neg = sem("a_neg")
        a_exp = sem("a_exp")
        a_rinv = sem("a_rinv")
        a_prob = sem("a_prob")
        a_pdone = sem("a_pdone")
        a_pevac = sem("a_pevac")
        a_odone = sem("a_odone")
        a_gated = sem("a_gated")
        a_hi = sem("a_hi")
        a_lo = sem("a_lo")
        dve_a = sem("dve_a")

        l_consts = sem("l_consts")
        l_chain = sem("l_chain")
        l_pads = sem("l_pads")
        l_sums = sem("l_sums")
        l_roots = sem("l_roots")
        l_latok = sem("l_latok")
        l_gastored = [sem(f"l_gastored{n}") for n in range(2)]
        l_diff = sem("l_diff")
        l_ydone = sem("l_ydone")
        l_yready = sem("l_yready")
        l_yhi = sem("l_yhi")
        l_ylo = sem("l_ylo")
        l_lturned = sem("l_lturned")
        l_lhi = sem("l_lhi")
        l_llo = sem("l_llo")
        l_rcopied = sem("l_rcopied")
        l_updone = sem("l_updone")
        l_upfree = sem("l_upfree")
        l_sq = sem("l_sq")
        l_rr = sem("l_rr")
        l_qdone = sem("l_qdone")
        l_kdone = sem("l_kdone")
        l_kchain = sem("l_kchain")
        l_sdone = sem("l_sdone")
        l_max = sem("l_max")
        l_neg = sem("l_neg")
        l_exp = sem("l_exp")
        l_rinv = sem("l_rinv")
        l_prob = sem("l_prob")
        l_headhi = sem("l_headhi")
        l_pdone = sem("l_pdone")
        l_pevac = sem("l_pevac")
        l_odone = sem("l_odone")
        l_sgin = sem("l_sgin")
        l_gated = sem("l_gated")
        l_hi = sem("l_hi")
        l_lo = sem("l_lo")

        def unit_of(l, u):
            return (4 * (u // 8) + u % 4, (u // 4) % 2) if l == "r" else (u % 8, u // 8)

        qk_tables = b["qk_tables"][:, :].rearrange("p (s e c m n) -> p s e c m n", s=2, e=2, c=2, m=NT)
        squares = [b["squares"][:, n, 0:LH * LQK] for n in range(2)]
        k_scratch = b["k_scratch"]

        qk_stats = st[:, 0:2 * NT * LH].rearrange("p (s m h) -> p s m h", s=2, m=NT)

        DVE_SCALED = 4

        def scale_keys(engine, m):
            x = l_k[:, m].rearrange("p (h n) -> p h n", h=LH)
            return engine.tensor_tensor(x, x, qk_stats[:, 1, m].unsqueeze(2).to_broadcast([P, LH, LQK]), ALU.mult)

        def up_bank(u):
            return 2 * ((u + 3) % 4)

        def l_turned(h, k, low):
            block = {(0, 1): 5, (1, 0): 6, (1, 1): 7, (3, 1): 7, (5, 1): 7}.get((h, low))
            if block is not None:
                return (h_lo if k else h_hi)[:, block].rearrange("p (m n) -> p m n", m=NT)
            if h % 2 == 0 and not low:
                return (l_kT if k else l_qT)[:, :].rearrange("p (m n) -> p m n", m=NT)
            c = 0 if h % 2 == 0 else 2 if low else 1
            return b["l_k_spare" if k else "l_q_spare"][:, :, c * P:(c + 1) * P]

        def l_head_bank(n):
            bank = 6 if n == 1 else 4
            return psf[0:LQK, bank * 512:bank * 512 + S].rearrange("p (m n) -> p m n", m=NT)

        def rope_parts(src, m):
            x = src[:, m].rearrange("p (h n) -> p h n", h=LH)
            return x[:, :, LNOPE:LNOPE + HR], x[:, :, LNOPE + HR:]

        TURN_AT = {GH: (2, 4), LH: (1, 3)}

        def head_unit(h, k, heads=GH):
            return k if h == 0 else (NT + 2) * (h - 1) + 2 + TURN_AT[heads][k] + k + 1

        ORDER = (0, 4, 1, 5, 2, 6, 3, 7)

        def tile_of(e):
            return e // NT, ORDER[e % NT]

        def prob_unit(e, heads=GH):
            h, i = divmod(e, NT)
            return (NT + 2) * h + 2 + i + (sum(i > at for at in TURN_AT[heads]) if h + 1 < heads else 0)

        block = ctx.enter_context(nc.Block())

        @block.sync
        def _(sp):
            for n in range(PIECES):
                buf = ada_a[:, n] if n < 3 else ada_b[:, n - 3]
                if n == 0:
                    for c, landed in enumerate((*ada_first, ada_in[0])):
                        third = slice(c * ADA // 3, (c + 1) * ADA // 3)
                        sp.dma_start(buf[:, third], t["ada"][n][:, third]).then_inc(landed, 16)
                else:
                    sp.dma_start(buf, t["ada"][n]).then_inc(ada_in[n], 16)
                if 0 < n <= STAGE:
                    sp.dma_start(stage[:, n - 1], t["w"][n - 1]).then_inc(w_landed[n - 1], 16)
            with sp.Fori(1, SLOTS // STAGE) as i:
                for n in range(STAGE):
                    sp.wait_ge(w_split, i * STAGE + (n + 1 - STAGE))
                    sp.dma_start(stage[:, n], t["w"][bass.ds(i * STAGE + n, 1)].rearrange(
                        "a p n -> (a p) n")).then_inc(w_landed[n], 16)

        @block.gpsimd
        def _(pool):
            pool.wait_ge(dve_init, 2)
            def stream(first, count):
                with pool.Fori(first // RING, (first + count) // RING) as i:
                    for n in range(RING):
                        pool.wait_ge(w_landed[n % STAGE], i * (16 * RING // STAGE) + 16 * (n // STAGE + 1))
                        pool.wait_ge(w_used, i * RING + n + 1)
                        pool.tensor_tensor(w_hi[:, n], stage[:, n % STAGE],
                                           ones[:, 0:1].to_broadcast([P, 512]), ALU.mult).then_inc(w_rounded, 1)
                        pool.wait_ge(w_rounded, i * RING + n + 1)
                        pool.tensor_tensor(w_lo[:, n], stage[:, n % STAGE], w_hi[:, n].bitcast(F32),
                                           ALU.subtract).then_inc(w_split, 1)

            before_out = MIX0 + 5 * RING
            stream(0, before_out)
            for m in range(NT):
                def chained(ins, n):
                    ins.then_inc(l_kchain, 1)
                    pool.wait_ge(l_kchain, 4 * m + n)

                pool.wait_ge(l_rr, m + 1)
                if m >= DVE_SCALED:
                    chained(scale_keys(pool, m), 1)
                else:
                    pool.sem_inc(l_kchain, 1)
                x1, x2 = rope_parts(l_k, m)
                (cos1, sin1), (cos2_, sin2_) = (
                    [qk_tables[:, 1, e, c, m].unsqueeze(1).to_broadcast([P, LH, HR]) for c in range(2)]
                    for e in range(2))
                pool.tensor_tensor(k_scratch[:, 0], x1, sin1, ALU.mult)
                chained(pool.tensor_tensor(k_scratch[:, 1], x2, sin2_, ALU.mult), 2)
                pool.tensor_tensor(x1, x1, cos1, ALU.mult)
                chained(pool.tensor_tensor(x2, x2, cos2_, ALU.mult), 3)
                pool.tensor_tensor(x1, x1, k_scratch[:, 1], ALU.subtract)
                chained(pool.tensor_tensor(x2, x2, k_scratch[:, 0], ALU.add), 4)
            pool.sem_inc(l_kdone, 1)
            stream(before_out, SLOTS - before_out)

        @block.tensor
        def _(pe):
            def product(out, a_hi_, a_lo_, b_hi_, b_lo_, first, last):
                pe.matmul(out, a_hi_, b_hi_, start=first, stop=False)
                pe.matmul(out, a_hi_, b_lo_, start=False, stop=False)
                return pe.matmul(out, a_lo_, b_hi_, start=False, stop=last)

            def token_tile(m, slot0, l, wait_bank, width=512):
                wait_bank(m)
                for k in range(KD):
                    if m == 0:
                        pe.wait_ge(w_split, slot0 + (k + 1))
                    mm = product(ps[:, m % 4, 0:width], h_hi[:, k, m * P:(m + 1) * P],
                                 h_lo[:, k, m * P:(m + 1) * P], w_hi[:, k, 0:width], w_lo[:, k, 0:width],
                                 k == 0, k == KD - 1)
                    if m == NT - 1:
                        mm.then_inc(w_used, 1)
                    elif k == KD - 1:
                        mm.then_inc(bank_done[l], 1)

            def tokens(slot0, l, wait_bank):
                for k in range(KD):
                    pe.wait_ge(w_split, slot0 + (k + 1))
                    for m in range(NT):
                        if k == 0:
                            wait_bank(m)
                        mm = product(ps[:, m], h_hi[:, k, m * P:(m + 1) * P],
                                     h_lo[:, k, m * P:(m + 1) * P], w_hi[:, k], w_lo[:, k],
                                     k == 0, k == KD - 1)
                        if m == NT - 1:
                            mm.then_inc(w_used, 1)
                        elif k == KD - 1:
                            mm.then_inc(bank_done[l], 1)

            def features(slot0, l, wait_bank):
                for k in range(KD):
                    pe.wait_ge(w_split, slot0 + (k + 1))
                    for m in range(4):
                        for a in range(2):
                            if k == 0:
                                wait_bank(2 * m + a)
                            mm = product(ps[:, 2 * m + a], w_hi[:, k, m * P:(m + 1) * P],
                                         w_lo[:, k, m * P:(m + 1) * P], h_hi[:, k, a * 512:(a + 1) * 512],
                                         h_lo[:, k, a * 512:(a + 1) * 512], k == 0, k == KD - 1)
                            if 2 * m + a == 7:
                                mm.then_inc(w_used, 1)
                            elif k == KD - 1:
                                mm.then_inc(bank_done[l], 1)

            def in_halves(slot0, l, one, wait_bank, meanwhile):
                for n0 in (0, 4):
                    for k in range(KD):
                        if n0:
                            meanwhile(k)
                        else:
                            pe.wait_ge(w_split, slot0 + (k + 1))
                        for n in range(n0, n0 + 4):
                            if k == 0:
                                wait_bank(n)
                            mm = one(k, n)
                            if n == 7:
                                mm.then_inc(w_used, 1)
                            elif k == KD - 1:
                                mm.then_inc(bank_done[l], 1)

            def token_bank(k, m):
                return product(ps[:, m], h_hi[:, k, m * P:(m + 1) * P], h_lo[:, k, m * P:(m + 1) * P],
                               w_hi[:, k], w_lo[:, k], k == 0, k == KD - 1)

            def feature_bank(k, n):
                cols, half = slice(n // 2 * P, n // 2 * P + P), slice((n % 2) * 512, (n % 2 + 1) * 512)
                return product(ps[:, n], w_hi[:, k, cols], w_lo[:, k, cols], h_hi[:, k, half], h_lo[:, k, half],
                               k == 0, k == KD - 1)

            def out_unit(l, u, o_hi, o_lo, tok, wait_free):
                wait_free(u)
                first_half = 4 * unit_of(l, u)[1]
                for k in range(4):
                    mm = product(ps[:, u % 4], o_hi[:, k, tok], o_lo[:, k, tok], w_hi[:, first_half + k],
                                 w_lo[:, first_half + k], k == 0, k == 3)
                    if k == 0 and u == (12 if l == "r" else 8):
                        mm.then_inc(w_used, 4)
                mm.then_inc(w_used, 4) if u == 15 else mm.then_inc(out_done[l], 1)

            def turn_norm(l, m):
                pe.wait_ge(n_xn, l * NT + m + 1)
                if l or m >= 2:
                    pe.wait_ge(n_lo, l * NT + m - 1)
                for k in range(KD):
                    tr = pe.transpose(psf[:, (4 + 2 * (m % 2)) * 512 + k * P:][:, 0:P],
                                      xn[l][:, m % 2, k * P:(k + 1) * P], ident[:, :])
                tr.then_inc(n_turned, 1)

            def norm_and_first(l, slot0, loop, width=512):
                turn_norm(l, 0)
                for m in range(NT):
                    if m + 1 < NT:
                        turn_norm(l, m + 1)
                    pe.wait_ge(n_lo, l * NT + m + 1)
                    if l == 0 and m == 2:
                        pe.wait_ge(mod_copied, PIECES)
                    token_tile(m, slot0, loop, lambda m: m >= 4 and pe.wait_ge(first_free, l * 4 + m - 3),
                               width)

            pe.sem_inc(w_used, RING)
            for credited in (out_free["r"], out_free["a"], out_ready["r"], out_ready["a"], r_lo, r_sq, a_max,
                             a_lo, *res_out["r"], *res_out["a"]):
                pe.sem_inc(credited, FREE)
            pe.wait_ge(c_ready, 1)
            pe.wait_ge(dve_init, 2)
            for n in range(PIECES):
                if n:
                    pe.wait_ge(ada_in[n], 16)
                if n >= 4:
                    pe.wait_ge(mod_copied, n - 1)
                buf, bank = ada_a[:, n] if n < 3 else ada_b[:, n - 3], n if n < 4 else n - 2
                for k in range(KD):
                    if n == 0 and k % 3 == 0:
                        pe.wait_ge((*ada_first, ada_in[0])[k // 3], 16)
                    pe.matmul(ps[0:1, bank], ccol[:, 0, k:k + 1], buf[:, k], start=(k == 0), stop=False)
                pe.matmul(ps[0:1, bank], ones[:, 0:1], buf[:, KD], start=False, stop=True).then_inc(mod_done, 1)
            pe.wait_ge(const_in, 16 * 3)
            norm_and_first(0, 0, "r")

            def retention(h, last):
                w0, f0 = h * RET_SLOTS, h * (3 * NT)
                features(w0 + 8, "r", lambda n: pe.wait_ge(bank_free["r"], f0 + (n + 1)))
                def scores(i):
                    if i >= 2:
                        pe.wait_ge(r_sready, h * NT + (i - 1))
                    if i == 4:
                        pe.wait_ge(out_free["r"], h * 16 + 8 + FREE)
                    for j in range(i + 1):
                        for k in range(2):
                            mm = pe.matmul(psf[:, (i % 2) * 1024 + j * P:][:, 0:P], r_k[:, k, j * P:(j + 1) * P],
                                           r_q[:, k, i * P:(i + 1) * P], start=(k == 0), stop=(k == 1))
                    mm.then_inc(r_sdone, 1)

                def values(i):
                    pe.wait_ge(r_sready, h * NT + (i + 1))
                    if i >= 2:
                        pe.wait_ge(r_gated, h * NT + (i - 1))
                    for j in range(i + 1):
                        mm = pe.matmul(ps[:, 4 + i % 2], r_s[:, i % 2, j * P:(j + 1) * P], r_v[:, j],
                                       start=(j == 0), stop=(j == i))
                    mm.then_inc(r_odone, 1)

                def turn(i):
                    pe.wait_ge(r_gated, h * NT + (i + 1))
                    if i:
                        pe.wait_ge(r_lo, h * NT + i + FREE)
                    for e in range(4):
                        tr = pe.transpose(ps[:, 6, e * P:(e + 1) * P], r_g[:, i, e * P:(e + 1) * P], ident[:, :])
                    tr.then_inc(r_turned, 1)

                def first_scores(k):
                    if k == 6:
                        pe.wait_ge(bank_free["r"], f0 + 20)
                        pe.wait_ge(r_rope, h + 1)
                        scores(0)
                        scores(1)

                in_halves(w0 + 16, "r", token_bank, lambda n: pe.wait_ge(bank_free["r"], f0 + (n + 9)),
                          first_scores)
                pe.wait_ge(bank_free["r"], f0 + 24)
                for a in range(2):
                    if a:
                        scores(4)
                    else:
                        pe.wait_ge(m_acc, h * 3 + 3)
                        for n in range(3):
                            pe.matmul(ps[0:1, 5 + n], ones[:, 0:1], acc[:, n], start=True,
                                      stop=True).then_inc(m_red, 1)
                        pe.wait_ge(m_row, h * 3 + 3)
                    for i in range(4 * a, 4 * a + 4):
                        if i % 4 < 3 and i > 0:
                            scores(i + 1)
                        values(i)
                        if i % 4:
                            turn(i - 1)
                    if a == 0:
                        pe.wait_ge(w_split, w0 + RET_SLOTS)
                    for u in range(8 * a, 8 * a + 8):
                        if u % 8 == 1:
                            turn(4 * a + 3)
                        if u % 8 < 4:
                            pe.wait_ge(r_lo, h * NT + (4 * a + u % 8 + 1) + FREE)
                        m = unit_of("r", u)[0] % 4
                        out_unit("r", u, r_ohi, r_olo, slice(m * P, (m + 1) * P),
                                 lambda u: u % 8 >= 4 and pe.wait_ge(out_free["r"], h * 16 + (u - 3) + FREE))
                if not last:
                    tokens(w0 + RET_SLOTS, "r", lambda m: m < 4 and pe.wait_ge(
                        out_free["r"], h * 16 + (13 + m) + FREE))

            with pe.Fori(0, RET_GROUPS - 1) as h:
                retention(h, False)
            retention(RET_GROUPS - 1, True)
            pe.wait_ge(out_free["r"], RET_GROUPS * 16 + FREE)
            norm_and_first(1, ATT0, "a")

            def attention(g, last):
                w0, f0 = g * ATT_SLOTS + ATT0, g * (4 * NT)
                tokens(w0 + 8, "a", lambda n: pe.wait_ge(bank_free["a"], f0 + (n + 1)))
                tokens(w0 + 16, "a", lambda n: pe.wait_ge(bank_free["a"], f0 + (n + 9)))
                e0, t0 = g * (GH * NT), g * (GH * (NT + 2))

                def turn_head(h, k):
                    n = head_unit(h, k)
                    if n > 1:
                        pe.wait_ge(a_pevac, t0 + n)
                    for m in range(NT):
                        tr = pe.transpose(psf[:, (2 * n if n < 2 else 4) * 512 + m * P:][:, 0:P],
                                          (a_k if k else a_q)[:, h, m * P:(m + 1) * P], ident[:, :])
                    tr.then_inc(a_pdone, 1)

                def scores(e):
                    h, i = tile_of(e)
                    if e % NT == 0:
                        pe.wait_ge(a_pevac, t0 + (head_unit(h, 1) + 1))
                    if e >= 2:
                        pe.wait_ge(a_max, e0 + (e - 1) + FREE)
                    lo = max(0, i - LEFT) * P
                    width = (i + 1) * P - lo
                    base = (e % 2) * 1024
                    for c in range(0, width, 512):
                        w = min(512, width - c)
                        mm = pe.matmul(psf[:, base + c:base + c + w], a_q[:, h, i * P:(i + 1) * P],
                                       a_k[:, h, lo + c:lo + c + w], start=True, stop=True)
                    mm.then_inc(a_sdone, 1)

                def turn(e):
                    pe.wait_ge(a_prob, e0 + (e + 1))
                    pe.wait_ge(a_pevac, t0 + prob_unit(e))
                    for n in range(min(tile_of(e)[1], LEFT) + 1):
                        tr = pe.transpose(psf[:, 4 * 512 + n * P:][:, 0:P],
                                          a_p[:, e % 3, n * P:(n + 1) * P], ident[:, :])
                    tr.then_inc(a_pdone, 1)

                def values(e):
                    h, i = tile_of(e)
                    pe.wait_ge(a_pevac, t0 + (prob_unit(e) + 1))
                    if h and i % 4 == 0:
                        pe.wait_ge(a_gated, g * (2 * GH) + (2 * h - 1 + i // 4))
                    n = min(i, LEFT) + 1
                    for c in range(n):
                        j = i + 1 - n + c
                        mm = pe.matmul(ps[:, 6 + i // 4, (i % 4) * P:(i % 4 + 1) * P],
                                       a_v[:, j, h * P:(h + 1) * P], a_pT[:, e % 2, c * P:(c + 1) * P],
                                       start=(c == 0), stop=(c == n - 1))
                    mm.then_inc(a_odone, 1)

                def first_scores(k):
                    if k == 2:
                        pe.wait_ge(bank_free["a"], f0 + 28)
                        pe.wait_ge(a_normed, g * 2 + 2)
                        turn_head(0, 0)
                        turn_head(0, 1)
                    if k == 6:
                        scores(0)
                        scores(1)

                in_halves(w0 + 24, "a", feature_bank, lambda n: pe.wait_ge(bank_free["a"], f0 + (n + 17)),
                          first_scores)
                pe.wait_ge(bank_free["a"], f0 + 32)
                for e in range(GH * NT):
                    h, i = divmod(e, NT)
                    if e + 2 < GH * NT:
                        scores(e + 2)
                    if h + 1 < GH and i - 1 in TURN_AT[GH]:
                        values(e - 1)
                        turn(e)
                    else:
                        turn(e)
                        if e:
                            values(e - 1)
                    if h + 1 < GH and i in TURN_AT[GH]:
                        turn_head(h + 1, TURN_AT[GH].index(i))
                values(GH * NT - 1)
                pe.wait_ge(w_split, w0 + ATT_SLOTS)
                for u in range(16):
                    m = unit_of("a", u)[0]
                    if u in (0, 4):
                        pe.wait_ge(a_lo, g * (2 * GH) + (2 * GH - 1 + u // 4) + FREE)
                    out_unit("a", u, a_ohi, a_olo, slice(m * P, (m + 1) * P),
                             lambda u: u >= 4 and pe.wait_ge(out_free["a"], g * 16 + (u - 3) + FREE))
                if not last:
                    tokens(w0 + ATT_SLOTS, "a", lambda m: m < 4 and pe.wait_ge(
                        out_free["a"], g * 16 + (13 + m) + FREE))

            with pe.Fori(0, ATT_GROUPS - 1) as g:
                attention(g, False)
            attention(ATT_GROUPS - 1, True)
            pe.wait_ge(out_free["a"], ATT_GROUPS * 16 + FREE)

            norm_and_first(2, MIX0, "m", LATW)
            features(MIX0 + 8, "m", lambda n: pe.wait_ge(bank_free["m"], n + 1))
            features(MIX0 + 16, "m", lambda n: pe.wait_ge(bank_free["m"], n + 9))
            features(MIX0 + 24, "m", lambda n: pe.wait_ge(bank_free["m"], n + 17))
            pe.wait_ge(l_consts, 16 * 6)
            for n in range(4):
                pe.wait_ge(l_diff, n + 1)
                for a in range(2):
                    pe.wait_ge(bank_free["m"], 24 + 2 * n + a + 1)
                    pe.matmul(ps[:, 2 * n + a], l_pw[:, n], l_u[:, n, PAD + 512 * a:PAD + 512 * a + 512],
                              start=True, stop=True).then_inc(l_ydone, 1)
            pe.wait_ge(l_latok, 2)
            for n in range(3):
                pe.wait_ge(l_ylo, 2 * n + 2)
                for m in range(NT):
                    c = (n + 2) % 3
                    tr = pe.transpose(psf[:, n * 1024 + m * P:][:, 0:P], l_lat[:, m, c * P:(c + 1) * P],
                                      ident[:, :])
                tr.then_inc(l_lturned, 1)
            pe.wait_ge(l_ylo, 8)
            pe.wait_ge(w_split, MIX0 + 40)
            for u in range(2 * NT):
                if u < 4:
                    pe.wait_ge(l_llo, max(1, u))
                else:
                    pe.wait_ge(l_upfree, u - 3)
                bank, tok = up_bank(u), slice((u % NT) * P, (u % NT + 1) * P)
                for c in range(2):
                    if u < NT:
                        mm = product(ps[:, bank + c], l_klhi[:, tok], l_kllo[:, tok], w_hi[:, 4 + c],
                                     w_lo[:, 4 + c], True, True)
                    else:
                        for k in range(2):
                            mm = product(ps[:, bank + c, 0:384], l_qlhi[:, k, tok], l_qllo[:, k, tok],
                                         w_hi[:, 2 * c + k, 0:384], w_lo[:, 2 * c + k, 0:384], k == 0, k == 1)
                mm.then_inc(w_used, 8) if u == 2 * NT - 1 else mm.then_inc(l_updone, 1)
            pe.wait_ge(l_upfree, 2 * NT)
            pe.wait_ge(l_qdone, NT)
            pe.wait_ge(l_kdone, 1)

            def l_turn_head(h, k):
                n = head_unit(h, k, LH)
                if n > 1:
                    pe.wait_ge(l_pevac, n)
                for m in range(NT):
                    tr = pe.transpose(psf[0:LQK, (6 if n == 1 else 4) * 512 + m * P:][:, 0:P],
                                      (l_k if k else l_q)[:, m, h * LQK:(h + 1) * LQK], ident[:, :])
                tr.then_inc(l_pdone, 1)

            def l_scores(e):
                h, i = divmod(e, NT)
                if i == 0:
                    pe.wait_ge(l_pevac, head_unit(h, 1, LH) + 1)
                if e >= 2:
                    pe.wait_ge(l_exp, e - 1)
                (q_hi, q_lo), (k_hi, k_lo) = ([l_turned(h, k, low) for low in range(2)] for k in range(2))
                for c in range(2):
                    keys = slice(4 * c, 4 * c + 4)
                    mm = product(ps[:, 2 * (e % 2) + c].rearrange("p (m n) -> p m n", m=4), q_hi[0:LQK, i],
                                 q_lo[0:LQK, i], k_hi[0:LQK, keys], k_lo[0:LQK, keys], True, True)
                mm.then_inc(l_sdone, 1)

            def l_turn(e):
                pe.wait_ge(l_prob, e + 1)
                pe.wait_ge(l_pevac, prob_unit(e, LH))
                for n in range(NT):
                    tr = pe.transpose(psf[:, 4 * 512 + n * P:][:, 0:P], l_p[:, e % 3, n * P:(n + 1) * P],
                                      ident[:, :])
                tr.then_inc(l_pdone, 1)

            def l_values(e):
                h, i = divmod(e, NT)
                rows = slice(LV * (h % 2), LV * (h % 2) + LV)
                pe.wait_ge(l_pevac, prob_unit(e, LH) + 1)
                if h and i % 4 == 0:
                    pe.wait_ge(l_gated, 2 * h - 1 + i // 4)
                for n in range(NT):
                    mm = pe.matmul(ps[rows, 6 + i // 4, (i % 4) * P:(i % 4 + 1) * P],
                                   l_v[:, n, h * LV:(h + 1) * LV], l_pT[:, e % 2, n * P:(n + 1) * P],
                                   start=(n == 0), stop=(n == NT - 1))
                mm.then_inc(l_odone, 1)

            l_turn_head(0, 0)
            l_turn_head(0, 1)
            l_scores(0)
            l_scores(1)
            for e in range(LH * NT):
                h, i = divmod(e, NT)
                if e + 2 < LH * NT:
                    l_scores(e + 2)
                if h + 1 < LH and i - 1 in TURN_AT[LH]:
                    l_values(e - 1)
                    l_turn(e)
                else:
                    l_turn(e)
                    if e:
                        l_values(e - 1)
                if h + 1 < LH and i in TURN_AT[LH]:
                    l_turn_head(h + 1, TURN_AT[LH].index(i))
            l_values(LH * NT - 1)
            pe.wait_ge(l_lo, 2 * LH)
            for a in range(2):
                for m in range(NT):
                    u = 8 * a + m
                    if u >= 4:
                        pe.wait_ge(out_free["m"], u - 3)
                    for k in range(KD):
                        if m == 0:
                            pe.wait_ge(w_split, MIX0 + 40 + 8 * a + k + 1)
                        mm = product(ps[:, u % 4], h_hi[:, k, m * P:(m + 1) * P], h_lo[:, k, m * P:(m + 1) * P],
                                     w_hi[:, k], w_lo[:, k], k == 0, k == KD - 1)
                        if m == NT - 1:
                            mm.then_inc(w_used, 1)
                        elif k == KD - 1:
                            mm.then_inc(out_done["m"], 1)

        @block.scalar
        def _(act):
            def wait_bank(l, slots0, done0, blk, n):
                if n < 7:
                    act.wait_ge(bank_done[l], done0 + (7 * blk + n + 1))
                else:
                    act.wait_ge(w_used, slots0 + (RING + 8 * blk + 8))

            def norm_load(l, m):
                src = t["x"] if l == 0 else t["res"]
                act.dma_start(x_in[l][:, m % 3], src[m * P:(m + 1) * P, :]).then_inc(n_x[m % 3], 16)

            def norm_rows(l):
                act.dma_start(arow[l][:, :], t["mod"][6 * l + 2:6 * l + 4, :].rearrange("a n -> (a n)")
                              .partition_broadcast(P)).then_inc(n_rows, 16)
                act.dma_start(ngrow[l][:, :], t["norm_g"][l].partition_broadcast(P)).then_inc(n_rows, 16)
                act.dma_start(srow[l][:, :], t["mod"][6 * l:6 * l + 2, :].rearrange("a n -> (a n)")
                              .partition_broadcast(P)).then_inc(n_rows, 16)

            def norm_stats(l, m):
                e = l * NT + m
                act.wait_ge(n_x[m % 3], 16 * (l * (3, 3, 2)[m % 3] + m // 3 + 1))
                if e >= 2:
                    act.wait_ge(n_turned, e - 1)
                act.activation(xn[l][:, m % 2], x_in[l][:, m % 3], ACT.Square,
                               accum_out=st[:, m:m + 1]).then_inc(n_sq, 1)
                act.wait_ge(n_sq, e + 1)
                act.activation(st[:, 8 + m:9 + m], st[:, m:m + 1], ACT.Sqrt, scale=1.0 / D,
                               bias=eps[:, 0:1]).then_inc(n_root, 1)

            def copied(ins, l, m):
                ins.then_inc(first_free, 1) if m < 4 else ins.then_inc(bank_free[l], 5 if m == 7 else 1)

            def norm_layer(l, done, first_copy):
                def gate_row():
                    act.dma_start(gate[:, :], t["mod"][6 * l + 4:6 * l + 6, :].rearrange("a n -> (a n)")
                                  .partition_broadcast(P)).then_inc(n_gate, 16)

                if l:
                    gate_row()
                for m in range(NT + 2):
                    if l == 0 and m == 2:
                        act.wait_ge(mod_copied, 6)
                        act.dma_start(t["mod"][4:6, :].rearrange("a n -> (a n)").unsqueeze(0), gate[0:1, :])\
                           .then_inc(mod_stored, 16)
                    if l == 0 and m == 4:
                        act.wait_ge(mod_stored, 48)
                        gate_row()
                    if done <= m < NT:
                        norm_stats(l, m)
                    if 1 <= m <= NT:
                        e = l * NT + m - 1
                        act.wait_ge(n_turned, e + 1)
                        act.activation(h_hi[:, :, (m - 1) * P:m * P],
                                       psf[:, (4 + 2 * ((m - 1) % 2)) * 512:][:, 0:D].rearrange(
                                           "p (k n) -> p k n", k=KD), ACT.Copy).then_inc(n_hi, 1)
                        if m + 2 < NT:
                            act.wait_ge(n_mul, e + 1)
                            norm_load(l, m + 2)
                    if m >= 2:
                        first_copy(m - 2)

            act.dma_start(ident[:, :], t["ident"]).then_inc(const_in, 16)
            act.dma_start(ccol[:, :, :], t["cond"]).then_inc(const_in, 16)
            act.dma_start(gains[:, :], t["gains"]).then_inc(const_in, 16)
            act.dma_start(cos[:, :].bitcast(I32), t["pos"].partition_broadcast(P)).then_inc(pos_in, 16)
            for m in range(3):
                norm_load(0, m)
            act.wait_ge(const_in, 48)
            act.activation(ccol[:, :, :], ccol[:, :, :], ACT.Silu).then_inc(c_ready, 1)
            act.wait_ge(rope_reduced, 1)
            act.activation(sin[:, :], sin[:, :], ACT.Sin).then_inc(rope_tables, 1)
            act.wait_ge(rope_reduced, 2)
            act.activation(cos[:, :], cos[:, :], ACT.Sin).then_inc(rope_tables, 1)
            norm_stats(0, 0)
            for n, row in enumerate((srow[0], arow[0])):
                act.wait_ge(mod_copied, 2 * n + 2)
                act.dma_start(t["mod"][2 * n:2 * n + 2, :].rearrange("a n -> (a n)").unsqueeze(0), row[0:1, :])\
                   .then_inc(mod_stored, 16)
            act.wait_ge(mod_stored, 32)
            norm_rows(0)

            def unit_rows(l, u):
                m, half = unit_of(l, u)
                return t["res"][m * P:(m + 1) * P, half * 512:(half + 1) * 512]

            def residual_load(l, u):
                buf = r_x if l == "r" else a_x
                act.dma_start(buf[:, u % 4], unit_rows(l, u)).then_inc(res_in[l][u % 4], 16)

            def residual_units(l, i, units, meanwhile=None):
                buf = r_x if l == "r" else a_x
                units = list(units)
                for u in units:
                    act.wait_ge(out_ready[l], i * 16 + (u + 1) + FREE)
                    act.dma_start(unit_rows(l, u), buf[:, u % 4]).then_inc(res_out[l][u % 4], 16)
                    if u + 3 in units and u + 3 >= units[0] + 4:
                        v = u + 3
                        act.wait_ge(res_out[l][v % 4], i * 64 + 16 * (v // 4) + FREE)
                        residual_load(l, v)
                    if meanwhile:
                        meanwhile(u)

            def first_loads(l, i, units):
                for v in list(units)[0:4]:
                    act.wait_ge(res_out[l][v % 4], i * 64 + 16 * (v // 4) + FREE)
                    residual_load(l, v)

            def ada_load(n):
                act.dma_start(ada_c[:, :, :], t["ada"][bass.ds(n + PIECES, 1)].rearrange(
                    "a p k n -> (a p) k n")).then_inc(m_in, 16)

            def retention_loads(h):
                act.wait_ge(w_used, h * RET_SLOTS + RING)
                act.wait_ge(r_lo, h * NT + FREE)
                act.wait_ge(out_ready["r"], h * 16 + FREE)
                act.dma_start(r_gn[:, :], t["ret_gn"][bass.ds(h, 1)].rearrange("a n -> (a n)")
                              .partition_broadcast(P)).then_inc(r_consts, 16)
                act.dma_start(r_decay[:, :], t["decay"][bass.ds(h, 1)].rearrange("a p n -> (a p) n"))\
                    .then_inc(r_consts, 16)
                ada_load(h * 3)

            def retention_values(h, m, first=False):
                wait_bank("r", h * RET_SLOTS, h * 21, 0, m)
                return act.activation(r_v[:, m], ps[:, m % 4 if first else m], ACT.Copy)

            def retention(h, last):
                w0, d0 = h * RET_SLOTS, h * 21
                act.wait_ge(m_acc, h * 3 + 1)
                ada_load(h * 3 + 1)
                for n in range(8):
                    wait_bank("r", w0, d0, 1, n)
                    dst = (r_q if n < 4 else r_k)[:, (n // 2) % 2, (n % 2) * 512:(n % 2 + 1) * 512]
                    act.activation(dst, ps[:, n], ACT.Copy).then_inc(bank_free["r"], 1)
                act.wait_ge(m_acc, h * 3 + 2)
                ada_load(h * 3 + 2)
                for m in range(NT):
                    wait_bank("r", w0, d0, 2, m)
                    act.activation(r_g[:, m], ps[:, m], ACT.Silu).then_inc(bank_free["r"], 1)

                def squares(i):
                    act.wait_ge(r_odone, h * NT + (i + 1))
                    act.wait_ge(r_sq, h * NT + i + FREE)
                    act.activation(r_tmp[:, :], ps[:, 4 + i % 2], ACT.Square,
                                   accum_out=st[:, 16 + i:17 + i]).then_inc(r_sq, 1)
                    act.wait_ge(r_sq, h * NT + (i + 1) + FREE)
                    act.activation(st[:, 24 + i:25 + i], st[:, 16 + i:17 + i], ACT.Sqrt, scale=1.0 / 512,
                                   bias=eps[:, 0:1]).then_inc(r_root, 1)

                def high(i):
                    act.wait_ge(r_turned, h * NT + (i + 1))
                    act.activation(r_ohi[:, :, (i % 4) * P:(i % 4 + 1) * P],
                                   ps[:, 6].rearrange("p (e n) -> p e n", e=4), ACT.Copy).then_inc(r_hi, 1)

                for n in range(3):
                    act.wait_ge(m_row, h * 3 + (n + 1))
                    act.dma_start(t["mod"][bass.ds(h * 3 + (n + PIECES), 1)], acc[0:1, n]).then_inc(m_st, 16)
                for a in range(2):
                    for i in range(4 * a, 4 * a + 4):
                        squares(i)
                        if i % 4:
                            high(i - 1)
                        if i % 4 == 2:
                            if a == 0:
                                act.wait_ge(m_st, h * 48 + 48)
                            first_loads("r", h, range(8 * a, 8 * a + 8))
                    high(4 * a + 3)
                    if a and last:
                        norm_rows(1)
                        for m in range(3):
                            norm_load(1, m)
                        residual_units("r", h, range(8, 16), lambda u: u == 12 and norm_stats(1, 0))
                    else:
                        residual_units("r", h, range(8 * a, 8 * a + 8))
                if not last:
                    retention_loads(h + 1)
                    for m in range(NT):
                        retention_values(h + 1, m).then_inc(bank_free["r"], 1)

            norm_layer(0, 1, lambda m: copied(retention_values(0, m, True), "r", m))
            act.dma_start(t["res"], t["x"]).then_inc(res_copied, 16)
            retention_loads(0)
            act.wait_ge(res_copied, 16)
            with act.Fori(0, RET_GROUPS - 1) as h:
                retention(h, False)
            retention(RET_GROUPS - 1, True)
            for n in range(4):
                act.wait_ge(res_out["r"][n], 64 * RET_GROUPS + FREE)

            def bias_load(g, h):
                act.dma_start(a_bias[:, h % 2], t["band"][bass.ds(g * GH + h, 1)].rearrange(
                    "a p n -> (a p) n")).then_inc(a_biasin[h % 2], 16)

            def attention_loads(g):
                act.wait_ge(a_max, g * (GH * NT) + FREE)
                act.wait_ge(a_lo, g * (2 * GH) + FREE)
                act.wait_ge(out_ready["a"], g * 16 + FREE)
                bias_load(g, 0)

            def attention_values(g, m, first=False):
                wait_bank("a", g * ATT_SLOTS + ATT0, g * 28, 0, m)
                return act.activation(a_v[:, m], ps[:, m % 4 if first else m], ACT.Copy)

            def attention(g, last):
                w0, d0 = g * ATT_SLOTS + ATT0, g * 28
                for blk, dst in ((1, a_q), (2, a_k)):
                    for m in range(NT):
                        wait_bank("a", w0, d0, blk, m)
                        act.activation(dst[:, :, m * P:(m + 1) * P],
                                       ps[:, m].rearrange("p (h n) -> p h n", h=GH), ACT.Copy)\
                            .then_inc(bank_free["a"], 1)
                    act.wait_ge(a_sums, g * 2 + blk)
                    c = 32 + 64 * (blk - 1)
                    act.activation(st[:, c + 32:c + 64], st[:, c:c + 32], ACT.Sqrt, scale=1.0 / P,
                                   bias=eps[:, 0:1]).then_inc(a_roots, 1)

                def gate_copied(n):
                    wait_bank("a", w0, d0, 3, n)
                    act.activation(a_g[:, n // 2, (n % 2) * 512:(n % 2 + 1) * 512], ps[:, n],
                                   ACT.Silu).then_inc(bank_free["a"], 1)

                e0, t0 = g * (GH * NT), g * (GH * (NT + 2))
                for n in range(4):
                    act.wait_ge(res_out["a"][n], g * 64 + FREE)

                def head_turned(h, k):
                    n = head_unit(h, k)
                    act.wait_ge(a_pdone, t0 + (n + 1))
                    bank = 2 * n if n < 2 else 4
                    act.activation((a_k if k else a_q)[:, h], psf[:, bank * 512:bank * 512 + S], ACT.Identity,
                                   scale=gains[:, k:k + 1]).then_inc(a_pevac, 1)

                def exps(e):
                    w = min(tile_of(e)[1] + 1, LEFT + 1) * P
                    act.wait_ge(a_neg, e0 + (e + 1))
                    act.activation(a_p[:, e % 3, 0:w], a_p[:, e % 3, 0:w], ACT.Exp,
                                   bias=st[:, 168 + e % 4:169 + e % 4],
                                   accum_out=st[:, 172 + e % 4:173 + e % 4]).then_inc(a_exp, 1)

                def prob_turned(e):
                    w = min(tile_of(e)[1] + 1, LEFT + 1) * P
                    act.wait_ge(a_pdone, t0 + (prob_unit(e) + 1))
                    if e >= 2:
                        act.wait_ge(a_odone, e0 + (e - 1))
                    act.activation(a_pT[:, e % 2, 0:w], psf[:, 4 * 512:4 * 512 + w], ACT.Copy)\
                        .then_inc(a_pevac, 1)

                def high(h, a):
                    act.wait_ge(a_gated, g * (2 * GH) + (2 * h + a + 1))
                    act.activation(a_ohi[:, h, a * 512:(a + 1) * 512], a_o[:, a], ACT.Copy)\
                        .then_inc(a_hi, 1)

                for n in range(4):
                    gate_copied(n)
                head_turned(0, 0)
                head_turned(0, 1)
                exps(0)
                for n in range(4, 8):
                    gate_copied(n)
                for e in range(GH * NT):
                    h, i = divmod(e, NT)
                    if i == 1 and h + 1 < GH:
                        if h:
                            act.wait_ge(a_max, e0 + h * NT + FREE)
                        bias_load(g, h + 1)
                    if e + 1 < GH * NT:
                        exps(e + 1)
                    prob_turned(e)
                    if h + 1 < GH and i in TURN_AT[GH]:
                        head_turned(h + 1, TURN_AT[GH].index(i))
                    if h and i in (1, 2):
                        high(h - 1, i - 1)
                high(GH - 1, 0)
                high(GH - 1, 1)
                first_loads("a", g, range(16))

                def next_norm(u):
                    if 9 <= u <= 11:
                        act.wait_ge(res_out["a"][(u - 1) % 4], g * 64 + 16 * ((u - 1) // 4 + 1) + FREE)
                        norm_load(2, u - 9)
                    if u == 13:
                        norm_stats(2, 0)

                if last:
                    act.wait_ge(a_lo, ATT_GROUPS * 2 * GH + FREE)
                    norm_rows(2)
                    residual_units("a", g, range(16), next_norm)
                else:
                    residual_units("a", g, range(16))
                    attention_loads(g + 1)
                    for m in range(NT):
                        attention_values(g + 1, m).then_inc(bank_free["a"], 1)

            attention_loads(0)
            norm_layer(1, 1, lambda m: copied(attention_values(0, m, True), "a", m))
            with act.Fori(0, ATT_GROUPS - 1) as g:
                attention(g, False)
            attention(ATT_GROUPS - 1, True)
            for n in range(4):
                act.wait_ge(res_out["a"][n], 64 * ATT_GROUPS + FREE)

            def latents(m):
                wait_bank("m", MIX0, 0, 0, m)
                copied(act.activation(l_lat[:, m], ps[:, m % 4, 0:LATW], ACT.Copy), "m", m)

            norm_layer(2, 1, latents)
            act.dma_start(l_pw[:, :, :], t["pool_w"]).then_inc(l_consts, 16)
            act.dma_start(l_edge[:, :, :, :], t["edge"]).then_inc(l_consts, 16)
            act.dma_start(st[:, 184:192].bitcast(I32), t["pos2"]).then_inc(l_consts, 16)
            act.dma_start(cos2[:, :, :], t["inv2"].partition_broadcast(P)).then_inc(l_consts, 16)
            act.dma_start(qk_rows[:, 0], t["g_qnorm"][LNOPE:].partition_broadcast(P)).then_inc(l_consts, 16)
            act.dma_start(qk_rows[:, 1], t["g_knorm"][LNOPE:].partition_broadcast(P)).then_inc(l_consts, 16)
            act.wait_ge(rope_reduced, 4)
            act.activation(sin2[:, :, :], sin2[:, :, :], ACT.Sin).then_inc(rope_tables, 1)
            act.activation(cos2[:, :, :], cos2[:, :, :], ACT.Sin).then_inc(rope_tables, 1)
            act.wait_ge(l_sums, 2)
            act.activation(st[:, 16:24], st[:, 0:8], ACT.Sqrt, scale=1.0 / QLAT, bias=eps[:, 0:1])
            act.activation(st[:, 24:32], st[:, 8:16], ACT.Sqrt, scale=1.0 / KVLAT,
                           bias=eps[:, 0:1]).then_inc(l_roots, 1)
            for n in range(8):
                wait_bank("m", MIX0, 0, 1, n)
                act.activation(l_u[:, n // 2, PAD + 512 * (n % 2):PAD + 512 * (n % 2) + 512], ps[:, n],
                               ACT.Copy).then_inc(bank_free["m"], 1)
            for n in range(8):
                wait_bank("m", MIX0, 0, 2, n)
                act.activation(l_gp[:, n // 2, (n % 2) * 512:(n % 2 + 1) * 512], ps[:, n],
                               ACT.Silu).then_inc(bank_free["m"], 1)
            for n in range(8):
                wait_bank("m", MIX0, 0, 3, n)
                if n >= 2:
                    act.wait_ge(l_gastored[n % 2], 16 * (n // 2))
                act.activation(l_ga[:, n % 2], ps[:, n], ACT.Silu).then_inc(bank_free["m"], 1)
                act.wait_ge(bank_free["m"], 24 + n + 1)
                act.dma_start(t["sg"][(n // 2) * P:(n // 2 + 1) * P, (n % 2) * 512:(n % 2 + 1) * 512],
                              l_ga[:, n % 2]).then_inc(l_gastored[n % 2], 16)
            for n in range(8):
                act.wait_ge(l_yready, n + 1)
                act.activation(h_hi[:, n // 2, (n % 2) * 512:(n % 2 + 1) * 512], l_y[:, n % 2],
                               ACT.Copy).then_inc(l_yhi, 1)
            for n in range(3):
                act.wait_ge(l_lturned, n + 1)
                act.activation(l_qlhi[:, n - 1] if n else l_klhi[:, :], psf[:, n * 1024:(n + 1) * 1024],
                               ACT.Identity, scale=gains[:, 7 + (n + 2) % 3:8 + (n + 2) % 3]).then_inc(l_lhi, 1)

            def roots(u):
                act.wait_ge(l_sums, 2 + u + 1)
                sums = qk_stats[:, u // NT ^ 1, u % NT]
                act.activation(sums, sums, ACT.Sqrt, scale=1.0 / LQK, bias=eps[:, 0:1]).then_inc(l_roots, 1)

            for n in range(2):
                act.wait_ge(l_gastored[n], 64)
            for u in range(2 * NT):
                bank, m = up_bank(u), u % NT
                if u < 2 * NT - 1:
                    act.wait_ge(l_updone, u + 1)
                else:
                    act.wait_ge(w_used, MIX0 + 40 + RING)
                if u < NT:
                    kv = ps[:, bank:bank + 2].rearrange("p c n -> p (c n)").rearrange("p (h n) -> p h n", h=LH)
                    act.activation(l_k[:, m].rearrange("p (h n) -> p h n", h=LH)[:, :, 0:LNOPE],
                                   kv[:, :, 0:LNOPE], ACT.Copy)
                    act.activation(l_v[:, m].rearrange("p (h n) -> p h n", h=LH), kv[:, :, LNOPE:],
                                   ACT.Copy).then_inc(l_upfree, 1)
                else:
                    act.activation(l_q[:, m].rearrange("p (c n) -> p c n", c=2), ps[:, bank:bank + 2, 0:384],
                                   ACT.Copy).then_inc(l_upfree, 1)
                if u == 0:
                    act.wait_ge(l_rcopied, 1)
                act.wait_ge(l_upfree, u + 1)
                if u >= 2:
                    act.wait_ge(l_sums, 2 + u - 1)
                act.activation(squares[u % 2], (l_k if u < NT else l_q)[:, m], ACT.Square).then_inc(l_sq, 1)
                if u:
                    roots(u - 1)
            roots(2 * NT - 1)

            def gate_load(n):
                h, a = n // 2, n % 2
                rows = slice(LV * (h % 2), LV * (h % 2) + LV)
                act.dma_start(l_sg[rows, :], t["sg"][h * LV:(h + 1) * LV, a * 512:(a + 1) * 512])\
                   .then_inc(l_sgin, 16)

            act.wait_ge(l_llo, 3)
            act.wait_ge(w_used, MIX0 + 40 + RING)
            gate_load(0)

            def l_head_turned(h, k):
                n = head_unit(h, k, LH)
                act.wait_ge(l_pdone, n + 1)
                act.activation(l_turned(h, k, 0)[0:LQK], l_head_bank(n), ACT.Identity,
                               scale=gains[0:LQK, 10 + k:11 + k]).then_inc(l_headhi, 1)

            def l_exps(e):
                h, i = divmod(e, NT)
                act.wait_ge(l_neg, e + 1)
                if e >= 3:
                    act.wait_ge(l_pdone, prob_unit(e - 3, LH) + 1)
                act.activation(l_p[:, e % 3], psf[:, (e % 2) * 1024:(e % 2) * 1024 + S], ACT.Exp,
                               scale=qk_stats[:, 0, i, h:h + 1], bias=st[:, 132 + e % 4:133 + e % 4],
                               accum_out=st[:, 136 + e % 4:137 + e % 4]).then_inc(l_exp, 1)

            def l_prob_turned(e):
                act.wait_ge(l_pdone, prob_unit(e, LH) + 1)
                if e >= 2:
                    act.wait_ge(l_odone, e - 1)
                act.activation(l_pT[:, e % 2], psf[:, 4 * 512:4 * 512 + S], ACT.Copy).then_inc(l_pevac, 1)

            def l_high(h, a):
                rows = slice(LV * (h % 2), LV * (h % 2) + LV)
                act.wait_ge(l_gated, 2 * h + a + 1)
                act.activation(h_hi[rows, 4 + h // 2, a * 512:(a + 1) * 512], l_o[rows, :],
                               ACT.Copy).then_inc(l_hi, 1)
                if 2 * h + a + 1 < 2 * LH:
                    gate_load(2 * h + a + 1)

            l_head_turned(0, 0)
            l_head_turned(0, 1)
            l_exps(0)
            for e in range(LH * NT):
                h, i = divmod(e, NT)
                if e + 1 < LH * NT:
                    l_exps(e + 1)
                l_prob_turned(e)
                if h + 1 < LH and i in TURN_AT[LH]:
                    l_head_turned(h + 1, TURN_AT[LH].index(i))
                if h and i == 2:
                    l_high(h - 1, 1)
                if i == 6:
                    l_high(h, 0)
            l_high(LH - 1, 1)
            def unit(u):
                return slice((u % 8) * P, (u % 8 + 1) * P), slice((u // 8) * 512, (u // 8 + 1) * 512)

            for u in range(19):
                if 3 <= u:
                    v = u - 3
                    act.wait_ge(out_ready["m"], v + 1)
                    act.dma_start(t["out"][unit(v)], l_x[:, v % 4]).then_inc(res_out["m"][v % 4], 16)
                if u < 16:
                    if u >= 4:
                        act.wait_ge(res_out["m"][u % 4], 16 * (u // 4))
                    act.dma_start(l_x[:, u % 4], t["res"][unit(u)]).then_inc(res_in["m"][u % 4], 16)
            for n in range(4):
                act.wait_ge(res_out["m"][n], 64)

        @block.vector
        def _(dve):
            links = [0]

            def link(ins, chain, base=0):
                links[0] += 1
                ins.then_inc(chain, 1)
                dve.wait_ge(chain, base + links[0])

            dve.memset(eps[:, :], EPS).then_inc(dve_init, 1)
            dve.memset(ones[:, :], 1.0).then_inc(dve_init, 1)
            dve.wait_ge(dve_init, 2)
            ang, turns = xn[0][:, 0], xn[0][:, 1]
            dve.wait_ge(pos_in, 16)
            dve.wait_ge(const_in, 48)
            link(dve.tensor_copy(ang, cos[:, :].bitcast(I32)), rope_chain)
            link(dve.tensor_scalar(ang, ang, gains[:, 2:3], None, ALU.mult), rope_chain)
            for table, quarter in ((sin, 0.0), (cos, 0.25)):
                link(dve.tensor_scalar(turns, ang, 1.0 / TWO_PI, quarter, ALU.mult, ALU.add), rope_chain)
                link(dve.tensor_scalar(turns, turns, MAGIC, MAGIC, ALU.add, ALU.subtract), rope_chain)
                link(dve.scalar_tensor_tensor(table[:, :], turns, -C1, ang, ALU.mult, ALU.add), rope_chain)
                link(dve.scalar_tensor_tensor(table[:, :], turns, -C2, table[:, :], ALU.mult, ALU.add),
                     rope_chain)
                link(dve.scalar_tensor_tensor(table[:, :], turns, -C3, table[:, :], ALU.mult, ALU.add),
                     rope_chain)
                link(dve.tensor_scalar(table[:, :], table[:, :], quarter * TWO_PI, math.pi, ALU.add, ALU.min),
                     rope_chain)
                dve.tensor_scalar(table[:, :], table[:, :], -math.pi, None, ALU.max).then_inc(rope_reduced, 1)
            link(dve.tensor_scalar(gains[:, 0:1], gains[:, 0:1], P ** -0.5, None, ALU.mult), rope_chain)
            def modulation_row(n):
                row, bank = (srow[0], arow[0], gate)[n // 2], n if n < 4 else n - 2
                dve.wait_ge(mod_done, n + 1)
                dve.tensor_copy(row[0:1, (n % 2) * 512:(n % 2 + 1) * 512], ps[0:1, bank]).then_inc(mod_copied, 1)

            for n in range(4):
                modulation_row(n)

            def norm_layer(l):
                dve.wait_ge(n_rows, 48 * (l + 1))
                dve.scalar_tensor_tensor(arow[l][:, :], arow[l][:, :], 1.0, ngrow[l][:, :], ALU.add,
                                         ALU.mult).then_inc(n_arow, 1)
                dve.wait_ge(n_arow, l + 1)
                for m in range(NT + 1):
                    if m < NT:
                        e = l * NT + m
                        tile = xn[l][:, m % 2]
                        dve.wait_ge(n_root, e + 1)
                        dve.reciprocal(st[:, 8 + m:9 + m], st[:, 8 + m:9 + m]).then_inc(n_rr, 1)
                        dve.wait_ge(n_rr, e + 1)
                        dve.scalar_tensor_tensor(tile, x_in[l][:, m % 3], st[:, 8 + m:9 + m], arow[l][:, :],
                                                 ALU.mult, ALU.mult).then_inc(n_mul, 1)
                        dve.wait_ge(n_mul, e + 1)
                        dve.tensor_tensor(tile, tile, srow[l][:, :], ALU.add).then_inc(n_xn, 1)
                    if l == 0 and m == 0:
                        modulation_row(4)
                        modulation_row(5)
                    if m:
                        e = l * NT + m - 1
                        sl = slice((m - 1) * P, m * P)
                        dve.wait_ge(n_hi, e + 1)
                        dve.tensor_tensor(h_lo[:, :, sl], psf[:, (4 + 2 * ((m - 1) % 2)) * 512:][:, 0:D]
                                          .rearrange("p (k n) -> p k n", k=KD), h_hi[:, :, sl].bitcast(F32),
                                          ALU.subtract).then_inc(n_lo, 1)
                dve.wait_ge(n_gate, 16 * (l + 1))

            norm_layer(0)

            def residual(l, i, units, tmp, chain, base):
                buf = r_x if l == "r" else a_x
                for u in units:
                    half = unit_of(l, u)[1]
                    if u == 15:
                        slots = (RET_SLOTS, 0) if l == "r" else (ATT_SLOTS, ATT0)
                        dve.wait_ge(w_used, i * slots[0] + (slots[0] + slots[1] + RING))
                    else:
                        dve.wait_ge(out_done[l], i * 15 + (u + 1))
                    if u:
                        dve.wait_ge(out_ready[l], i * 16 + u + FREE)
                    dve.tensor_tensor(tmp, ps[:, u % 4], gate[:, half * 512:(half + 1) * 512],
                                      ALU.mult).then_inc(out_free[l], 1)
                    dve.wait_ge(out_free[l], i * 16 + (u + 1) + FREE)
                    dve.wait_ge(res_in[l][u % 4], i * 64 + 16 * (u // 4 + 1))
                    dve.tensor_tensor(buf[:, u % 4], buf[:, u % 4], tmp, ALU.add).then_inc(out_ready[l], 1)

            RL = 1 + 3 * (KD - 1) + 5
            dve.wait_ge(rope_tables, 2)
            with dve.Fori(0, RET_GROUPS) as h:
                links[0] = 0
                base = h * RL

                def modulation(n):
                    dve.wait_ge(m_in, h * 48 + 16 * (n + 1))
                    for k in range(KD):
                        other = ada_c[:, KD] if k == 0 else acc[:, n]
                        ins = dve.scalar_tensor_tensor(acc[:, n], ada_c[:, k], cnext[:, k:k + 1], other,
                                                       ALU.mult, ALU.add)
                        if k < KD - 1:
                            link(ins, dve_r, base)
                        else:
                            ins.then_inc(m_acc, 1)

                for n in range(4):
                    dve.wait_ge(res_out["r"][n], h * 64 + FREE)
                dve.wait_ge(w_used, h * RET_SLOTS + RING)
                cnext = st[:, 176:176 + KD]
                link(dve.tensor_copy(cnext, ccol[:, :, :].rearrange("p l k -> p (l k)")[
                    :, bass.ds(h * KD + KD, KD)]), dve_r, base)
                modulation(0)
                modulation(1)
                dve.wait_ge(bank_free["r"], h * 24 + 16)
                for src in (r_q, r_k):
                    first, second = src[:, 0], src[:, 1]
                    dve.tensor_tensor(r_s[:, 0], first, sin[:, :], ALU.mult)
                    link(dve.tensor_tensor(r_s[:, 1], second, sin[:, :], ALU.mult), dve_r, base)
                    dve.tensor_tensor(first, first, cos[:, :], ALU.mult)
                    link(dve.tensor_tensor(second, second, cos[:, :], ALU.mult), dve_r, base)
                    dve.tensor_tensor(first, first, r_s[:, 1], ALU.subtract)
                    ins = dve.tensor_tensor(second, second, r_s[:, 0], ALU.add)
                    if src is r_q:
                        link(ins, dve_r, base)
                    else:
                        ins.then_inc(r_rope, 1)
                modulation(2)
                dve.wait_ge(r_consts, h * 32 + 32)

                def gain(m):
                    dve.wait_ge(bank_free["r"], h * 24 + (17 + m))
                    dve.tensor_tensor(r_g[:, m], r_g[:, m], r_gn[:, :], ALU.mult).then_inc(r_gready, 1)

                for m in range(4):
                    gain(m)
                dve.wait_ge(r_rope, h + 1)

                def decay(i):
                    dve.wait_ge(r_sdone, h * NT + (i + 1))
                    if i >= 2:
                        dve.wait_ge(r_odone, h * NT + (i - 1))
                    w = (i + 1) * P
                    dve.tensor_tensor(r_s[:, i % 2, 0:w], psf[:, (i % 2) * 1024:(i % 2) * 1024 + w],
                                      r_decay[:, (NT - 1 - i) * P:], ALU.mult).then_inc(r_sready, 1)

                def gated(i):
                    dve.wait_ge(r_root, h * NT + (i + 1))
                    dve.reciprocal(st[:, 24 + i:25 + i], st[:, 24 + i:25 + i]).then_inc(r_rinv, 1)
                    dve.wait_ge(r_rinv, h * NT + (i + 1))
                    dve.wait_ge(r_gready, h * NT + (i + 1))
                    dve.scalar_tensor_tensor(r_g[:, i], ps[:, 4 + i % 2], st[:, 24 + i:25 + i], r_g[:, i],
                                             ALU.mult, ALU.mult).then_inc(r_gated, 1)

                def low(i):
                    sl = slice((i % 4) * P, (i % 4 + 1) * P)
                    dve.wait_ge(r_hi, h * NT + (i + 1))
                    dve.tensor_tensor(r_olo[:, :, sl], ps[:, 6].rearrange("p (e n) -> p e n", e=4),
                                      r_ohi[:, :, sl].bitcast(F32), ALU.subtract).then_inc(r_lo, 1)

                for a in range(2):
                    decay(4 * a)
                    if a == 0:
                        decay(1)
                        for m in range(4, NT):
                            gain(m)
                        for n in range(3):
                            dve.wait_ge(m_red, h * 3 + (n + 1))
                            dve.tensor_copy(acc[0:1, n], ps[0:1, 5 + n]).then_inc(m_row, 1)
                    for i in range(4 * a, 4 * a + 4):
                        if i % 4 < 3 and i > 0:
                            decay(i + 1)
                        gated(i)
                        if i % 4:
                            low(i - 1)
                    low(4 * a + 3)
                    residual("r", h, range(8 * a, 8 * a + 8), r_tmp[:, :], dve_r, base)
            assert links[0] == RL, links
            norm_layer(1)

            AL = 2 * 2 * GH
            with dve.Fori(0, ATT_GROUPS) as g:
                links[0] = 0
                base = g * AL
                for blk, src in ((1, a_q), (2, a_k)):
                    dve.wait_ge(bank_free["a"], g * 32 + 8 * (blk + 1))
                    c = 32 + 64 * (blk - 1)
                    for h in range(GH):
                        link(dve.tensor_tensor(a_sq[:, :], src[:, h], src[:, h], ALU.mult), dve_a, base)
                        ins = dve.tensor_reduce(st[:, c + 8 * h:c + 8 * h + 8],
                                                a_sq[:, :].rearrange("p (m n) -> p m n", m=NT), AX.X, ALU.add)
                        if h < GH - 1:
                            link(ins, dve_a, base)
                        else:
                            ins.then_inc(a_sums, 1)
                    dve.wait_ge(a_sums, g * 2 + blk)
                    dve.wait_ge(a_roots, g * 2 + blk)
                    r = st[:, c + 32:c + 64]
                    link(dve.reciprocal(r, r), dve_a, base)
                    whole = src[:, :, :].rearrange("p h (m n) -> p (h m) n", m=NT)
                    dve.tensor_tensor(whole, whole, r.unsqueeze(2).to_broadcast([P, GH * NT, P]),
                                      ALU.mult).then_inc(a_normed, 1)
                e0, t0 = g * (GH * NT), g * (GH * (NT + 2))
                for n in range(4):
                    dve.wait_ge(res_out["a"][n], g * 64 + FREE)

                def bias_masked(h):
                    dve.wait_ge(a_biasin[h % 2], g * 32 + 16 * (h // 2 + 1))
                    dve.memset(a_bias[64:128, h % 2, 0:64], NEG).then_inc(a_biasok, 1)
                    dve.memset(a_bias[0:64, h % 2, BANDW - 64:BANDW], NEG).then_inc(a_biasok, 1)
                    dve.wait_ge(a_biasok, g * (2 * GH) + (2 * h + 2))

                def maxima(e):
                    h, i = tile_of(e)
                    w = min(i + 1, LEFT + 1) * P
                    if e % NT == 0:
                        bias_masked(h)
                    dve.wait_ge(a_sdone, e0 + (e + 1))
                    if e >= 3:
                        dve.wait_ge(a_pdone, t0 + (prob_unit(e - 3) + 1))
                    dve.memset(st[:, 160:161], 0.0)
                    dve.tensor_tensor_reduce(a_p[:, e % 3, 0:w], psf[:, (e % 2) * 1024:(e % 2) * 1024 + w],
                                             a_bias[:, h % 2, BANDW - w:], 1.0, -3.0e38, ALU.add, ALU.max,
                                             st[:, 164 + e % 4:165 + e % 4]).then_inc(a_max, 1)
                    dve.wait_ge(a_max, e0 + (e + 1) + FREE)
                    dve.tensor_scalar(st[:, 168 + e % 4:169 + e % 4], st[:, 164 + e % 4:165 + e % 4], -1.0,
                                      None, ALU.mult).then_inc(a_neg, 1)

                def normed(e):
                    w = min(tile_of(e)[1] + 1, LEFT + 1) * P
                    dve.wait_ge(a_exp, e0 + (e + 1))
                    r = st[:, 172 + e % 4:173 + e % 4]
                    dve.reciprocal(r, r).then_inc(a_rinv, 1)
                    dve.wait_ge(a_rinv, e0 + (e + 1))
                    dve.tensor_scalar(a_p[:, e % 3, 0:w], a_p[:, e % 3, 0:w], r, None,
                                      ALU.mult).then_inc(a_prob, 1)

                def gated(h, a):
                    dve.wait_ge(a_odone, e0 + (h * NT + 7 + a))
                    if h:
                        dve.wait_ge(a_lo, g * (2 * GH) + (2 * h + a - 1) + FREE)
                    dve.tensor_tensor(a_o[:, a], ps[:, 6 + a], a_g[:, h, a * 512:(a + 1) * 512],
                                      ALU.mult).then_inc(a_gated, 1)

                def low(h, a):
                    dve.wait_ge(a_hi, g * (2 * GH) + (2 * h + a + 1))
                    dve.tensor_tensor(a_olo[:, h, a * 512:(a + 1) * 512], a_o[:, a],
                                      a_ohi[:, h, a * 512:(a + 1) * 512].bitcast(F32),
                                      ALU.subtract).then_inc(a_lo, 1)

                maxima(0)
                for e in range(GH * NT):
                    h, i = divmod(e, NT)
                    if e + 1 < GH * NT:
                        maxima(e + 1)
                    normed(e)
                    if h and i in (0, 1):
                        gated(h - 1, i)
                    if h and i in (2, 3):
                        low(h - 1, i - 2)
                gated(GH - 1, 0)
                gated(GH - 1, 1)
                low(GH - 1, 0)
                low(GH - 1, 1)
                residual("a", g, range(16), a_o[:, 0], dve_a, base)
            assert links[0] == AL, links
            norm_layer(2)

            links[0] = 0
            for n in range(4):
                dve.memset(l_u[:, n, 0:PAD], 0.0)
                dve.memset(l_u[:, n, PAD + S:PADW], 0.0).then_inc(l_pads, 1)
            dve.wait_ge(l_consts, 16 * 6)
            fr, ang, turns = l_tmp[:, 0, 0:P], l_tmp[:, 0, P:2 * P], l_tmp[:, 0, 2 * P:3 * P]
            fr, ang, turns = (v.rearrange("p (m n) -> p m n", m=NT) for v in (fr, ang, turns))
            link(dve.tensor_copy(fr[:, :, 0], st[:, 184:192].bitcast(I32)), l_chain)
            link(dve.tensor_tensor(ang, cos2[:, :, :], fr[:, :, 0:1].to_broadcast([P, NT, HR]), ALU.mult), l_chain)
            for table, quarter in ((sin2, 0.0), (cos2, 0.25)):
                link(dve.tensor_scalar(turns, ang, 1.0 / TWO_PI, quarter, ALU.mult, ALU.add), l_chain)
                link(dve.tensor_scalar(turns, turns, MAGIC, MAGIC, ALU.add, ALU.subtract), l_chain)
                link(dve.scalar_tensor_tensor(table[:, :, :], turns, -C1, ang, ALU.mult, ALU.add), l_chain)
                link(dve.scalar_tensor_tensor(table[:, :, :], turns, -C2, table[:, :, :], ALU.mult, ALU.add),
                     l_chain)
                link(dve.scalar_tensor_tensor(table[:, :, :], turns, -C3, table[:, :, :], ALU.mult, ALU.add),
                     l_chain)
                link(dve.tensor_scalar(table[:, :, :], table[:, :, :], quarter * TWO_PI, math.pi, ALU.add,
                                       ALU.min), l_chain)
                dve.tensor_scalar(table[:, :, :], table[:, :, :], -math.pi, None, ALU.max).then_inc(rope_reduced, 1)
            dve.wait_ge(bank_free["m"], 8)
            for n, (lo, width) in enumerate(((0, QLAT), (QLAT, KVLAT))):
                part = l_lat[:, :, lo:lo + width]
                sq = l_tmp[:, :, :].rearrange("p a n -> p (a n)")[:, 0:NT * width].rearrange(
                    "p (m n) -> p m n", m=NT)
                link(dve.tensor_tensor(sq, part, part, ALU.mult), l_chain)
                dve.tensor_reduce(st[:, 8 * n:8 * n + 8], sq, AX.X, ALU.add).then_inc(l_sums, 1)
                dve.wait_ge(l_sums, n + 1)
            dve.wait_ge(l_roots, 1)
            link(dve.reciprocal(st[:, 16:32], st[:, 16:32]), l_chain)
            for n, (lo, width) in enumerate(((0, QLAT), (QLAT, KVLAT))):
                part = l_lat[:, :, lo:lo + width]
                r = st[:, 16 + 8 * n:24 + 8 * n].unsqueeze(2).to_broadcast([P, NT, width])
                dve.tensor_tensor(part, part, r, ALU.mult).then_inc(l_latok, 1)
            dve.wait_ge(l_pads, 4)
            for n, window in enumerate(POOLS):
                dve.wait_ge(bank_free["m"], 8 + 2 * n + 2)
                src, step, lo = l_u[:, n], 1, 1
                link(dve.tensor_tensor(l_sum[:, 0, 1:PADW], l_u[:, n, 1:PADW], l_u[:, n, 0:PADW - 1],
                                       ALU.add), l_chain)
                cur, reach, lo, hi = 0, 1, 1, PADW
                while 2 * reach < window:
                    lo, hi = lo + reach, hi - reach
                    link(dve.tensor_tensor(l_sum[:, 1 - cur, lo:hi], l_sum[:, cur, lo - reach:hi - reach],
                                           l_sum[:, cur, lo + reach:hi + reach], ALU.add), l_chain)
                    cur, reach = 1 - cur, 2 * reach
                sums = l_sum[:, cur]
                for e, c in enumerate((PAD, PAD + S - 8)):
                    link(dve.tensor_tensor(l_e8[:, e], sums[:, c:c + 8], l_edge[:, n, e], ALU.mult), l_chain)
                for e, c in enumerate((PAD, PAD + S - 8)):
                    link(dve.tensor_tensor(l_u[:, n, c:c + 8], l_e8[:, e], l_u[:, n, c:c + 8],
                                           ALU.subtract), l_chain)
                inner = slice(PAD + 8, PAD + S - 8)
                dve.scalar_tensor_tensor(l_u[:, n, inner], sums[:, inner], 1.0 / window, l_u[:, n, inner],
                                         ALU.mult, ALU.subtract).then_inc(l_diff, 1)
                dve.wait_ge(l_diff, n + 1)
            for n in range(9):
                if n < 8:
                    dve.wait_ge(l_ydone, n + 1)
                    if n >= 2:
                        dve.wait_ge(l_ylo, n - 1)
                    dve.scalar_tensor_tensor(l_y[:, n % 2], ps[:, n], gains[:, 3 + n // 2:4 + n // 2],
                                             l_gp[:, n // 2, (n % 2) * 512:(n % 2 + 1) * 512], ALU.mult,
                                             ALU.mult).then_inc(l_yready, 1)
                if n:
                    v = n - 1
                    sl = slice((v % 2) * 512, (v % 2 + 1) * 512)
                    dve.wait_ge(l_yhi, v + 1)
                    dve.tensor_tensor(h_lo[:, v // 2, sl], l_y[:, v % 2], h_hi[:, v // 2, sl].bitcast(F32),
                                      ALU.subtract).then_inc(l_ylo, 1)
            for n in range(3):
                dve.wait_ge(l_lhi, n + 1)
                hi, lo = (l_qlhi[:, n - 1], l_qllo[:, n - 1]) if n else (l_klhi[:, :], l_kllo[:, :])
                dve.scalar_tensor_tensor(lo, psf[:, n * 1024:(n + 1) * 1024],
                                         gains[:, 7 + (n + 2) % 3:8 + (n + 2) % 3],
                                         hi.bitcast(F32), ALU.mult, ALU.subtract).then_inc(l_llo, 1)
            def heads(x):
                return x[:, :, :].rearrange("p m (h n) -> p m h n", h=LH)

            dve.wait_ge(l_ydone, 8)
            dve.wait_ge(rope_tables, 4)
            for n in range(2):
                for e in range(2):
                    row = qk_rows[:, n, e * HR:(e + 1) * HR].unsqueeze(1).to_broadcast([P, NT, HR])
                    for c, table in enumerate((cos2, sin2)):
                        dve.tensor_tensor(qk_tables[:, n, e, c], table[:, :, :], row, ALU.mult)
            link(dve.tensor_scalar(gains[:, 10:11], gains[:, 10:11], LQK ** -0.5, None, ALU.mult), l_chain)
            dve.tensor_copy(heads(l_k)[:, :, :, LNOPE:], l_lat[:, :, QLAT + KVLAT:].unsqueeze(2)
                            .to_broadcast([P, NT, LH, LROPE])).then_inc(l_rcopied, 1)
            dve.wait_ge(l_rcopied, 1)

            def qk_sums(u):
                dve.wait_ge(l_sq, u + 1)
                dve.tensor_reduce(qk_stats[:, u // NT ^ 1, u % NT], squares[u % 2].rearrange(
                    "p (h n) -> p h n", h=LH), AX.X, ALU.add).then_inc(l_sums, 1)
                dve.wait_ge(l_sums, 2 + u + 1)

            def one_over(u):
                dve.wait_ge(l_roots, u + 2)
                r = qk_stats[:, u // NT ^ 1, u % NT]
                if u < DVE_SCALED:
                    link(dve.reciprocal(r, r), l_chain)
                    scale_keys(dve, u).then_inc(l_rr, 1)
                else:
                    dve.reciprocal(r, r).then_inc(l_rr, 1)

            def q_rope(m):
                x1, x2 = rope_parts(l_q, m)
                (cos1, sin1), (cos2_, sin2_) = (
                    [qk_tables[:, 0, e, c, m].unsqueeze(1).to_broadcast([P, LH, HR]) for c in range(2)]
                    for e in range(2))
                t1, t2 = (l_tmp[:, 0, LH * LQK + a * P:][:, 0:P].rearrange("p (h n) -> p h n", h=LH)
                          for a in range(2))
                dve.tensor_tensor(t1, x1, sin1, ALU.mult)
                link(dve.tensor_tensor(t2, x2, sin2_, ALU.mult), l_chain)
                dve.tensor_tensor(x1, x1, cos1, ALU.mult)
                link(dve.tensor_tensor(x2, x2, cos2_, ALU.mult), l_chain)
                dve.tensor_tensor(x1, x1, t2, ALU.subtract)
                dve.tensor_tensor(x2, x2, t1, ALU.add).then_inc(l_qdone, 1)
                dve.wait_ge(l_qdone, m + 1)

            for u in range(2 * NT + 1):
                if u < 2 * NT:
                    qk_sums(u)
                if u:
                    one_over(u - 1)
                if u > NT:
                    q_rope(u - 1 - NT)
            dve.wait_ge(l_rr, 2 * NT)

            def l_maxima(e):
                h, i = divmod(e, NT)
                dve.wait_ge(l_sdone, e + 1)
                dve.tensor_reduce(st[:, 128 + e % 4:129 + e % 4], psf[:, (e % 2) * 1024:(e % 2) * 1024 + S],
                                  AX.X, ALU.max).then_inc(l_max, 1)
                dve.wait_ge(l_max, e + 1)
                dve.tensor_scalar(st[:, 132 + e % 4:133 + e % 4], st[:, 128 + e % 4:129 + e % 4],
                                  qk_stats[:, 0, i, h:h + 1], -1.0, ALU.mult, ALU.mult).then_inc(l_neg, 1)

            def l_normed(e):
                dve.wait_ge(l_exp, e + 1)
                r = st[:, 136 + e % 4:137 + e % 4]
                dve.reciprocal(r, r).then_inc(l_rinv, 1)
                dve.wait_ge(l_rinv, e + 1)
                dve.tensor_scalar(l_p[:, e % 3], l_p[:, e % 3], r, None, ALU.mult).then_inc(l_prob, 1)

            def l_gate(h, a):
                rows, n = slice(LV * (h % 2), LV * (h % 2) + LV), 2 * h + a
                dve.wait_ge(l_odone, h * NT + 4 * a + 4)
                dve.wait_ge(l_sgin, 16 * (n + 1))
                if n:
                    dve.wait_ge(l_lo, n)
                dve.tensor_tensor(l_o[rows, :], ps[rows, 6 + a], l_sg[rows, :], ALU.mult).then_inc(l_gated, 1)

            def l_low(h, a):
                rows, sl = slice(LV * (h % 2), LV * (h % 2) + LV), slice(a * 512, (a + 1) * 512)
                dve.wait_ge(l_hi, 2 * h + a + 1)
                dve.tensor_tensor(h_lo[rows, 4 + h // 2, sl], l_o[rows, :],
                                  h_hi[rows, 4 + h // 2, sl].bitcast(F32), ALU.subtract).then_inc(l_lo, 1)

            def l_head_low(h, k):
                dve.wait_ge(l_headhi, 2 * h + k + 1)
                dve.scalar_tensor_tensor(l_turned(h, k, 1)[0:LQK], l_head_bank(head_unit(h, k, LH)),
                                         gains[0:LQK, 10 + k:11 + k], l_turned(h, k, 0)[0:LQK].bitcast(F32),
                                         ALU.mult, ALU.subtract).then_inc(l_pevac, 1)

            l_head_low(0, 0)
            l_head_low(0, 1)
            l_maxima(0)
            for e in range(LH * NT):
                h, i = divmod(e, NT)
                if e + 1 < LH * NT:
                    l_maxima(e + 1)
                l_normed(e)
                if h + 1 < LH and i - 1 in TURN_AT[LH]:
                    l_head_low(h + 1, TURN_AT[LH].index(i - 1))
                if h and i == 1:
                    l_gate(h - 1, 1)
                if h and i == 3:
                    l_low(h - 1, 1)
                if i == 5:
                    l_gate(h, 0)
                if i == 7:
                    l_low(h, 0)
            l_gate(LH - 1, 1)
            l_low(LH - 1, 1)
            for u in range(16):
                if u % 8 == 7:
                    dve.wait_ge(w_used, MIX0 + 40 + u + 1 + RING)
                else:
                    dve.wait_ge(out_done["m"], u - u // 8 + 1)
                if u:
                    dve.wait_ge(out_ready["m"], u)
                dve.tensor_tensor(l_t[:, :], ps[:, u % 4], gate[:, (u // 8) * 512:(u // 8 + 1) * 512],
                                  ALU.mult).then_inc(out_free["m"], 1)
                dve.wait_ge(out_free["m"], u + 1)
                dve.wait_ge(res_in["m"][u % 4], 16 * (u // 4 + 1))
                dve.tensor_tensor(l_x[:, u % 4], l_x[:, u % 4], l_t[:, :], ALU.add).then_inc(out_ready["m"], 1)


SCRATCH = {"sg": (512, 1024)}


def lay_out(inputs):
    f = {k: np.asarray(v) for k, v in inputs.items()}
    w = []

    def slots(m):
        w.extend(m.reshape(-1, P, 512))

    def halves(m):
        slots(m[:, :512])
        slots(m[:, 512:])

    wi, wo = f["ret_w_in"][0], f["ret_w_out"][0]
    for h in range(4):
        slots(wi[:, 2048 + 512 * h:2560 + 512 * h])
        slots(np.concatenate([wi[:, 256 * h:256 * h + 256], wi[:, 1024 + 256 * h:1280 + 256 * h]], 1))
        slots(wi[:, 4096 + 512 * h:4608 + 512 * h])
        halves(wo[512 * h:512 * h + 512])
    wi, wo = f["att_w_in"][0], f["att_w_out"][0]
    for g in range(4):
        for part in (2, 0, 1, 3):
            slots(wi[:, 2048 * part + 512 * g:2048 * part + 512 * g + 512])
        halves(wo[512 * g:512 * g + 512])
    wi = f["w_in_2"][0]
    slots(np.pad(wi[:, 1024:1440], ((0, 0), (0, 96))))
    slots(wi[:, 0:512])
    slots(wi[:, 512:1024])
    slots(wi[:, 1440:1952])
    uq = f["w_uq_2"][0]
    for c in range(2):
        slots(np.pad(uq[:, 384 * c:384 * c + 384], ((0, 0), (0, 128))))
    uk = f["w_ukv_2"][0]
    slots(uk[:, :512])
    slots(uk[:, 512:])
    w.extend([np.zeros((P, 512), np.float32)] * 2)
    halves(f["w_out_2"][0])
    w = np.stack(w)
    assert w.shape[0] == SLOTS, w.shape

    aw = np.concatenate([f["ada_w"], f["ada_w_2"]])
    ab = np.concatenate([f["ada_b"], f["ada_b_2"]])
    aw = aw.reshape(3, KD, P, PIECES, 512).transpose(0, 3, 2, 1, 4).reshape(18, P, KD, 512)
    bias = np.concatenate([ab.reshape(18, 1, 1, 512), np.zeros((18, P - 1, 1, 512), np.float32)], 1)
    ada = np.concatenate([aw, bias], 2)

    c1, c2 = f["c"].reshape(KD, P).T, f["c_2"].reshape(KD, P).T
    cond = np.stack([c1, c1, c1, c2, c2], 1)
    i = np.arange(0, 256, 2, dtype=np.float32)
    inv = (1.0 / (np.float32(10000.0) ** (i / np.float32(256.0)))).astype(np.float32)
    col = lambda v: v.reshape(-1, P).T
    nope = [np.concatenate([f[n][0, :LNOPE], np.ones(P - LNOPE, np.float32)])[:, None]
            for n in ("g_qnorm_2", "g_knorm_2")]
    gains = np.concatenate([col(f["att_q_g"]), col(f["att_k_g"]), col(inv), col(f["pool_scale_2"]),
                            col(f["g_q_lat_2"]), col(f["g_kv_lat_2"]), *nope, np.zeros((P, 4), np.float32)], 1)

    lg = np.log(1.0 - 2.0 ** (-5.0 - np.arange(4)))
    j, q = np.arange(P)[:, None], np.arange(P)[None, :]
    far = np.stack([q - j + P * n for n in range(NT - 1, 0, -1)])
    near = np.abs(q - j)[None]
    power = np.exp(lg[:, None, None, None] * np.concatenate([far, near])[None])
    power[:, -1][:, (j // 64) > (q // 64)] = 0.0
    decay = (power / 16.0).transpose(0, 2, 1, 3).reshape(4, P, NT * P).astype(np.float32)

    rel = f["att_rel_bias"][0]
    diag = np.concatenate([np.repeat(rel[:, 256:257], 511, 1), rel[:, ::-1][:, :256]], 1)
    band = np.stack([diag[:, 127 - n:127 - n + BANDW] for n in range(P)], 1)

    edge = np.zeros((P, 4, 2, 8), np.float32)
    for n, window in enumerate(POOLS):
        for e, c in enumerate((0, S - 8)):
            tt = np.arange(c, c + 8)
            edge[:, n, e] = 1.0 / (np.clip(tt + window // 2, 0, S) - np.clip(tt - window // 2, 0, S))
    inv2 = (np.float32(10000.0) ** (-np.arange(0, LROPE, 2, dtype=np.float32) / np.float32(LROPE)))

    return {
        "w": w, "ada": ada, "cond": cond, "gains": gains, "x": f["x"][0], "pos": f["positions"][0],
        "norm_g": np.concatenate([f["norm_g"], f["norm_g_2"]]), "ret_gn": f["ret_gn_g"].reshape(4, 512),
        "pool_w": f["pool_w_2"][0].transpose(1, 0, 2), "edge": edge, "pos2": f["positions_2"].reshape(NT, P).T,
        "inv2": np.repeat(inv2[None], NT, 0), "g_qnorm": f["g_qnorm_2"][0], "g_knorm": f["g_knorm_2"][0],
        "decay": decay, "ident": np.eye(P, dtype=np.float32), "band": band,
    }


def kernel(**inputs):
    import concourse.bacc as bacc
    from concourse.bass_utils import run_bass_kernel_spmd

    nc = bacc.Bacc("TRN2", target_bir_lowering=False, num_devices=1)
    arrays = {f"in_{k}": np.ascontiguousarray(v) for k, v in lay_out(inputs).items()}
    t = {k[3:]: nc.dram_tensor(k, v.shape, mybir.dt.from_np(v.dtype), kind="ExternalInput").ap()
         for k, v in arrays.items()}
    t["out"] = nc.dram_tensor("out", (S, D), F32, kind="ExternalOutput").ap()
    t["res"] = nc.dram_tensor("res", (S, D), F32, kind="Internal").ap()
    t["mod"] = nc.dram_tensor("mod", (18, 512), F32, kind="Internal").ap()
    for name, shape in SCRATCH.items():
        t[name] = nc.dram_tensor(name, shape, F32, kind="Internal").ap()
    build_program(nc, t)
    result = run_bass_kernel_spmd(nc, [arrays], core_ids=[0])
    return np.asarray(result.results[0]["out"]).reshape(1, S, D)
```
